# Optimizing a Trainium2 kernel written in Bass

```python
import jax, jax.numpy as jnp
from jax import lax
import numpy as np

D_MODEL = 1024
BATCH = 1
SEQ = 256
DEPTH = 4

N_MIXERS = 3
EPS = 1e-6
N_NORMS = 6
D_FF = 2816
CONV_W = 3
ATT_HEADS = 16
ATT_HD = 64
DILATION_PAIRS = ((128, 1), (512, 4), (2048, 16))
N_GROUPS = len(DILATION_PAIRS)
ATT_BLOCK = 128
ROPE_THETA = 500000.0
ROT_DIM = ATT_HD // 4
ML_HEADS = 4
ML_DQK = 128
ML_DV = D_MODEL // ML_HEADS
ML_CHUNK = 64
ML_PROJ = 2 * ML_HEADS * ML_DQK + 2 * ML_HEADS * ML_DV + 2 * ML_HEADS
N_CONV_LAYERS = (DEPTH + 2) // 3
N_ATTN_LAYERS = (DEPTH + 1) // 3
N_MLSTM_LAYERS = DEPTH // 3

kernel_name = "hybrid_conv_dilattn_mlstm_macaron"

def rmsnorm(x, g):
    x32 = x.astype(jnp.float32)
    y = x32 * lax.rsqrt(jnp.mean(x32 * x32, axis=-1, keepdims=True) + EPS)
    return (y * g.astype(jnp.float32)).astype(x.dtype)

def swiglu(x, wg, wu, wd):
    return (jax.nn.silu(x @ wg) * (x @ wu)) @ wd

def short_conv_mixer(x, w_in, k, w_out):
    S = x.shape[1]
    b, c, u = jnp.split(x @ w_in, 3, axis=-1)
    u = c * u
    up = jnp.pad(u, ((0, 0), (CONV_W - 1, 0), (0, 0)))
    conv = sum(k[j] * up[:, CONV_W - 1 - j:CONV_W - 1 - j + S] for j in range(CONV_W))
    return (b * conv) @ w_out

def rope_tables(S):
    pos = jnp.arange(S, dtype=jnp.float32)
    inv = ROPE_THETA ** (-jnp.arange(0, ROT_DIM, 2, dtype=jnp.float32) / ROT_DIM)
    ang = pos[:, None] * inv[None, :]
    return jnp.cos(ang), jnp.sin(ang)

def apply_partial_rope(x, cos, sin):
    half = ROT_DIM // 2
    x1, x2, rest = x[..., :half], x[..., half:ROT_DIM], x[..., ROT_DIM:]
    c, s = cos[None, :, None, :], sin[None, :, None, :]
    return jnp.concatenate([x1 * c - x2 * s, x2 * c + x1 * s, rest], axis=-1).astype(x.dtype)

def dilated_window_attention(q, k, v, win, dil):
    B, S, H, hd = q.shape
    L = S // dil
    nb = -(-L // ATT_BLOCK)
    Lp = nb * ATT_BLOCK

    def to_sub(t):
        t = t.reshape(B, L, dil, H, hd).transpose(0, 2, 3, 1, 4)
        t = jnp.pad(t, ((0, 0), (0, 0), (0, 0), (0, Lp - L), (0, 0)))
        return t.reshape(B, dil, H, nb, ATT_BLOCK, hd)

    def with_prev(t):
        prev = jnp.pad(t, ((0, 0), (0, 0), (0, 0), (1, 0), (0, 0), (0, 0)))[:, :, :, :-1]
        return jnp.concatenate([prev, t], axis=-2)

    qb = to_sub(q)
    kk = with_prev(to_sub(k))
    vv = with_prev(to_sub(v)).astype(jnp.float32)
    scores = jnp.einsum('brhnqd,brhnkd->brhnqk', qb, kk,
                        preferred_element_type=jnp.float32) * (hd ** -0.5)
    qi = jnp.arange(ATT_BLOCK)[:, None] + ATT_BLOCK
    kj = jnp.arange(2 * ATT_BLOCK)[None, :]
    rel = qi - kj
    band = (rel >= 0) & (rel <= win)
    key_ok = (jnp.arange(nb)[:, None] * ATT_BLOCK - ATT_BLOCK + kj) >= 0
    mask = band[None] & key_ok[:, None, :]
    scores = jnp.where(mask, scores, -jnp.inf)
    m = jnp.max(scores, axis=-1, keepdims=True)
    p = jnp.exp(scores - m)
    den = jnp.sum(p, axis=-1)
    out = jnp.einsum('brhnqk,brhnkd->brhnqd', p, vv) / den[..., None]
    lse = m[..., 0] + jnp.log(den)
    out = out.reshape(B, dil, H, Lp, hd)[:, :, :, :L].transpose(0, 3, 1, 2, 4).reshape(B, S, H, hd)
    lse = lse.reshape(B, dil, H, Lp)[..., :L].transpose(0, 3, 1, 2).reshape(B, S, H)
    return out, lse

def dilated_attention_mixer(x, w_in, w_out, cos, sin):
    B, S, _ = x.shape
    qkv = (x @ w_in).reshape(B, S, N_GROUPS, 3, ATT_HEADS, ATT_HD)
    outs, lses = [], []
    for g, (win, dil) in enumerate(DILATION_PAIRS):
        q = apply_partial_rope(qkv[:, :, g, 0], cos, sin)
        k = apply_partial_rope(qkv[:, :, g, 1], cos, sin)
        v = qkv[:, :, g, 2]
        o, l = dilated_window_attention(q, k, v, win // dil, dil)
        outs.append(o)
        lses.append(l)
    alpha = jax.nn.softmax(jnp.stack(lses, axis=0), axis=0)
    o = jnp.sum(alpha[..., None] * jnp.stack(outs, axis=0), axis=0)
    return o.reshape(B, S, ATT_HEADS * ATT_HD).astype(x.dtype) @ w_out

def mlstm_mixer(x, w_in, b_i, b_f, w_out):
    B, S, _ = x.shape
    NH, L = ML_HEADS, ML_CHUNK
    nc = S // L
    p = x @ w_in
    o1 = NH * ML_DQK
    o2 = 2 * o1
    o3 = o2 + NH * ML_DV
    o4 = o3 + NH * ML_DV
    o5 = o4 + NH
    q = p[..., :o1].reshape(B, S, NH, ML_DQK).astype(jnp.float32)
    k = p[..., o1:o2].reshape(B, S, NH, ML_DQK).astype(jnp.float32) * (ML_DQK ** -0.5)
    v = p[..., o2:o3].reshape(B, S, NH, ML_DV).astype(jnp.float32)
    og = jax.nn.sigmoid(p[..., o3:o4].astype(jnp.float32))
    ig = (p[..., o4:o5] + b_i).astype(jnp.float32)
    lf = jax.nn.log_sigmoid((p[..., o5:] + b_f).astype(jnp.float32))

    def vec_chunks(t):
        return t.reshape(B, nc, L, NH, -1).transpose(1, 0, 3, 2, 4)

    def gate_chunks(t):
        return t.reshape(B, nc, L, NH).transpose(1, 0, 3, 2)

    tril = jnp.tril(jnp.ones((L, L), dtype=bool))

    def step(carry, inp):
        C, n, m = carry
        qc, kc, vc, ic, fc = inp
        b = jnp.cumsum(fc, axis=-1)
        dlog = jnp.where(tril, b[..., :, None] - b[..., None, :] + ic[..., None, :], -jnp.inf)
        inter = b + m[..., None]
        mt = jnp.maximum(inter, jnp.max(dlog, axis=-1))
        w = jnp.exp(dlog - mt[..., None])
        wi = jnp.exp(inter - mt)
        a = jnp.einsum('bhtd,bhsd->bhts', qc, kc) * w
        num = jnp.einsum('bhts,bhsv->bhtv', a, vc) + wi[..., None] * jnp.einsum('bhvd,bhtd->bhtv', C, qc)
        den = jnp.sum(a, axis=-1) + wi * jnp.einsum('bhd,bhtd->bht', n, qc)
        h = num / jnp.maximum(jnp.abs(den), jnp.exp(-mt))[..., None]
        m_new = mt[..., -1]
        we = jnp.exp(b[..., -1:] - b + ic - m_new[..., None])
        decay = jnp.exp(b[..., -1] + m - m_new)
        C = decay[..., None, None] * C + jnp.einsum('bhs,bhsv,bhsd->bhvd', we, vc, kc)
        n = decay[..., None] * n + jnp.einsum('bhs,bhsd->bhd', we, kc)
        return (C, n, m_new), h

    init = (jnp.zeros((B, NH, ML_DV, ML_DQK), jnp.float32),
            jnp.zeros((B, NH, ML_DQK), jnp.float32),
            jnp.zeros((B, NH), jnp.float32))
    _, h = lax.scan(step, init, (vec_chunks(q), vec_chunks(k), vec_chunks(v),
                                 gate_chunks(ig), gate_chunks(lf)))
    h = h.transpose(1, 0, 3, 2, 4).reshape(B, S, NH * ML_DV)
    return (h * og).astype(x.dtype) @ w_out

def setup_inputs(seed: int = 0) -> dict:
    key = jax.random.key(seed)
    ks = jax.random.split(key, 18)
    D = D_MODEL

    def w(k, shape, fan_in):
        return jax.random.normal(k, shape, jnp.float32) * fan_in ** -0.5

    return {
        "x": jax.random.normal(ks[0], (BATCH, SEQ, D), jnp.float32),
        "norm_g": 1.0 + 0.05 * jax.random.normal(ks[1], (DEPTH, N_NORMS, D), jnp.float32),
        "ffn1_wg": w(ks[2], (DEPTH, D, D_FF), D),
        "ffn1_wu": w(ks[3], (DEPTH, D, D_FF), D),
        "ffn1_wd": w(ks[4], (DEPTH, D_FF, D), D_FF),
        "ffn2_wg": w(ks[5], (DEPTH, D, D_FF), D),
        "ffn2_wu": w(ks[6], (DEPTH, D, D_FF), D),
        "ffn2_wd": w(ks[7], (DEPTH, D_FF, D), D_FF),
        "conv_w_in": w(ks[8], (N_CONV_LAYERS, D, 3 * D), D),
        "conv_k": w(ks[9], (N_CONV_LAYERS, CONV_W, D), CONV_W),
        "conv_w_out": w(ks[10], (N_CONV_LAYERS, D, D), D),
        "attn_w_in": w(ks[11], (N_ATTN_LAYERS, D, N_GROUPS * 3 * ATT_HEADS * ATT_HD), D),
        "attn_w_out": w(ks[12], (N_ATTN_LAYERS, ATT_HEADS * ATT_HD, D), ATT_HEADS * ATT_HD),
        "mlstm_w_in": w(ks[13], (N_MLSTM_LAYERS, D, ML_PROJ), D),
        "mlstm_b_i": 0.01 * jax.random.normal(ks[14], (N_MLSTM_LAYERS, ML_HEADS), jnp.float32),
        "mlstm_b_f": jnp.linspace(3.0, 6.0, ML_HEADS, dtype=jnp.float32)[None, :]
                     + 0.01 * jax.random.normal(ks[15], (N_MLSTM_LAYERS, ML_HEADS), jnp.float32),
        "mlstm_w_out": w(ks[16], (N_MLSTM_LAYERS, ML_HEADS * ML_DV, D), ML_HEADS * ML_DV),
    }

def reference(x, norm_g, ffn1_wg, ffn1_wu, ffn1_wd, ffn2_wg, ffn2_wu, ffn2_wd,
              conv_w_in, conv_k, conv_w_out, attn_w_in, attn_w_out,
              mlstm_w_in, mlstm_b_i, mlstm_b_f, mlstm_w_out):
    cos, sin = rope_tables(x.shape[1])
    for i in range(DEPTH):
        g = norm_g[i]
        x = x + 0.5 * rmsnorm(swiglu(rmsnorm(x, g[0]), ffn1_wg[i], ffn1_wu[i], ffn1_wd[i]), g[1])
        xn = rmsnorm(x, g[2])
        mixer, j = i % N_MIXERS, i // N_MIXERS
        if mixer == 0:
            y = short_conv_mixer(xn, conv_w_in[j], conv_k[j], conv_w_out[j])
        elif mixer == 1:
            y = dilated_attention_mixer(xn, attn_w_in[j], attn_w_out[j], cos, sin)
        else:
            y = mlstm_mixer(xn, mlstm_w_in[j], mlstm_b_i[j], mlstm_b_f[j], mlstm_w_out[j])
        x = x + rmsnorm(y, g[3])
        x = x + 0.5 * rmsnorm(swiglu(rmsnorm(x, g[4]), ffn2_wg[i], ffn2_wu[i], ffn2_wd[i]), g[5])
    return x


_drawn_inputs = setup_inputs


def setup_inputs(seed=0):
    import zlib

    import numpy as np

    out = dict(_drawn_inputs(seed))
    spreads = {}
    factors = {'mlstm_b_i': 56.402}
    for name, (base, spread) in spreads.items():
        noise = np.random.default_rng([zlib.crc32(name.encode()), seed]).standard_normal(out[name].shape)
        drawn = base * np.exp(spread * noise) if base else spread * noise
        out[name] = __import__('jax').numpy.asarray(drawn.astype(out[name].dtype))
    for name, factor in factors.items():
        out[name] = (out[name] * factor).astype(out[name].dtype)
    return out
```

```python
from contextlib import ExitStack

import concourse.bass as bass
from concourse import mybir

F32 = mybir.dt.float32
F32R = mybir.dt.float32r
ALU = mybir.AluOpType
ACT = mybir.ActivationFunctionType

P = 128
D = 1024
SEQ = 256
TILES = SEQ // P
DEPTH = 4
D_FF = 2816
EPS = 1e-6
KD = D // P
CHUNK = 256
CHUNKS = D_FF // CHUNK
FT = CHUNK // P
PIECE = 2048
RAW = 3
RING = 6
CONV_W = 3
CONV_STEPS = D // 256
GROUPS = ((128, 1), (512, 4), (2048, 16))
NG = len(GROUPS)
HD = 64
ROT = HD // 4
QUARTERS = 4
QH = 4
QP = 3 * NG
NH = 4
DQK = 128
DV = D // NH
NEG = -1e30
MASK_LOW = -3e38

REGION = 8900

FFN_PIECES = 3 * CHUNKS
OUT_PIECES = 4
CONV_PIECES = 3 * CONV_STEPS + OUT_PIECES
ATT_PIECES = QUARTERS * QP + OUT_PIECES
ML_PIECES = 12 + OUT_PIECES
LAYER_KINDS = ("conv", "att", "ml", "conv")
KINDS = [k for mixer in LAYER_KINDS for k in ("ffn", mixer, "ffn")]
COUNT = {"ffn": FFN_PIECES, "conv": CONV_PIECES, "att": ATT_PIECES, "ml": ML_PIECES}
BASE = [sum(COUNT[k] for k in KINDS[:n]) for n in range(len(KINDS) + 1)]
PIECES = BASE[-1]
SUBLAYERS = len(KINDS)

GU_BANK = 0
T_BANK = 2
Y_BANK = 4


def build(nc, x_in, gains, stream, gate_w, gate_b, conv_k, ident_in, rope_in, att_mask_in, ml_mask_in,
          tri_in, out):
    with ExitStack() as ctx:
        def sb(name, shape, dt=F32):
            return ctx.enter_context(nc.sbuf_tensor(name, shape, dt))

        def sem(name):
            return ctx.enter_context(nc.semaphore(name))

        ps = ctx.enter_context(nc.psum_tensor("ps", [P, 8, 512], F32))

        raw = sb("raw", [P, RAW, PIECE])
        w_high = sb("w_high", [P, RING, PIECE], F32R)
        w_low = sb("w_low", [P, RING, PIECE], F32R)
        x = sb("x", [P, TILES, D])
        xn = sb("xn", [P, TILES, D])
        gain = sb("gain", [P, 2, D])
        mean_y = sb("mean_y", [P, TILES])
        mean_x = sb("mean_x", [P, TILES])
        mean_eps = sb("mean_eps", [P, 2 * TILES])
        rstd_y = sb("rstd_y", [P, TILES])
        rstd_x = sb("rstd_x", [P, TILES])
        minus_half = sb("minus_half", [P, 1])
        xT_high = sb("xT_high", [P, KD, SEQ], F32R)
        xT_low = sb("xT_low", [P, KD, SEQ], F32R)
        ident = sb("ident", [P, P])

        region = sb("region", [P, REGION])
        used = [0]

        def from_region(shape, dt=F32):
            n = 1
            for s in shape:
                n *= s
            a = region[:, used[0]:used[0] + n]
            used[0] += n
            assert used[0] <= REGION, used[0]
            if dt is not F32:
                a = a.bitcast(dt)
            if len(shape) == 2:
                a = a.rearrange("p (a b) -> p a b", a=shape[0])
            if len(shape) == 3:
                a = a.rearrange("p (a b c) -> p a b c", a=shape[0], b=shape[1])
            return a

        conv_kT = sb("conv_kT", [P, 2, CONV_W, KD])
        rope = sb("rope", [P, TILES, 2, QH * ROT])
        att_mask = sb("att_mask", [P, NG, 2 * P])
        ml_mask = sb("ml_mask", [P, 2 * P])
        tri = sb("tri", [P, P])
        ones = sb("ones", [P, P])
        gw_raw = sb("gw_raw", [P, KD, 2 * NH])
        gw_high = sb("gw_high", [P, KD, 2 * NH], F32R)
        gw_low = sb("gw_low", [P, KD, 2 * NH], F32R)
        gate_bias = sb("gate_bias", [P, 2 * NH])
        oT_hi = sb("oT_hi", [P, KD, SEQ], F32R)
        oT_lo = sb("oT_lo", [P, KD, SEQ], F32R)
        silu = from_region([TILES, CHUNK])
        h = from_region([TILES, CHUNK])
        hT_hi = sb("hT_hi", [P, TILES, CHUNK], F32R)
        hT_lo = sb("hT_lo", [P, TILES, CHUNK], F32R)

        loaded = sem("loaded")
        raw_landed = [sem(f"raw_landed{n}") for n in range(RAW)]
        piece_high = sem("piece_high")
        piece_split = sem("piece_split")
        piece_used = sem("piece_used")
        y_ready = sem("y_ready")
        y_mean = sem("y_mean")
        y_rstd = sem("y_rstd")
        y_scaled = sem("y_scaled")
        x_updated = sem("x_updated")
        x_mean = sem("x_mean")
        x_rstd = sem("x_rstd")
        eps_added = sem("eps_added")
        xn_ready = sem("xn_ready")
        xT_in_psum = sem("xT_in_psum")
        xT_high_done = sem("xT_high_done")
        xT_split = sem("xT_split")
        gain_landed = sem("gain_landed")
        consts_set = sem("consts_set")
        gu_ready = sem("gu_ready")
        silu_done = sem("silu_done")
        h_ready = sem("h_ready")
        hT_in_psum = sem("hT_in_psum")
        hT_high_done = sem("hT_high_done")
        hT_split = sem("hT_split")
        oT_high_done = sem("oT_high_done")
        oT_split = sem("oT_split")
        c_copied = sem("c_copied")
        pads_zeroed = sem("pads_zeroed")
        cu_ready = sem("cu_ready")
        tap_done = sem("tap_done")
        conv_ready = sem("conv_ready")
        proj_ready = sem("proj_ready")
        proj_copied = sem("proj_copied")
        rope_products = sem("rope_products")
        rope_done = sem("rope_done")
        qkT_in_psum = sem("qkT_in_psum")
        qkT_done = sem("qkT_done")
        scores_ready = sem("scores_ready")
        masked = sem("masked")
        max_ready = sem("max_ready")
        exp_done = sem("exp_done")
        recip_done = sem("recip_done")
        probs_ready = sem("probs_ready")
        pT_in_psum = sem("pT_in_psum")
        pT_done = sem("pT_done")
        o_ready = sem("o_ready")
        gw_high_done = sem("gw_high_done")
        gw_split = sem("gw_split")
        gates_in_psum = sem("gates_in_psum")
        gate_step = sem("gate_step")
        gate_exp = sem("gate_exp")
        gate_ln = sem("gate_ln")
        lf_ready = sem("lf_ready")
        cum_in_psum = sem("cum_in_psum")
        diag_ready = sem("diag_ready")
        rows_in_psum = sem("rows_in_psum")
        ml_masked = sem("ml_masked")
        ml_max_ready = sem("ml_max_ready")
        ml_floor_sum = sem("ml_floor_sum")
        ml_floor = sem("ml_floor")
        decay_ready = sem("decay_ready")
        ml_copied = sem("ml_copied")
        ml_scores = sem("ml_scores")
        a_ready = sem("a_ready")
        den_step = sem("den_step")
        aT_in_psum = sem("aT_in_psum")
        aT_done = sem("aT_done")
        num_ready = sem("num_ready")
        mh_scaled = sem("mh_scaled")
        mhT_in_psum = sem("mhT_in_psum")
        stored = sem("stored")

        CONSTS = 16 * 10

        used[0] = 0
        c_sb = from_region([2, SEQ])
        cu = from_region([2, SEQ + 2])
        z = from_region([2, SEQ])
        used[0] = 0
        pT = from_region([NG, 3 * P])
        used[0] = 0
        qk = from_region([2, TILES * QH * HD]).rearrange("p a (t c) -> p a t c", t=TILES)
        rope_c, rope_s = ([from_region([QH, ROT]) for _ in range(TILES)] for _ in range(2))
        qT = from_region([NG, 2, SEQ])
        kT = from_region([NG, 2, SEQ])
        v = from_region([NG, TILES, QH * HD])
        probs = [from_region([NG, 3 * P]) for _ in range(2)]
        smax = from_region([2, 2])
        nmax = from_region([2, 2])
        den = from_region([2, 2])
        rden = from_region([2, 2])
        used[0] = 0
        mqT = from_region([NH, SEQ])
        mkT = from_region([NH, SEQ])
        mv = from_region([NH, TILES, DV])
        mog = region[:, 0:2 * NH * SEQ].rearrange("p (a b c) -> p a b c", a=NH, b=TILES)
        gates = from_region([TILES, 2 * NH])
        neg_f = from_region([TILES, NH])
        neg_abs = from_region([TILES, NH])
        exp_f = from_region([TILES, NH])
        ln_f = from_region([TILES, NH])
        lf = from_region([TILES, NH])
        cum = from_region([TILES, NH])
        r_col = from_region([TILES, NH])
        diag = from_region([2, TILES * P])
        decay = from_region([2, 3 * P])
        rmax = from_region([NH, TILES])
        neg_m = from_region([NH, TILES])
        floor_in = from_region([NH, TILES])
        floor_e = from_region([NH, TILES])
        a = from_region([2, 3 * P])
        aT = from_region([NH, 3 * P])
        mden = from_region([NH, TILES])
        neg_den = from_region([NH, TILES])
        abs_den = from_region([NH, TILES])
        safe_den = from_region([NH, TILES])
        mrden = from_region([NH, TILES])
        mh = from_region([2, TILES * DV]).rearrange("p a (t c) -> p a t c", t=TILES)

        def w_of(sub):
            return BASE[sub]

        def ffn_no(sub):
            return KINDS[:sub].count("ffn")

        def conv_no(sub):
            return KINDS[:sub].count("conv")

        OT = {"ffn": 0, "conv": CONV_STEPS, "att": 2 * QUARTERS, "ml": NH}

        def ot_before(sub):
            return sum(OT[k] for k in KINDS[:sub])

        def interleaved(joint):
            return joint == 0 or KINDS[joint - 1] == "ffn"

        def masked_row(n, t):
            base = xn[:, n // 2, :]
            return base[:, (n % 2) * 384:(n % 2) * 384 + P] if t == 0 else \
                base[:, (n % 2) * 384 + P:(n % 2) * 384 + 3 * P]

        block = ctx.enter_context(nc.Block())

        @block.sync
        def _(sp):
            for t in range(TILES):
                sp.dma_start(x[:, t, :], x_in[t * P:(t + 1) * P, :]).then_inc(loaded, 16)
            for n in range(RAW):
                sp.dma_start(raw[:, n, :], stream[n]).then_inc(raw_landed[n], 16)
            with sp.Fori(1, PIECES // RAW) as turn:
                for n in range(RAW):
                    sp.wait_ge(piece_split, RAW * turn + n - RAW + 1)
                    sp.dma_start(raw[:, n, :], stream[RAW * turn + n]).then_inc(raw_landed[n], 16)
            for p in range(PIECES // RAW * RAW, PIECES):
                sp.wait_ge(piece_split, p - RAW + 1)
                sp.dma_start(raw[:, p % RAW, :], stream[p]).then_inc(raw_landed[p % RAW], 16)
            for t in range(TILES):
                sp.wait_ge(x_updated, TILES * (SUBLAYERS - 1) + t + 1)
                sp.dma_start(out[t * P:(t + 1) * P, :], x[:, t, :]).then_inc(stored, 16)
            sp.wait_ge(stored, 16 * TILES)

        @block.tensor
        def _(pe):
            def products(acc, lh, ll, rh, rl, start, stop):
                nc.tensor.matmul(acc, lh, rh, start=start, stop=False)
                nc.tensor.matmul(acc, lh, rl, start=False, stop=False)
                return nc.tensor.matmul(acc, ll, rh, start=False, stop=stop)

            def weights_ready(p):
                pe.wait_ge(piece_split, p + 1)

            def transpose_x(joint, t):
                pe.wait_ge(xn_ready, TILES * joint + t + 1)
                if joint == 0 and t == 0:
                    pe.wait_ge(loaded, CONSTS)
                for b in range(2):
                    if t == 1:
                        pe.wait_ge(xT_split, 4 * joint + b + 1)
                    for k in range(4):
                        f = (4 * b + k) * P
                        last = nc.tensor.transpose(ps[:, T_BANK + b, k * P:(k + 1) * P], xn[:, t, f:f + P], ident[:, :])
                    last.then_inc(xT_in_psum, 1)

            def x_ready(joint, t):
                pe.wait_ge(xT_split, 4 * joint + 2 * t + 2)

            def ffn(sub):
                f, w0 = ffn_no(sub), w_of(sub)

                def gate_up(c, cs, t, turn):
                    first = 3 * cs - 1 if cs else 0
                    for half in range(2):
                        p = w0 + first + half
                        slot = p % RING
                        weights_ready(p + RING * turn)
                        for k4 in range(4):
                            k = 4 * half + k4
                            tok = slice(t * P, (t + 1) * P)
                            cols = slice(k4 * 512, (k4 + 1) * 512)
                            last = products(ps[:, GU_BANK + t, :], xT_high[:, k, tok], xT_low[:, k, tok],
                                            w_high[:, slot, cols], w_low[:, slot, cols], k == 0, k == KD - 1)
                        if t == 1:
                            last.then_inc(piece_used, 1)
                    if t == 0:
                        last.then_inc(gu_ready, 1)

                def transpose_h(c, t):
                    pe.wait_ge(h_ready, 2 * CHUNKS * f + 2 * c + t + 1)
                    for j in range(FT):
                        last = nc.tensor.transpose(ps[:, T_BANK + t, j * P:(j + 1) * P], h[:, t, j * P:(j + 1) * P],
                                                   ident[:, :])
                    last.then_inc(hT_in_psum, 1)

                def down(c, cs, t, turn):
                    p = w0 + 3 * (cs + 1) + 1 if cs < CHUNKS - 1 else w0 + FFN_PIECES - 1
                    slot = p % RING
                    weights_ready(p + RING * turn)
                    pe.wait_ge(hT_split, 2 * CHUNKS * f + 2 * c + t + 1)
                    for half in range(2):
                        for j in range(FT):
                            cols = slice(j * D + half * 512, j * D + half * 512 + 512)
                            last = products(ps[:, Y_BANK + 2 * t + half, :], hT_hi[:, t, j * P:(j + 1) * P],
                                            hT_lo[:, t, j * P:(j + 1) * P], w_high[:, slot, cols],
                                            w_low[:, slot, cols], cs == 0 and j == 0,
                                            cs == CHUNKS - 1 and j == FT - 1)
                    if t == 1:
                        last.then_inc(piece_used, 1)
                    elif cs == CHUNKS - 1:
                        last.then_inc(y_ready, 1)

                def chunk(c, cs, turn):
                    gate_up(c, cs, 0, turn)
                    transpose_h(c - 1, 1)
                    down(c - 1, cs - 1, 0, turn)
                    gate_up(c, cs, 1, turn)
                    transpose_h(c, 0)
                    down(c - 1, cs - 1, 1, turn)

                transpose_x(sub, 0)
                x_ready(sub, 0)
                gate_up(0, 0, 0, 0)
                transpose_x(sub, 1)
                x_ready(sub, 1)
                gate_up(0, 0, 1, 0)
                transpose_h(0, 0)
                chunk(1, 1, 0)
                with pe.Fori(0, (CHUNKS - 3) // 2) as turn:
                    chunk(2 * turn + 2, 2, turn)
                    chunk(2 * turn + 3, 3, turn)
                chunk(CHUNKS - 1, CHUNKS - 1, 0)
                transpose_h(CHUNKS - 1, 1)
                down(CHUNKS - 1, CHUNKS - 1, 0, 0)
                down(CHUNKS - 1, CHUNKS - 1, 1, 0)

            def project_out(sub):
                p0 = w_of(sub + 1) - OUT_PIECES
                pe.wait_ge(oT_split, ot_before(sub + 1))
                for t in range(TILES):
                    tok = slice(t * P, (t + 1) * P)
                    for q in range(OUT_PIECES):
                        slot = (p0 + q) % RING
                        weights_ready(p0 + q)
                        for k in range(KD):
                            cols = slice(k * 256, (k + 1) * 256)
                            last = products(ps[:, Y_BANK + 2 * t + q // 2, q % 2 * 256:q % 2 * 256 + 256],
                                            oT_hi[:, k, tok], oT_lo[:, k, tok], w_high[:, slot, cols],
                                            w_low[:, slot, cols], k == 0, k == KD - 1)
                        if t == 1:
                            last.then_inc(piece_used, 1)
                    if t == 0:
                        last.then_inc(y_ready, 1)

            def features_first(slot, bank, turned=False):
                for j in range(2):
                    for k in range(KD):
                        cols = slice(k * 256 + j * P, k * 256 + (j + 1) * P)
                        last = products(ps[:, bank, j * SEQ:(j + 1) * SEQ], w_high[:, slot, cols],
                                        w_low[:, slot, cols], xT_high[:, k, :], xT_low[:, k, :],
                                        k == 0, k == KD - 1)
                return last

            def tokens_first(slot, acc, t):
                for k in range(KD):
                    tok, cols = slice(t * P, (t + 1) * P), slice(k * 256, (k + 1) * 256)
                    last = products(acc, xT_high[:, k, tok], xT_low[:, k, tok], w_high[:, slot, cols],
                                    w_low[:, slot, cols], k == 0, k == KD - 1)
                return last

            def conv(sub):
                w0 = w_of(sub)
                for t in range(TILES):
                    transpose_x(sub, t)
                    x_ready(sub, t)
                with pe.Fori(0, CONV_STEPS // 2) as turn:
                    for s in range(2):
                        for part in range(3):
                            p = w0 + 3 * s + part
                            weights_ready(p + RING * turn)
                            features_first(p % RING, 4 * s + part).then_inc(piece_used, 1)
                project_out(sub)

            def attention(sub):
                w0 = w_of(sub)
                for t in range(TILES):
                    transpose_x(sub, t)
                    x_ready(sub, t)

                def project(quarter, qs, turn):
                    def transpose_qk(i, t):
                        n = 2 * (i // 3 * 2 + i % 3) + t
                        pe.wait_ge(rope_done, 4 * NG * quarter + n + 1)
                        if n >= 2:
                            pe.wait_ge(qkT_done, 4 * NG * quarter + n - 1)
                        for j in range(2):
                            last = nc.tensor.transpose(ps[:, 4 + t, j * P:(j + 1) * P], qk[:, i % 2, t, j * P:(j + 1) * P],
                                                       ident[:, :])
                        last.then_inc(qkT_in_psum, 1)

                    for i in range(QP):
                        p = w0 + QP * qs + i
                        weights_ready(p + 3 * RING * turn)
                        for t in range(TILES):
                            if i >= 2:
                                pe.wait_ge(proj_copied, 2 * QP * quarter + 2 * (i - 2) + t + 1)
                            last = tokens_first(p % RING, ps[:, (2 * i + t) % 4, 0:256], t)
                            last.then_inc(proj_ready if t == 0 else piece_used, 1)
                            if i % 3:
                                transpose_qk(i - 1, t)

                def attend(quarter, qs):
                    def scores(hh):
                        rows, j = slice(hh % 2 * HD, hh % 2 * HD + HD), hh // 2
                        if hh >= 1:
                            pe.wait_ge(masked, QH * quarter + hh)
                        for g in range(NG):
                            nc.tensor.matmul(ps[:, g // 2, g % 2 * 256:g % 2 * 256 + 256], qT[rows, g, j, P:2 * P],
                                             kT[rows, g, j, :], start=True, stop=True)
                            last = nc.tensor.matmul(ps[:, 2, g * P:(g + 1) * P], qT[rows, g, j, 0:P],
                                                    kT[rows, g, j, 0:P], start=True, stop=True)
                        last.then_inc(scores_ready, 1)

                    def transpose_probs(hh):
                        pe.wait_ge(probs_ready, QH * quarter + hh + 1)
                        for g in range(NG):
                            for n in range(3):
                                last = nc.tensor.transpose(ps[:, 3 + g, n * P:(n + 1) * P],
                                                           probs[hh % 2][:, g, n * P:(n + 1) * P], ident[:, :])
                        last.then_inc(pT_in_psum, 1)

                    def times_v(hh):
                        pe.wait_ge(pT_done, QH * quarter + hh + 1)
                        cols = slice(hh * HD, (hh + 1) * HD)
                        rows = slice(hh % 2 * HD, hh % 2 * HD + HD)
                        bank = 6 + hh // 2
                        if hh % 2 == 0:
                            pe.wait_ge(oT_split, ot_before(sub) + 2 * quarter)
                        for g in range(NG):
                            nc.tensor.matmul(ps[rows, bank, 0:SEQ], v[:, g, 0, cols], pT[:, g, 0:2 * P],
                                             start=g == 0, stop=False, skip_group_check=True)
                            last = nc.tensor.matmul(ps[rows, bank, P:SEQ], v[:, g, 1, cols], pT[:, g, 2 * P:3 * P],
                                                    start=False, stop=g == NG - 1, skip_group_check=True)
                        if hh % 2:
                            last.then_inc(o_ready, 1)

                    pe.wait_ge(proj_copied, 2 * QP * (quarter + 1))
                    pe.wait_ge(qkT_done, 4 * NG * (quarter + 1))
                    scores(0)
                    for hh in range(QH):
                        if hh + 1 < QH:
                            scores(hh + 1)
                        if hh:
                            times_v(hh - 1)
                        transpose_probs(hh)
                    times_v(QH - 1)

                with pe.Fori(0, QUARTERS // 2) as turn:
                    for qs in range(2):
                        project(2 * turn + qs, qs, turn)
                        attend(2 * turn + qs, qs)
                project_out(sub)

            def mlstm(sub):
                w0 = w_of(sub)
                for t in range(TILES):
                    transpose_x(sub, t)
                    x_ready(sub, t)
                pe.wait_ge(gw_split, 1)
                for t in range(TILES):
                    tok = slice(t * P, (t + 1) * P)
                    for k in range(KD):
                        last = products(ps[:, 6, t * 2 * NH:(t + 1) * 2 * NH], xT_high[:, k, tok], xT_low[:, k, tok],
                                        gw_high[:, k, :], gw_low[:, k, :], k == 0, k == KD - 1)
                last.then_inc(gates_in_psum, 1)

                def feature_piece(i):
                    weights_ready(w0 + i)
                    features_first((w0 + i) % RING, i % 4).then_inc(piece_used, 1)

                def token_piece(i):
                    weights_ready(w0 + i)
                    pe.wait_ge(ml_copied, i - 4 + 1)
                    for t in range(TILES):
                        last = tokens_first((w0 + i) % RING, ps[:, i % 4, t * 256:(t + 1) * 256], t)
                    last.then_inc(piece_used, 1)

                def scores(n):
                    if n >= 2:
                        pe.wait_ge(a_ready, n - 1)
                    nc.tensor.matmul(ps[:, 6 + n % 2, 0:P], mqT[:, n, 0:P], mkT[:, n, 0:P], start=True, stop=True)
                    nc.tensor.matmul(ps[:, 6 + n % 2, P:3 * P], mqT[:, n, P:2 * P], mkT[:, n, :], start=True,
                                     stop=True).then_inc(ml_scores, 1)

                def transpose_a(n):
                    pe.wait_ge(a_ready, n + 1)
                    if n >= 2:
                        pe.wait_ge(aT_done, n - 1)
                    for j in range(3):
                        last = nc.tensor.transpose(ps[:, 4 + n % 2, j * P:(j + 1) * P], a[:, n % 2, j * P:(j + 1) * P],
                                                   ident[:, :])
                    last.then_inc(aT_in_psum, 1)

                def numerator(n):
                    pe.wait_ge(aT_done, n + 1)
                    if n >= 2:
                        pe.wait_ge(mh_scaled, 2 * (n - 1))
                    nc.tensor.matmul(ps[:, 6 + n % 2, 0:DV], aT[:, n, 0:P], mv[:, n, 0, :], start=True, stop=True)
                    for s in range(2):
                        last = nc.tensor.matmul(ps[:, 6 + n % 2, DV:2 * DV], aT[:, n, (s + 1) * P:(s + 2) * P],
                                                mv[:, n, s, :], start=s == 0, stop=s == 1)
                    last.then_inc(num_ready, 1)

                def transpose_out(n):
                    pe.wait_ge(mh_scaled, 2 * n + 2)
                    pe.wait_ge(aT_done, NH)
                    if n >= 2:
                        pe.wait_ge(oT_split, ot_before(sub) + n - 1)
                    for j in range(2):
                        for t in range(TILES):
                            last = nc.tensor.transpose(ps[:, 4 + n % 2, j * SEQ + t * P:j * SEQ + (t + 1) * P],
                                                       mh[:, n % 2, t, j * P:(j + 1) * P], ident[:, :])
                    last.then_inc(mhT_in_psum, 1)

                feature_piece(0)
                feature_piece(1)
                pe.wait_ge(lf_ready, 1)
                nc.tensor.matmul(ps[:, 7, 0:NH], tri[:, :], lf[:, 0, :], start=True, stop=True)
                nc.tensor.matmul(ps[:, 7, NH:2 * NH], ones[:, :], lf[:, 0, :], start=True, stop=False)
                nc.tensor.matmul(ps[:, 7, NH:2 * NH], tri[:, :], lf[:, 1, :], start=False,
                                 stop=True).then_inc(cum_in_psum, 1)
                feature_piece(2)
                feature_piece(3)
                for n in range(NH):
                    pe.wait_ge(diag_ready, n + 1)
                    nc.tensor.matmul(ps[:, 4 + n // 2, n % 2 * SEQ:n % 2 * SEQ + SEQ], ones[:, :], diag[:, n % 2, :],
                                     start=True, stop=True).then_inc(rows_in_psum, 1)
                for n in range(NH):
                    token_piece(4 + n)
                    if n == 0:
                        pe.wait_ge(ml_copied, 4)
                        pe.wait_ge(ml_max_ready, 1)
                    scores(n)
                    if n:
                        transpose_a(n - 1)
                for n in range(NH):
                    token_piece(8 + n)
                    if n == 0:
                        transpose_a(NH - 1)
                    numerator(n)
                    if n:
                        transpose_out(n - 1)
                transpose_out(NH - 1)
                project_out(sub)

            program = {"ffn": ffn, "conv": conv, "att": attention, "ml": mlstm}
            for sub, kind in enumerate(KINDS):
                program[kind](sub)

        @block.scalar
        def _(act):
            act.dma_start(ident[:, :], ident_in).then_inc(loaded, 16)
            act.dma_start(gain[:, 1, :], gains[0].partition_broadcast(P)).then_inc(gain_landed, 16)
            act.dma_start(conv_kT[:, :, :, :], conv_k).then_inc(loaded, 16)
            act.dma_start(rope[:, :, :, :], rope_in).then_inc(loaded, 16)
            act.dma_start(att_mask[:, :, :], att_mask_in).then_inc(loaded, 16)
            act.dma_start(ml_mask[:, :], ml_mask_in).then_inc(loaded, 16)
            act.dma_start(tri[:, :], tri_in).then_inc(loaded, 16)
            act.dma_start(gw_raw[:, :, :], gate_w).then_inc(loaded, 16)
            act.dma_start(gate_bias[:, :], gate_b.partition_broadcast(P)).then_inc(loaded, 16)

            def high(p, turn=0):
                if p >= PIECES:
                    return
                act.wait_ge(raw_landed[p % RAW], 16 * (p // RAW + 1) + 32 * turn)
                if p >= RING:
                    act.wait_ge(piece_used, p - RING + 1 + RING * turn)
                nc.scalar.activation(w_high[:, p % RING, :], raw[:, p % RAW, :], ACT.Copy).then_inc(piece_high, 1)

            def square_y(joint, t):
                if t == 0:
                    act.wait_ge(y_ready, joint)
                else:
                    act.wait_ge(piece_used, BASE[joint])
                y = ps[:, Y_BANK + 2 * t:Y_BANK + 2 * t + 2, :].rearrange("p a b -> p (a b)")
                nc.scalar.activation(xn[:, t, :], y, ACT.Square, scale=1.0 / 32,
                                     accum_out=mean_y[:, t:t + 1]).then_inc(y_mean, 1)

            def square_x(joint, t):
                if joint:
                    act.wait_ge(x_updated, TILES * (joint - 1) + t + 1)
                else:
                    act.wait_ge(loaded, CONSTS)
                nc.scalar.activation(xn[:, t, :], x[:, t, :], ACT.Square, scale=1.0 / 32,
                                     accum_out=mean_x[:, t:t + 1]).then_inc(x_mean, 1)

            def xT(joint, t):
                for b in range(2):
                    act.wait_ge(xT_in_psum, 4 * joint + 2 * t + b + 1)
                    nc.scalar.activation(xT_high[:, 4 * b:4 * b + 4, t * P:(t + 1) * P],
                                         ps[:, T_BANK + b, :].rearrange("p (k c) -> p k c", k=4),
                                         ACT.Copy).then_inc(xT_high_done, 1)

            def joint_part(joint, between):
                if interleaved(joint):
                    if joint:
                        for t in range(TILES):
                            square_y(joint, t)
                    if joint < SUBLAYERS:
                        for t in range(TILES):
                            square_x(joint, t)
                        for t in range(TILES):
                            xT(joint, t)
                else:
                    for t in range(TILES):
                        square_y(joint, t)
                        square_x(joint, t)
                        xT(joint, t)
                        if t == 0:
                            between()
                if joint < SUBLAYERS:
                    act.dma_start(gain[:, 0, :], gains[2 * joint + 1].partition_broadcast(P)).then_inc(gain_landed, 16)
                    if joint + 1 < SUBLAYERS:
                        act.dma_start(gain[:, 1, :], gains[2 * joint + 2].partition_broadcast(P)).then_inc(gain_landed, 16)

            def ffn(sub):
                f, w0 = ffn_no(sub), w_of(sub)

                def silu_of(c, t):
                    if t == 0:
                        act.wait_ge(gu_ready, CHUNKS * f + c + 1)
                    else:
                        act.wait_ge(piece_used, w0 + (2 if isinstance(c, int) and c == 0 else 3 * c + 1))
                    nc.scalar.activation(silu[:, t, :], ps[:, GU_BANK + t, 0:CHUNK], ACT.Silu).then_inc(silu_done, 1)

                def hT(c, t):
                    act.wait_ge(hT_in_psum, 2 * CHUNKS * f + 2 * c + t + 1)
                    nc.scalar.activation(hT_hi[:, t, :], ps[:, T_BANK + t, 0:CHUNK], ACT.Copy).then_inc(hT_high_done, 1)

                def chunk(c, cs, turn):
                    p = w0 + 3 * cs + 2
                    silu_of(c - 1, 1)
                    high(p, turn)
                    hT(c - 1, 1)
                    high(p + 1, turn)
                    silu_of(c, 0)
                    high(p + 2, turn)
                    hT(c, 0)

                silu_of(0, 0)
                hT(0, 0)
                chunk(1, 1, 0)
                with act.Fori(0, (CHUNKS - 3) // 2) as turn:
                    chunk(2 * turn + 2, 2, turn)
                    chunk(2 * turn + 3, 3, turn)
                chunk(CHUNKS - 1, CHUNKS - 1, 0)
                silu_of(CHUNKS - 1, 1)
                high(w0 + FFN_PIECES + 2)
                hT(CHUNKS - 1, 1)
                high(w0 + FFN_PIECES + 3)

            def conv(sub):
                w0, n0 = w_of(sub), CONV_STEPS * conv_no(sub)
                with act.Fori(0, CONV_STEPS // 2) as turn:
                    for s in range(2):
                        p = w0 + 3 * s
                        act.wait_ge(piece_used, p + 1 + RING * turn)
                        nc.scalar.activation(c_sb.rearrange("p a b -> p (a b)"), ps[:, 4 * s, :], ACT.Copy).then_inc(c_copied, 1)
                        high(p + 5, turn)
                        high(p + 6, turn)
                        high(p + 7, turn)
                        act.wait_ge(conv_ready, n0 + s + 1 + 2 * turn)
                        nc.scalar.activation(oT_hi[:, bass.ds(4 * turn + 2 * s, 2), :], z, ACT.Copy).then_inc(oT_high_done, 1)

            def attention(sub):
                w0 = w_of(sub)

                def project(quarter, qs, turn):
                    def copy_out(i, t):
                        p = w0 + QP * qs + i
                        if t == 0:
                            act.wait_ge(proj_ready, QP * quarter + i + 1)
                        else:
                            act.wait_ge(piece_used, p + 1 + 3 * RING * turn)
                        to = v[:, i // 3, t, :] if i % 3 == 2 else qk[:, i % 2, t, :]
                        nc.scalar.activation(to, ps[:, (2 * i + t) % 4, 0:256], ACT.Copy).then_inc(proj_copied, 1)

                    def copy_qkT(i, t):
                        act.wait_ge(qkT_in_psum, 4 * NG * quarter + 2 * (i // 3 * 2 + i % 3) + t + 1)
                        to = (kT if i % 3 else qT)[:, i // 3, :, t * P:(t + 1) * P]
                        nc.scalar.activation(to, ps[:, 4 + t, 0:2 * P].rearrange("p (j c) -> p j c", j=2),
                                             ACT.Copy).then_inc(qkT_done, 1)

                    for i in range(QP):
                        for t in range(TILES):
                            copy_out(i, t)
                            if i % 3:
                                copy_qkT(i - 1, t)
                        high(w0 + QP * qs + i + 5, 3 * turn)

                def attend(quarter, qs):
                    def exp(hh):
                        pr = probs[hh % 2]
                        act.wait_ge(max_ready, QH * quarter + hh + 1)
                        for t, cols in ((1, slice(P, 3 * P)), (0, slice(0, P))):
                            last = nc.scalar.activation(pr[:, :, cols], pr[:, :, cols], ACT.Exp, scale=HD ** -0.5,
                                                        bias=nmax[:, hh % 2, t:t + 1], accum_out=den[:, hh % 2, t:t + 1])
                        last.then_inc(exp_done, 1)

                    exp(0)
                    for hh in range(QH):
                        act.wait_ge(pT_in_psum, QH * quarter + hh + 1)
                        nc.scalar.activation(pT, ps[:, 3:6, 0:3 * P], ACT.Copy).then_inc(pT_done, 1)
                        if hh + 1 < QH:
                            exp(hh + 1)
                        if hh % 2 == 0 and hh:
                            o_high(quarter, qs, hh // 2 - 1)
                    o_high(quarter, qs, QH // 2 - 1)

                def o_high(quarter, qs, j):
                    act.wait_ge(o_ready, 2 * quarter + j + 1)
                    nc.scalar.activation(oT_hi[:, bass.ds(2 * quarter + j, 1), :].rearrange("p a b -> p (a b)"),
                                         ps[:, 6 + j, 0:SEQ], ACT.Copy).then_inc(oT_high_done, 1)

                with act.Fori(0, QUARTERS // 2) as turn:
                    for qs in range(2):
                        project(2 * turn + qs, qs, turn)
                        attend(2 * turn + qs, qs)

            def mlstm(sub):
                w0 = w_of(sub)
                nc.scalar.activation(gw_high[:, :, :], gw_raw[:, :, :], ACT.Copy).then_inc(gw_high_done, 1)
                act.wait_ge(gate_step, 3)
                nc.scalar.activation(exp_f, neg_abs, ACT.Exp).then_inc(gate_exp, 1)
                act.wait_ge(gate_exp, 1)
                nc.scalar.activation(ln_f, exp_f, ACT.Ln, bias=1.0).then_inc(gate_ln, 1)

                def copy_out(i):
                    act.wait_ge(piece_used, w0 + i + 1)
                    if i < 4:
                        to = (mqT if i < 2 else mkT)[:, 2 * (i % 2):2 * (i % 2) + 2, :].rearrange("p a b -> p (a b)")
                        nc.scalar.activation(to, ps[:, i % 4, :], ACT.Copy, scale=1.0 if i < 2 else DQK ** -0.5)\
                          .then_inc(ml_copied, 1)
                    elif i < 8:
                        nc.scalar.activation(mv[:, i - 4, :, :].rearrange("p a b -> p (a b)"), ps[:, i % 4, :],
                                             ACT.Copy).then_inc(ml_copied, 1)
                    else:
                        nc.scalar.activation(mog[:, i - 8, :, :].rearrange("p a b -> p (a b)"), ps[:, i % 4, :],
                                             ACT.Sigmoid).then_inc(ml_copied, 1)

                def decay_of(n):
                    if n >= 2:
                        act.wait_ge(a_ready, n - 1)
                    act.wait_ge(ml_max_ready, 1)
                    if n == 0:
                        act.wait_ge(ml_floor_sum, 1)
                        nc.scalar.activation(floor_e, floor_in, ACT.Exp).then_inc(ml_floor, 1)
                    nc.scalar.activation(decay[:, n % 2, 0:P], masked_row(n, 0), ACT.Exp, bias=neg_m[:, n, 0:1])
                    nc.scalar.activation(decay[:, n % 2, P:3 * P], masked_row(n, 1), ACT.Exp,
                                         bias=neg_m[:, n, 1:2]).then_inc(decay_ready, 1)

                def copy_aT(n):
                    act.wait_ge(aT_in_psum, n + 1)
                    nc.scalar.activation(aT[:, n, :], ps[:, 4 + n % 2, 0:3 * P], ACT.Copy).then_inc(aT_done, 1)

                def o_high(n):
                    act.wait_ge(mhT_in_psum, n + 1)
                    nc.scalar.activation(oT_hi[:, 2 * n:2 * n + 2, :].rearrange("p a b -> p (a b)"), ps[:, 4 + n % 2, :],
                                         ACT.Copy).then_inc(oT_high_done, 1)

                for i in range(4):
                    copy_out(i)
                    high(w0 + i + 5)
                decay_of(0)
                for n in range(NH):
                    if n + 1 < NH:
                        decay_of(n + 1)
                    copy_out(4 + n)
                    high(w0 + 4 + n + 5)
                    if n:
                        copy_aT(n - 1)
                for n in range(NH):
                    copy_out(8 + n)
                    if n == 0:
                        copy_aT(NH - 1)
                    high(w0 + 8 + n + 5)
                    if n:
                        o_high(n - 1)
                o_high(NH - 1)

            program = {"ffn": ffn, "conv": conv, "att": attention, "ml": mlstm}
            act.wait_ge(loaded, CONSTS)
            for p in range(4):
                high(p)
            for sub, kind in enumerate(KINDS):
                w0 = w_of(sub)
                after_ffn = sub == 0 or KINDS[sub - 1] == "ffn"
                joint_part(sub, lambda: high(w0 + 1))
                for p in range(4 if after_ffn else 2, 5):
                    high(w0 + p)
                program[kind](sub)
            joint_part(SUBLAYERS, None)

        @block.vector
        def _(dve):
            nc.vector.memset(minus_half[:, :], -0.5).then_inc(consts_set, 1)
            nc.vector.memset(ones[:, :], 1.0).then_inc(consts_set, 1)

            def low(p, turn=0):
                if p >= PIECES:
                    return
                dve.wait_ge(piece_high, p + 1 + RING * turn)
                nc.vector.tensor_tensor(w_low[:, p % RING, :], raw[:, p % RAW, :], w_high[:, p % RING, :],
                                        ALU.subtract).then_inc(piece_split, 1)

            def update_x(joint, t):
                n = TILES * (joint - 1) + t + 1
                dve.wait_ge(y_rstd, n)
                dve.wait_ge(gain_landed, 16 * min(1 + 2 * joint, 2 * SUBLAYERS))
                y = ps[:, Y_BANK + 2 * t:Y_BANK + 2 * t + 2, :].rearrange("p a b -> p (a b)")
                nc.vector.scalar_tensor_tensor(out=xn[:, t, :], in0=y, scalar=rstd_y[:, t:t + 1], in1=gain[:, 0, :],
                                               op0=ALU.mult, op1=ALU.mult).then_inc(y_scaled, 1)
                dve.wait_ge(y_scaled, n)
                scale = 0.5 if KINDS[joint - 1] == "ffn" else 1.0
                nc.vector.scalar_tensor_tensor(out=x[:, t, :], in0=xn[:, t, :], scalar=scale, in1=x[:, t, :],
                                               op0=ALU.mult, op1=ALU.add).then_inc(x_updated, 1)

            def pre_norm(joint, t):
                dve.wait_ge(x_rstd, TILES * joint + t + 1)
                if joint == 0:
                    dve.wait_ge(gain_landed, 16)
                nc.vector.scalar_tensor_tensor(out=xn[:, t, :], in0=x[:, t, :], scalar=rstd_x[:, t:t + 1],
                                               in1=gain[:, 1, :], op0=ALU.mult, op1=ALU.mult).then_inc(xn_ready, 1)

            def xT(joint, t):
                for b in range(2):
                    dve.wait_ge(xT_high_done, 4 * joint + 2 * t + b + 1)
                    cols = slice(t * P, (t + 1) * P)
                    nc.vector.tensor_tensor(xT_low[:, 4 * b:4 * b + 4, cols],
                                            ps[:, T_BANK + b, :].rearrange("p (k c) -> p k c", k=4),
                                            xT_high[:, 4 * b:4 * b + 4, cols], ALU.subtract).then_inc(xT_split, 1)

            def joint_part(joint, between):
                if interleaved(joint):
                    if joint:
                        for t in range(TILES):
                            update_x(joint, t)
                    if joint < SUBLAYERS:
                        for t in range(TILES):
                            pre_norm(joint, t)
                            xT(joint, t)
                else:
                    for t in range(TILES):
                        update_x(joint, t)
                        pre_norm(joint, t)
                        xT(joint, t)
                        if t == 0:
                            between()

            def ffn(sub):
                f, w0 = ffn_no(sub), w_of(sub)

                def times_up(c, t):
                    dve.wait_ge(silu_done, 2 * CHUNKS * f + 2 * c + t + 1)
                    nc.vector.tensor_tensor(h[:, t, :], silu[:, t, :], ps[:, GU_BANK + t, CHUNK:2 * CHUNK],
                                            ALU.mult).then_inc(h_ready, 1)

                def hT(c, t):
                    dve.wait_ge(hT_high_done, 2 * CHUNKS * f + 2 * c + t + 1)
                    nc.vector.tensor_tensor(hT_lo[:, t, :], ps[:, T_BANK + t, 0:CHUNK], hT_hi[:, t, :],
                                            ALU.subtract).then_inc(hT_split, 1)

                def chunk(c, cs, turn):
                    p = w0 + 3 * cs + 2
                    times_up(c - 1, 1)
                    low(p, turn)
                    hT(c - 1, 1)
                    low(p + 1, turn)
                    times_up(c, 0)
                    low(p + 2, turn)
                    hT(c, 0)

                times_up(0, 0)
                hT(0, 0)
                chunk(1, 1, 0)
                with dve.Fori(0, (CHUNKS - 3) // 2) as turn:
                    chunk(2 * turn + 2, 2, turn)
                    chunk(2 * turn + 3, 3, turn)
                chunk(CHUNKS - 1, CHUNKS - 1, 0)
                times_up(CHUNKS - 1, 1)
                low(w0 + FFN_PIECES + 2)
                hT(CHUNKS - 1, 1)
                low(w0 + FFN_PIECES + 3)

            def conv(sub):
                w0, layer = w_of(sub), conv_no(sub)
                n0, o0 = CONV_STEPS * layer, ot_before(sub)
                nc.vector.memset(cu[:, :, 0:2], 0.0).then_inc(pads_zeroed, 1)
                dve.wait_ge(pads_zeroed, layer + 1)
                with dve.Fori(0, CONV_STEPS // 2) as turn:
                    for s in range(2):
                        p, n = w0 + 3 * s, n0 + s + 2 * turn
                        low(p + 5, turn)
                        dve.wait_ge(c_copied, n + 1)
                        dve.wait_ge(piece_used, p + 2 + RING * turn)
                        nc.vector.tensor_tensor(cu[:, :, 2:SEQ + 2], c_sb,
                                                ps[:, 4 * s + 1, :].rearrange("p (j c) -> p j c", j=2),
                                                ALU.mult).then_inc(cu_ready, 1)
                        dve.wait_ge(cu_ready, n + 1)
                        taps = 2 * CONV_W * n
                        for j in range(CONV_W):
                            for e in range(2):
                                k = conv_kT[:, layer, j, bass.ds(4 * turn + 2 * s + e, 1)]
                                shifted = cu[:, e, CONV_W - 1 - j:CONV_W - 1 - j + SEQ]
                                if j == 0:
                                    tap = nc.vector.tensor_scalar(z[:, e, :], shifted, k, None, ALU.mult)
                                else:
                                    dve.wait_ge(tap_done, taps + 2 * (j - 1) + e + 1)
                                    tap = nc.vector.scalar_tensor_tensor(out=z[:, e, :], in0=shifted, scalar=k,
                                                                         in1=z[:, e, :], op0=ALU.mult, op1=ALU.add)
                                tap.then_inc(tap_done, 1)
                        low(p + 6, turn)
                        dve.wait_ge(piece_used, p + 3 + RING * turn)
                        dve.wait_ge(tap_done, taps + 2 * CONV_W)
                        nc.vector.tensor_tensor(z, z, ps[:, 4 * s + 2, :].rearrange("p (j c) -> p j c", j=2),
                                                ALU.mult).then_inc(conv_ready, 1)
                        low(p + 7, turn)
                        dve.wait_ge(oT_high_done, o0 + s + 1 + 2 * turn)
                        block_at = bass.ds(4 * turn + 2 * s, 2)
                        nc.vector.tensor_tensor(oT_lo[:, block_at, :], z, oT_hi[:, block_at, :],
                                                ALU.subtract).then_inc(oT_split, 1)

            def attention(sub):
                w0, o0 = w_of(sub), ot_before(sub)

                def rotate(quarter, i, t):
                    n = 2 * (i // 3 * 2 + i % 3) + t
                    dve.wait_ge(proj_copied, 2 * QP * quarter + 2 * i + t + 1)
                    q = qk[:, i % 2, t, :].rearrange("p (h c) -> p h c", h=QH)
                    cos, sin = (rope[:, t, e, :].rearrange("p (h c) -> p h c", h=QH) for e in range(2))
                    by_cos, by_sin = rope_c[t], rope_s[t]
                    if n >= 2:
                        dve.wait_ge(rope_done, 4 * NG * quarter + n - 1)
                    nc.vector.tensor_tensor(by_cos, q[:, :, 0:ROT], cos, ALU.mult)
                    nc.vector.tensor_tensor(by_sin, q[:, :, 0:ROT], sin, ALU.mult).then_inc(rope_products, 1)
                    dve.wait_ge(rope_products, 4 * NG * quarter + n + 1)
                    half = ROT // 2
                    nc.vector.tensor_tensor(q[:, :, 0:half], by_cos[:, :, 0:half], by_sin[:, :, half:ROT], ALU.subtract)
                    nc.vector.tensor_tensor(q[:, :, half:ROT], by_cos[:, :, half:ROT], by_sin[:, :, 0:half],
                                            ALU.add).then_inc(rope_done, 1)

                def attend(quarter, qs):
                    for hh in range(QH):
                        n, pr = QH * quarter + hh, probs[hh % 2]
                        dve.wait_ge(loaded, CONSTS)
                        dve.wait_ge(scores_ready, n + 1)
                        nc.vector.memset(den[:, hh % 2, :], 0.0)
                        s1 = ps[:, 0:2, :].rearrange("p a b -> p (a b)")[:, 0:NG * 2 * P].rearrange("p (g c) -> p g c", g=NG)
                        nc.vector.tensor_tensor_reduce(pr[:, :, P:3 * P], s1, att_mask[:, :, :], 1.0, MASK_LOW, ALU.add,
                                                       ALU.max, smax[:, hh % 2, 1:2])
                        s0 = ps[:, 2, 0:NG * P].rearrange("p (g c) -> p g c", g=NG)
                        nc.vector.tensor_tensor_reduce(pr[:, :, 0:P], s0, att_mask[:, :, P:2 * P], 1.0, MASK_LOW,
                                                       ALU.add, ALU.max, smax[:, hh % 2, 0:1]).then_inc(masked, 1)
                        dve.wait_ge(masked, n + 1)
                        nc.vector.tensor_scalar(nmax[:, hh % 2, :], smax[:, hh % 2, :], -HD ** -0.5, None,
                                                ALU.mult).then_inc(max_ready, 1)
                        dve.wait_ge(exp_done, n + 1)
                        nc.vector.reciprocal(rden[:, hh % 2, :], den[:, hh % 2, :]).then_inc(recip_done, 1)
                        dve.wait_ge(recip_done, n + 1)
                        nc.vector.tensor_scalar(pr[:, :, 0:P], pr[:, :, 0:P], rden[:, hh % 2, 0:1], None, ALU.mult)
                        nc.vector.tensor_scalar(pr[:, :, P:3 * P], pr[:, :, P:3 * P], rden[:, hh % 2, 1:2], None,
                                                ALU.mult).then_inc(probs_ready, 1)
                    for j in range(QH // 2):
                        o_low(quarter, j)

                def o_low(quarter, j):
                    dve.wait_ge(oT_high_done, o0 + 2 * quarter + j + 1)
                    at = bass.ds(2 * quarter + j, 1)
                    nc.vector.tensor_tensor(oT_lo[:, at, :].rearrange("p a b -> p (a b)"), ps[:, 6 + j, 0:SEQ],
                                            oT_hi[:, at, :].rearrange("p a b -> p (a b)"),
                                            ALU.subtract).then_inc(oT_split, 1)

                with dve.Fori(0, QUARTERS // 2) as turn:
                    for qs in range(2):
                        quarter = 2 * turn + qs
                        for i in range(QP):
                            if i % 3 < 2:
                                for t in range(TILES):
                                    rotate(quarter, i, t)
                            low(w0 + QP * qs + i + 5, 3 * turn)
                        attend(quarter, qs)

            def mlstm(sub):
                w0, o0 = w_of(sub), ot_before(sub)
                dve.wait_ge(gw_high_done, 1)
                nc.vector.tensor_tensor(gw_low[:, :, :], gw_raw[:, :, :], gw_high[:, :, :], ALU.subtract).then_inc(gw_split, 1)
                dve.wait_ge(gates_in_psum, 1)
                for t in range(TILES):
                    step = nc.vector.tensor_tensor(gates[:, t, :], ps[:, 6, t * 2 * NH:(t + 1) * 2 * NH],
                                                   gate_bias[:, :], ALU.add)
                step.then_inc(gate_step, 1)
                forget = gates[:, :, NH:2 * NH]
                dve.wait_ge(gate_step, 1)
                nc.vector.tensor_scalar(neg_f, forget, -1.0, None, ALU.mult).then_inc(gate_step, 1)
                dve.wait_ge(gate_step, 2)
                nc.vector.tensor_tensor(neg_abs, forget, neg_f, ALU.min).then_inc(gate_step, 1)
                dve.wait_ge(gate_ln, 1)
                nc.vector.scalar_tensor_tensor(out=lf, in0=forget, scalar=0.0, in1=ln_f, op0=ALU.min,
                                               op1=ALU.subtract).then_inc(lf_ready, 1)
                low(w0 + 5)
                low(w0 + 6)
                dve.wait_ge(cum_in_psum, 1)
                nc.vector.tensor_copy(cum, ps[:, 7, 0:2 * NH].rearrange("p (t n) -> p t n", t=TILES)).then_inc(gate_step, 1)
                dve.wait_ge(gate_step, 4)
                nc.vector.tensor_tensor(r_col, gates[:, :, 0:NH], cum, ALU.subtract).then_inc(gate_step, 1)
                dve.wait_ge(gate_step, 5)
                for n in range(NH):
                    if n >= 2:
                        dve.wait_ge(rows_in_psum, n - 1)
                    for t in range(TILES):
                        last = nc.vector.tensor_scalar(diag[:, n % 2, t * P:(t + 1) * P], ident[:, :],
                                                       r_col[:, t, n:n + 1], None, ALU.mult)
                    last.then_inc(diag_ready, 1)
                low(w0 + 7)
                low(w0 + 8)
                for n in range(NH):
                    dve.wait_ge(rows_in_psum, n + 1 if n % 2 else n + 2)
                    rows = ps[:, 4 + n // 2, n % 2 * SEQ:n % 2 * SEQ + SEQ]
                    nc.vector.tensor_tensor_reduce(masked_row(n, 0), rows[:, 0:P], ml_mask[:, P:2 * P], 1.0, MASK_LOW,
                                                   ALU.add, ALU.max, rmax[:, n, 0:1])
                    last = nc.vector.tensor_tensor_reduce(masked_row(n, 1), rows, ml_mask[:, :], 1.0, MASK_LOW,
                                                          ALU.add, ALU.max, rmax[:, n, 1:2])
                last.then_inc(ml_masked, 1)
                dve.wait_ge(ml_masked, 1)
                nc.vector.tensor_scalar(neg_m, rmax, 0.0, -1.0, ALU.max, ALU.mult).then_inc(ml_max_ready, 1)
                dve.wait_ge(ml_max_ready, 1)
                nc.vector.tensor_tensor(floor_in, neg_m, cum.rearrange("p t n -> p n t"), ALU.subtract)\
                    .then_inc(ml_floor_sum, 1)

                def a_of(n):
                    dve.wait_ge(ml_scores, n + 1)
                    dve.wait_ge(decay_ready, n + 1)
                    if n >= 2:
                        dve.wait_ge(aT_in_psum, n - 1)
                    for t, cols in ((0, slice(0, P)), (1, slice(P, 3 * P))):
                        last = nc.vector.tensor_tensor_reduce(a[:, n % 2, cols], ps[:, 6 + n % 2, cols],
                                                              decay[:, n % 2, cols], 1.0, 0.0, ALU.mult, ALU.add,
                                                              mden[:, n, t:t + 1])
                    last.then_inc(a_ready, 1)
                    dve.wait_ge(a_ready, n + 1)
                    nc.vector.tensor_scalar(neg_den[:, n, :], mden[:, n, :], -1.0, None, ALU.mult).then_inc(den_step, 1)
                    dve.wait_ge(den_step, 4 * n + 1)
                    nc.vector.tensor_tensor(abs_den[:, n, :], mden[:, n, :], neg_den[:, n, :], ALU.max).then_inc(den_step, 1)
                    dve.wait_ge(den_step, 4 * n + 2)
                    dve.wait_ge(ml_floor, 1)
                    nc.vector.tensor_tensor(safe_den[:, n, :], abs_den[:, n, :], floor_e[:, n, :], ALU.max)\
                        .then_inc(den_step, 1)
                    dve.wait_ge(den_step, 4 * n + 3)
                    nc.vector.reciprocal(mrden[:, n, :], safe_den[:, n, :]).then_inc(den_step, 1)

                def gated_h(n):
                    dve.wait_ge(num_ready, n + 1)
                    dve.wait_ge(ml_copied, 8 + n + 1)
                    dve.wait_ge(den_step, 4 * n + 4)
                    if n >= 2:
                        dve.wait_ge(mhT_in_psum, n - 1)
                    for t in range(TILES):
                        nc.vector.scalar_tensor_tensor(out=mh[:, n % 2, t, :], in0=ps[:, 6 + n % 2, t * DV:(t + 1) * DV],
                                                       scalar=mrden[:, n, t:t + 1], in1=mog[:, n, t, :], op0=ALU.mult,
                                                       op1=ALU.mult).then_inc(mh_scaled, 1)

                def o_low(n):
                    dve.wait_ge(oT_high_done, o0 + n + 1)
                    nc.vector.tensor_tensor(oT_lo[:, 2 * n:2 * n + 2, :].rearrange("p a b -> p (a b)"),
                                            ps[:, 4 + n % 2, :], oT_hi[:, 2 * n:2 * n + 2, :].rearrange("p a b -> p (a b)"),
                                            ALU.subtract).then_inc(oT_split, 1)

                for n in range(NH):
                    a_of(n)
                    low(w0 + 9 + n)
                for n in range(NH):
                    gated_h(n)
                    low(w0 + 13 + n)
                    if n:
                        o_low(n - 1)
                o_low(NH - 1)

            program = {"ffn": ffn, "conv": conv, "att": attention, "ml": mlstm}
            for p in range(4):
                low(p)
            for sub, kind in enumerate(KINDS):
                w0 = w_of(sub)
                after_ffn = sub == 0 or KINDS[sub - 1] == "ffn"
                joint_part(sub, lambda: low(w0 + 1))
                for p in range(4 if after_ffn else 2, 5):
                    low(w0 + p)
                program[kind](sub)
            joint_part(SUBLAYERS, None)

        @block.gpsimd
        def _(pool):
            pool.wait_ge(consts_set, 1)
            steps = [0]

            def rstd(to, mean, n, arrived, value, done):
                pool.wait_ge(arrived, value)
                nc.gpsimd.tensor_scalar(mean_eps[:, n:n + 1], mean, EPS, None, ALU.add).then_inc(eps_added, 1)
                steps[0] += 1
                pool.wait_ge(eps_added, steps[0])
                nc.gpsimd.tensor_tensor(to, mean_eps[:, n:n + 1], minus_half[:, :], ALU.pow).then_inc(done, 1)

            def of_y(joint, t):
                rstd(rstd_y[:, t:t + 1], mean_y[:, t:t + 1], t, y_mean, TILES * (joint - 1) + t + 1, y_rstd)

            def of_x(joint, t):
                rstd(rstd_x[:, t:t + 1], mean_x[:, t:t + 1], TILES + t, x_mean, TILES * joint + t + 1, x_rstd)

            for joint in range(SUBLAYERS + 1):
                order = [(of_y, 0), (of_y, 1), (of_x, 0), (of_x, 1)] if interleaved(joint) else \
                    [(of_y, 0), (of_x, 0), (of_y, 1), (of_x, 1)]
                for of, t in order:
                    if of is of_y and joint == 0 or of is of_x and joint == SUBLAYERS:
                        continue
                    of(joint, t)


def lay_out(inputs):
    import numpy as np

    w = {k: np.asarray(v) for k, v in inputs.items()}
    stream = np.empty((PIECES, P, PIECE), np.float32)

    def columns(m, c, n):
        return m[:, c:c + n].reshape(KD, P, n).transpose(1, 0, 2)

    def put_out(p, m):
        for q in range(OUT_PIECES):
            stream[p + q] = columns(m, 256 * q, 256).reshape(P, PIECE)

    done = {"ffn": 0, "conv": 0, "att": 0, "ml": 0}
    for sub, kind in enumerate(KINDS):
        p, n = BASE[sub], done[kind]
        done[kind] += 1
        if kind == "ffn":
            name = "ffn1" if sub % 3 == 0 else "ffn2"
            wg, wu, wd = (w[f"{name}_{s}"][sub // 3] for s in ("wg", "wu", "wd"))
            for c in range(CHUNKS):
                at = p + (3 * c - 1 if c else 0)
                both = np.stack([columns(wg, c * CHUNK, CHUNK), columns(wu, c * CHUNK, CHUNK)], axis=2)
                for half in range(2):
                    stream[at + half] = both[:, 4 * half:4 * half + 4].reshape(P, PIECE)
                at = p + (3 * (c + 1) + 1 if c < CHUNKS - 1 else FFN_PIECES - 1)
                stream[at] = wd[c * CHUNK:(c + 1) * CHUNK].reshape(FT, P, D).transpose(1, 0, 2).reshape(P, PIECE)
        elif kind == "conv":
            for s in range(CONV_STEPS):
                for part, third in enumerate((1, 2, 0)):
                    stream[p + 3 * s + part] = columns(w["conv_w_in"][n], third * D + 256 * s, 256).reshape(P, PIECE)
            put_out(p + 3 * CONV_STEPS, w["conv_w_out"][n])
        elif kind == "att":
            for quarter in range(QUARTERS):
                for i in range(QP):
                    stream[p + QP * quarter + i] = columns(w["attn_w_in"][n], i * D + 256 * quarter, 256).reshape(P, PIECE)
            put_out(p + QP * QUARTERS, w["attn_w_out"][n])
        else:
            for i in range(12):
                stream[p + i] = columns(w["mlstm_w_in"][n], 256 * i, 256).reshape(P, PIECE)
            put_out(p + 12, w["mlstm_w_out"][n])

    gate_w = np.ascontiguousarray(columns(w["mlstm_w_in"][0], 12 * 256, 2 * NH))
    gate_b = np.concatenate([w["mlstm_b_i"][0], w["mlstm_b_f"][0]])
    conv_k = np.ascontiguousarray(w["conv_k"].reshape(2, CONV_W, KD, P).transpose(3, 0, 1, 2))

    inv = np.float32(500000.0) ** (-np.arange(0, ROT, 2, dtype=np.float32) / np.float32(ROT))
    ang = np.arange(SEQ, dtype=np.float32)[:, None] * inv[None, :].astype(np.float32)
    tables = np.stack([np.tile(np.cos(ang), (1, 2 * QH)), np.tile(np.sin(ang), (1, 2 * QH))], axis=1).astype(np.float32)
    rope = np.ascontiguousarray(tables.reshape(TILES, P, 2, QH * ROT).transpose(1, 0, 2, 3))
    q, k = np.arange(P)[:, None], np.arange(P)[None, :]
    att_mask = np.full((P, NG, 2 * P), NEG, np.float32)
    for g, (win, dil) in enumerate(GROUPS):
        for b, rel in enumerate((q + P - k, q - k)):
            att_mask[:, g, b * P:(b + 1) * P][(rel >= 0) & (rel % dil == 0) & (rel // dil <= win // dil)] = 0.0
    ml_mask = np.zeros((P, 2 * P), np.float32)
    ml_mask[:, P:][k > q] = NEG
    tri = np.triu(np.ones((P, P), np.float32))
    return {
        "x_in": w["x"].reshape(SEQ, D), "gains": w["norm_g"].reshape(-1, D), "stream": stream, "gate_w": gate_w,
        "gate_b": gate_b, "conv_k": conv_k, "ident_in": np.eye(P, dtype=np.float32), "rope_in": rope,
        "att_mask_in": att_mask, "ml_mask_in": ml_mask, "tri_in": tri,
    }


def kernel(**inputs):
    import concourse.bacc as bacc
    from concourse.bass_utils import run_bass_kernel_spmd

    nc = bacc.Bacc("TRN2", target_bir_lowering=False, num_devices=1, dynamic_dma_scratch_size=1024)
    arrays = lay_out(inputs)
    aps = {n: nc.dram_tensor(n, a.shape, F32, kind="ExternalInput").ap() for n, a in arrays.items()}
    out = nc.dram_tensor("out", (SEQ, D), F32, kind="ExternalOutput").ap()
    build(nc, out=out, **aps)
    result = run_bass_kernel_spmd(nc, [arrays], core_ids=[0])
    return result.results[0]["out"].reshape(1, SEQ, D)
```

```python
from contextlib import ExitStack

import concourse.bass as bass
from concourse import mybir

F32 = mybir.dt.float32
F32R = mybir.dt.float32r
ALU = mybir.AluOpType
ACT = mybir.ActivationFunctionType

P = 128
D = 1024
SEQ = 256
TILES = SEQ // P
DEPTH = 4
D_FF = 2816
EPS = 1e-6
KD = D // P
CHUNK = 256
CHUNKS = D_FF // CHUNK
FT = CHUNK // P
BLOCKS = D_FF // P
EARLY = 4
PIECE = 2048
RAW = 3
RING = 6
CONV_W = 3
CONV_STEPS = D // 256
GROUPS = ((128, 1), (512, 4), (2048, 16))
NG = len(GROUPS)
HD = 64
ROT = HD // 4
QUARTERS = 4
QH = 4
QP = 3 * NG
NH = 4
DQK = 128
DV = D // NH
NEG = -1e30
MASK_LOW = -3e38

REGION = 8900

FFN_PIECES = 3 * CHUNKS
OUT_PIECES = 4
CONV_PIECES = 3 * CONV_STEPS + OUT_PIECES
ATT_PIECES = QUARTERS * QP + OUT_PIECES
ML_PIECES = 12 + OUT_PIECES
LAYER_KINDS = ("conv", "att", "ml", "conv")
KINDS = [k for mixer in LAYER_KINDS for k in ("ffn", mixer, "ffn")]
COUNT = {"ffn": FFN_PIECES, "conv": CONV_PIECES, "att": ATT_PIECES, "ml": ML_PIECES}
BASE = [sum(COUNT[k] for k in KINDS[:n]) for n in range(len(KINDS) + 1)]
PIECES = BASE[-1]
SUBLAYERS = len(KINDS)

GU_BANK = 0
T_BANK = 2
Y_BANK = 4
CONV_BANKS = ((4, 5, 0), (1, 6, 7))


def early_piece(c):
    return 2 * c


def block_piece(i):
    return {4: 4, 5: 6}.get(i, i + i // 2 - 1) if i < BLOCKS - 2 else 3 * CHUNKS - 5 + i - (BLOCKS - 2)


def down_piece(c):
    return {0: 5, CHUNKS - 3: 3 * CHUNKS - 3, CHUNKS - 2: 3 * CHUNKS - 2, CHUNKS - 1: 3 * CHUNKS - 1}.get(c, 3 * c + 4)


def build(nc, x_in, gains, stream, gate_w, gate_b, conv_k, ident_in, rope_in, att_mask_in, ml_mask_in,
          tri_in, out):
    with ExitStack() as ctx:
        def sb(name, shape, dt=F32):
            return ctx.enter_context(nc.sbuf_tensor(name, shape, dt))

        def sem(name):
            return ctx.enter_context(nc.semaphore(name))

        ps = ctx.enter_context(nc.psum_tensor("ps", [P, 8, 512], F32))

        raw = sb("raw", [P, RAW, PIECE])
        w_high = sb("w_high", [P, RING, PIECE], F32R)
        w_low = sb("w_low", [P, RING, PIECE], F32R)
        x = sb("x", [P, TILES, D])
        xn = sb("xn", [P, TILES, D])
        gain = sb("gain", [P, 2, D])
        mean_y = sb("mean_y", [P, TILES])
        mean_x = sb("mean_x", [P, TILES])
        mean_eps = sb("mean_eps", [P, 2 * TILES])
        rstd_y = sb("rstd_y", [P, TILES])
        rstd_x = sb("rstd_x", [P, TILES])
        minus_half = sb("minus_half", [P, 1])
        xT_high = sb("xT_high", [P, KD, SEQ], F32R)
        xT_low = sb("xT_low", [P, KD, SEQ], F32R)
        ident = sb("ident", [P, P])

        region = sb("region", [P, REGION])
        used = [0]

        def from_region(shape, dt=F32):
            n = 1
            for s in shape:
                n *= s
            a = region[:, used[0]:used[0] + n]
            used[0] += n
            assert used[0] <= REGION, used[0]
            if dt is not F32:
                a = a.bitcast(dt)
            if len(shape) == 2:
                a = a.rearrange("p (a b) -> p a b", a=shape[0])
            if len(shape) == 3:
                a = a.rearrange("p (a b c) -> p a b c", a=shape[0], b=shape[1])
            return a

        conv_kT = sb("conv_kT", [P, 2, CONV_W, KD])
        rope = sb("rope", [P, TILES, 2, QH * ROT])
        att_mask = sb("att_mask", [P, NG, 2 * P])
        ml_mask = sb("ml_mask", [P, 2 * P])
        tri = sb("tri", [P, P])
        ones = sb("ones", [P, P])
        gw_raw = sb("gw_raw", [P, KD, 2 * NH])
        gw_high = sb("gw_high", [P, KD, 2 * NH], F32R)
        gw_low = sb("gw_low", [P, KD, 2 * NH], F32R)
        gate_bias = sb("gate_bias", [P, 2 * NH])
        oT_hi = sb("oT_hi", [P, KD, SEQ], F32R)
        oT_lo = sb("oT_lo", [P, KD, SEQ], F32R)
        silu = from_region([2, SEQ])
        h = from_region([2, SEQ])

        x_landed = [sem(f"x_landed{t}") for t in range(TILES)]
        ident_landed = sem("ident_landed")
        loaded = sem("loaded")
        raw_landed = [sem(f"raw_landed{n}") for n in range(RAW)]
        piece_high = sem("piece_high")
        piece_split = sem("piece_split")
        piece_used = sem("piece_used")
        y_ready = sem("y_ready")
        y_mean = sem("y_mean")
        y_rstd = sem("y_rstd")
        y_scaled = sem("y_scaled")
        x_updated = sem("x_updated")
        x_mean = sem("x_mean")
        x_rstd = sem("x_rstd")
        eps_added = sem("eps_added")
        xn_ready = sem("xn_ready")
        xT_in_psum = sem("xT_in_psum")
        xT_high_done = sem("xT_high_done")
        xT_split = sem("xT_split")
        gain_landed = sem("gain_landed")
        consts_set = sem("consts_set")
        gu_ready = sem("gu_ready")
        silu_done = sem("silu_done")
        h_ready = sem("h_ready")
        hT_in_psum = sem("hT_in_psum")
        hT_high_done = sem("hT_high_done")
        hT_split = sem("hT_split")
        oT_high_done = sem("oT_high_done")
        oT_split = sem("oT_split")
        c_copied = sem("c_copied")
        pads_zeroed = sem("pads_zeroed")
        cu_ready = sem("cu_ready")
        tap_done = sem("tap_done")
        conv_ready = sem("conv_ready")
        proj_ready = sem("proj_ready")
        proj_copied = sem("proj_copied")
        rope_products = sem("rope_products")
        rope_done = sem("rope_done")
        qkT_in_psum = sem("qkT_in_psum")
        qkT_done = sem("qkT_done")
        scores_ready = sem("scores_ready")
        masked = sem("masked")
        max_ready = sem("max_ready")
        exp_done = sem("exp_done")
        recip_done = sem("recip_done")
        probs_ready = sem("probs_ready")
        pT_in_psum = sem("pT_in_psum")
        pT_done = sem("pT_done")
        o_ready = sem("o_ready")
        gw_high_done = sem("gw_high_done")
        gw_split = sem("gw_split")
        gates_in_psum = sem("gates_in_psum")
        gate_step = sem("gate_step")
        gate_exp = sem("gate_exp")
        gate_ln = sem("gate_ln")
        lf_ready = sem("lf_ready")
        cum_in_psum = sem("cum_in_psum")
        diag_ready = sem("diag_ready")
        rows_in_psum = sem("rows_in_psum")
        ml_masked = sem("ml_masked")
        ml_max_ready = sem("ml_max_ready")
        ml_floor_sum = sem("ml_floor_sum")
        ml_floor = sem("ml_floor")
        decay_ready = sem("decay_ready")
        ml_copied = sem("ml_copied")
        ml_scores = sem("ml_scores")
        a_ready = sem("a_ready")
        den_step = sem("den_step")
        aT_in_psum = sem("aT_in_psum")
        aT_done = sem("aT_done")
        num_ready = sem("num_ready")
        mh_scaled = sem("mh_scaled")
        mhT_in_psum = sem("mhT_in_psum")
        stored = sem("stored")

        CONSTS = 16 * 7

        used[0] = 0
        c_sb = from_region([2, SEQ])
        cu = from_region([2, SEQ + 2])
        z = from_region([2, SEQ])
        used[0] = 0
        pT = from_region([NG, 3 * P])
        used[0] = 0
        qk = from_region([2, TILES * QH * HD]).rearrange("p a (t c) -> p a t c", t=TILES)
        rope_c, rope_s = ([from_region([QH, ROT]) for _ in range(TILES)] for _ in range(2))
        qT = from_region([NG, 2, SEQ])
        kT = from_region([NG, 2, SEQ])
        v = from_region([NG, TILES, QH * HD])
        probs = [from_region([NG, 3 * P]) for _ in range(2)]
        smax = from_region([2, 2])
        nmax = from_region([2, 2])
        den = from_region([2, 2])
        rden = from_region([2, 2])
        used[0] = 0
        mqT = from_region([NH, SEQ])
        mkT = from_region([NH, SEQ])
        mv = from_region([NH, TILES, DV])
        mog = region[:, 0:2 * NH * SEQ].rearrange("p (a b c) -> p a b c", a=NH, b=TILES)
        gates = from_region([TILES, 2 * NH])
        neg_f = from_region([TILES, NH])
        neg_abs = from_region([TILES, NH])
        exp_f = from_region([TILES, NH])
        ln_f = from_region([TILES, NH])
        lf = from_region([TILES, NH])
        cum = from_region([TILES, NH])
        r_col = from_region([TILES, NH])
        diag = from_region([2, TILES * P])
        decay = from_region([2, 3 * P])
        rmax = from_region([NH, TILES])
        neg_m = from_region([NH, TILES])
        floor_in = from_region([NH, TILES])
        floor_e = from_region([NH, TILES])
        a = from_region([2, 3 * P])
        aT = from_region([NH, 3 * P])
        mden = from_region([NH, TILES])
        neg_den = from_region([NH, TILES])
        abs_den = from_region([NH, TILES])
        safe_den = from_region([NH, TILES])
        mrden = from_region([NH, TILES])
        mh = from_region([2, TILES * DV]).rearrange("p a (t c) -> p a t c", t=TILES)

        def w_of(sub):
            return BASE[sub]

        def ffn_no(sub):
            return KINDS[:sub].count("ffn")

        def conv_no(sub):
            return KINDS[:sub].count("conv")

        OT = {"ffn": 0, "conv": CONV_STEPS, "att": 2 * QUARTERS, "ml": NH}

        def ot_before(sub):
            return sum(OT[k] for k in KINDS[:sub])

        def early(i):
            return i % 2, i // 2

        H_SPLITS = EARLY // 2 + BLOCKS - EARLY

        def splits_up_to(i):
            return EARLY // 2 + i - EARLY + 1

        def h_slot(i):
            return i % 4 if i < BLOCKS - 2 else 4 + i - (BLOCKS - 2)

        def after_ffn(joint):
            return joint > 0 and KINDS[joint - 1] == "ffn"

        def before_ffn(joint):
            return joint < SUBLAYERS and KINDS[joint] == "ffn"

        def xT_bank(joint, t, b):
            return (Y_BANK if t and before_ffn(joint) else T_BANK) + b

        def masked_row(n, t):
            base = xn[:, n // 2, :]
            return base[:, (n % 2) * 384:(n % 2) * 384 + P] if t == 0 else \
                base[:, (n % 2) * 384 + P:(n % 2) * 384 + 3 * P]

        block = ctx.enter_context(nc.Block())

        @block.sync
        def _(sp):
            for t in range(TILES):
                sp.dma_start(x[:, t, :], x_in[t * P:(t + 1) * P, :]).then_inc(x_landed[t], 16)
            for n in range(RAW):
                sp.dma_start(raw[:, n, :], stream[n]).then_inc(raw_landed[n], 16)
            sp.dma_start(conv_kT[:, :, :, :], conv_k).then_inc(loaded, 16)
            sp.dma_start(rope[:, :, :, :], rope_in).then_inc(loaded, 16)
            sp.dma_start(att_mask[:, :, :], att_mask_in).then_inc(loaded, 16)
            sp.dma_start(ml_mask[:, :], ml_mask_in).then_inc(loaded, 16)
            sp.dma_start(tri[:, :], tri_in).then_inc(loaded, 16)
            sp.dma_start(gw_raw[:, :, :], gate_w).then_inc(loaded, 16)
            sp.dma_start(gate_bias[:, :], gate_b.partition_broadcast(P)).then_inc(loaded, 16)
            with sp.Fori(1, PIECES // RAW) as turn:
                for n in range(RAW):
                    sp.wait_ge(piece_split, RAW * turn + n - RAW + 1)
                    sp.dma_start(raw[:, n, :], stream[RAW * turn + n]).then_inc(raw_landed[n], 16)
            for p in range(PIECES // RAW * RAW, PIECES):
                sp.wait_ge(piece_split, p - RAW + 1)
                sp.dma_start(raw[:, p % RAW, :], stream[p]).then_inc(raw_landed[p % RAW], 16)
            for t in range(TILES):
                sp.wait_ge(x_updated, TILES * (SUBLAYERS - 1) + t + 1)
                sp.dma_start(out[t * P:(t + 1) * P, :], x[:, t, :]).then_inc(stored, 16)
            sp.wait_ge(stored, 16 * TILES)

        @block.tensor
        def _(pe):
            def products(acc, lh, ll, rh, rl, start, stop):
                nc.tensor.matmul(acc, lh, rh, start=start, stop=False)
                nc.tensor.matmul(acc, lh, rl, start=False, stop=False)
                return nc.tensor.matmul(acc, ll, rh, start=False, stop=stop)

            def weights_ready(p):
                pe.wait_ge(piece_split, p + 1)

            def transpose_x(joint, t):
                pe.wait_ge(xn_ready, TILES * joint + t + 1)
                if joint == 0 and t == 0:
                    pe.wait_ge(ident_landed, 16)
                for b in range(2):
                    if t == 1:
                        pe.wait_ge(xT_split, 4 * joint + b + 1)
                    for k in range(4):
                        f = (4 * b + k) * P
                        last = nc.tensor.transpose(ps[:, xT_bank(joint, t, b), k * P:(k + 1) * P], xn[:, t, f:f + P], ident[:, :])
                    last.then_inc(xT_in_psum, 1)

            def x_ready(joint, t, half=1):
                pe.wait_ge(xT_split, 4 * joint + 2 * t + half + 1)

            def ffn(sub):
                h0, s0, w0 = BLOCKS * ffn_no(sub), H_SPLITS * ffn_no(sub), w_of(sub)

                def bank_free(i):
                    if i >= 2:
                        pe.wait_ge(h_ready, h0 + i - 1)

                def early_block(i, first_x=False, meanwhile=None):
                    c, t = early(i)
                    bank_free(i)
                    for half in range(2):
                        p = w0 + early_piece(c) + half
                        slot = p % RING
                        weights_ready(p)
                        if first_x:
                            x_ready(sub, t, half)
                        for k4 in range(4):
                            k = 4 * half + k4
                            tok = slice(t * P, (t + 1) * P)
                            cols = slice(k4 * 512, (k4 + 1) * 512)
                            last = products(ps[:, GU_BANK + i % 2, :], xT_high[:, k, tok], xT_low[:, k, tok],
                                            w_high[:, slot, cols], w_low[:, slot, cols], k == 0, k == KD - 1)
                            if meanwhile and k == meanwhile[0]:
                                meanwhile[1]()
                        if t == 1:
                            last.then_inc(piece_used, 1)
                    if t == 0:
                        last.then_inc(gu_ready, 1)

                def block(i, p, turn=0, before=0):
                    bank_free(i + before)
                    weights_ready(p + RING * turn)
                    for e in range(2):
                        for k in range(KD):
                            cols = slice(k * 256 + e * P, k * 256 + (e + 1) * P)
                            last = products(ps[:, GU_BANK + i % 2, e * SEQ:(e + 1) * SEQ], w_high[:, p % RING, cols],
                                            w_low[:, p % RING, cols], xT_high[:, k, :], xT_low[:, k, :],
                                            k == 0, k == KD - 1)
                    last.then_inc(piece_used, 1)

                def transpose_h(i):
                    c, t = early(i)
                    pe.wait_ge(h_ready, h0 + i + 1)
                    for j in range(FT):
                        last = nc.tensor.transpose(ps[:, T_BANK + c, j * SEQ + t * P:j * SEQ + (t + 1) * P],
                                                   h[:, i % 2, j * P:(j + 1) * P], ident[:, :])
                    if t == 1:
                        last.then_inc(hT_in_psum, 1)

                def down(c, p, t, turn=0):
                    weights_ready(p + RING * turn)
                    for half in range(2):
                        for j in range(FT):
                            cols = slice(j * D + half * 512, j * D + half * 512 + 512)
                            tok, at = slice(t * P, (t + 1) * P), h_slot(FT * c + j)
                            last = products(ps[:, Y_BANK + 2 * t + half, :], oT_hi[:, at, tok], oT_lo[:, at, tok],
                                            w_high[:, p % RING, cols], w_low[:, p % RING, cols],
                                            c == 0 and j == 0, c == CHUNKS - 1 and j == FT - 1)
                    if t == 1:
                        last.then_inc(piece_used, 1)
                    elif c == CHUNKS - 1:
                        last.then_inc(y_ready, 1)

                def down_both(c, turn=0):
                    if c < EARLY // 2:
                        pe.wait_ge(hT_split, s0 + c + 1)
                    else:
                        pe.wait_ge(hT_split, s0 + splits_up_to(FT * c + 1) + 4 * turn)
                    for t in range(TILES):
                        down(c, w0 + down_piece(c), t, turn)

                def unit(c, turn=0):
                    block(2 * c + 2, w0 + block_piece(2 * c + 2), turn, 4 * turn)
                    block(2 * c + 3, w0 + block_piece(2 * c + 3), turn, 4 * turn)
                    down_both(c, turn)

                transpose_x(sub, 0)
                early_block(0, first_x=True)
                early_block(1, meanwhile=(4, lambda: transpose_x(sub, 1)))
                transpose_h(0)
                early_block(2, first_x=True)
                transpose_h(1)
                early_block(3)
                transpose_h(2)
                block(4, w0 + block_piece(4))
                transpose_h(3)
                down_both(0)
                block(5, w0 + block_piece(5))
                down_both(1)
                with pe.Fori(0, (CHUNKS - 5) // 2) as turn:
                    unit(2, turn)
                    unit(3, turn)
                for i in range(BLOCKS - 4, BLOCKS):
                    block(i, w0 + block_piece(i))
                for t in range(TILES):
                    for c in range(CHUNKS - 3, CHUNKS):
                        if t == 0:
                            pe.wait_ge(hT_split, s0 + splits_up_to(FT * c + 1))
                        down(c, w0 + down_piece(c), t)

            def project_out(sub):
                p0 = w_of(sub + 1) - OUT_PIECES
                pe.wait_ge(oT_split, ot_before(sub + 1))
                for t in range(TILES):
                    tok = slice(t * P, (t + 1) * P)
                    for q in range(OUT_PIECES):
                        slot = (p0 + q) % RING
                        weights_ready(p0 + q)
                        for k4 in range(4):
                            k, cols = 4 * (q % 2) + k4, slice(k4 * 512, (k4 + 1) * 512)
                            last = products(ps[:, Y_BANK + 2 * t + q // 2, :], oT_hi[:, k, tok], oT_lo[:, k, tok],
                                            w_high[:, slot, cols], w_low[:, slot, cols], k == 0, k == KD - 1)
                        if t == 1:
                            last.then_inc(piece_used, 1)
                    if t == 0:
                        last.then_inc(y_ready, 1)

            def features_first(slot, bank):
                for j in range(2):
                    for k in range(KD):
                        cols = slice(k * 256 + j * P, k * 256 + (j + 1) * P)
                        last = products(ps[:, bank, j * SEQ:(j + 1) * SEQ], w_high[:, slot, cols],
                                        w_low[:, slot, cols], xT_high[:, k, :], xT_low[:, k, :],
                                        k == 0, k == KD - 1)
                return last

            def tokens_first(slot, acc, t):
                for k in range(KD):
                    tok, cols = slice(t * P, (t + 1) * P), slice(k * 256, (k + 1) * 256)
                    last = products(acc, xT_high[:, k, tok], xT_low[:, k, tok], w_high[:, slot, cols],
                                    w_low[:, slot, cols], k == 0, k == KD - 1)
                return last

            def conv(sub):
                w0 = w_of(sub)
                for t in range(TILES):
                    transpose_x(sub, t)
                    x_ready(sub, t)
                for s in range(CONV_STEPS):
                    for part in range(3):
                        p = w0 + 3 * s + part
                        weights_ready(p)
                        features_first(p % RING, CONV_BANKS[s % 2][part]).then_inc(piece_used, 1)
                project_out(sub)

            def attention(sub):
                w0 = w_of(sub)
                for t in range(TILES):
                    transpose_x(sub, t)
                    x_ready(sub, t)

                def project(quarter, qs, turn):
                    def transpose_qk(i, t):
                        n = 2 * (i // 3 * 2 + i % 3) + t
                        pe.wait_ge(rope_done, 4 * NG * quarter + n + 1)
                        if n >= 2:
                            pe.wait_ge(qkT_done, 4 * NG * quarter + n - 1)
                        for j in range(2):
                            last = nc.tensor.transpose(ps[:, 4 + t, j * P:(j + 1) * P], qk[:, i % 2, t, j * P:(j + 1) * P],
                                                       ident[:, :])
                        last.then_inc(qkT_in_psum, 1)

                    for i in range(QP):
                        p = w0 + QP * qs + i
                        weights_ready(p + 3 * RING * turn)
                        for t in range(TILES):
                            if i >= 2:
                                pe.wait_ge(proj_copied, 2 * QP * quarter + 2 * (i - 2) + t + 1)
                            last = tokens_first(p % RING, ps[:, (2 * i + t) % 4, 0:256], t)
                            last.then_inc(proj_ready if t == 0 else piece_used, 1)
                            if i % 3:
                                transpose_qk(i - 1, t)

                def attend(quarter, qs):
                    def scores(hh):
                        rows, j = slice(hh % 2 * HD, hh % 2 * HD + HD), hh // 2
                        if hh >= 1:
                            pe.wait_ge(masked, QH * quarter + hh)
                        for g in range(NG):
                            nc.tensor.matmul(ps[:, g // 2, g % 2 * 256:g % 2 * 256 + 256], qT[rows, g, j, P:2 * P],
                                             kT[rows, g, j, :], start=True, stop=True)
                            last = nc.tensor.matmul(ps[:, 2, g * P:(g + 1) * P], qT[rows, g, j, 0:P],
                                                    kT[rows, g, j, 0:P], start=True, stop=True)
                        last.then_inc(scores_ready, 1)

                    def transpose_probs(hh):
                        pe.wait_ge(probs_ready, QH * quarter + hh + 1)
                        for g in range(NG):
                            for n in range(3):
                                last = nc.tensor.transpose(ps[:, 3 + g, n * P:(n + 1) * P],
                                                           probs[hh % 2][:, g, n * P:(n + 1) * P], ident[:, :])
                        last.then_inc(pT_in_psum, 1)

                    def times_v(hh):
                        pe.wait_ge(pT_done, QH * quarter + hh + 1)
                        cols = slice(hh * HD, (hh + 1) * HD)
                        rows = slice(hh % 2 * HD, hh % 2 * HD + HD)
                        bank = 6 + hh // 2
                        if hh % 2 == 0:
                            pe.wait_ge(oT_split, ot_before(sub) + 2 * quarter)
                        for g in range(NG):
                            nc.tensor.matmul(ps[rows, bank, 0:SEQ], v[:, g, 0, cols], pT[:, g, 0:2 * P],
                                             start=g == 0, stop=False, skip_group_check=True)
                            last = nc.tensor.matmul(ps[rows, bank, P:SEQ], v[:, g, 1, cols], pT[:, g, 2 * P:3 * P],
                                                    start=False, stop=g == NG - 1, skip_group_check=True)
                        if hh % 2:
                            last.then_inc(o_ready, 1)

                    pe.wait_ge(proj_copied, 2 * QP * (quarter + 1))
                    pe.wait_ge(qkT_done, 4 * NG * (quarter + 1))
                    scores(0)
                    for hh in range(QH):
                        if hh + 1 < QH:
                            scores(hh + 1)
                        if hh:
                            times_v(hh - 1)
                        transpose_probs(hh)
                    times_v(QH - 1)

                with pe.Fori(0, QUARTERS // 2) as turn:
                    for qs in range(2):
                        project(2 * turn + qs, qs, turn)
                        attend(2 * turn + qs, qs)
                project_out(sub)

            def mlstm(sub):
                w0 = w_of(sub)
                for t in range(TILES):
                    transpose_x(sub, t)
                    x_ready(sub, t)
                pe.wait_ge(gw_split, 1)
                pe.wait_ge(loaded, CONSTS)
                for t in range(TILES):
                    tok = slice(t * P, (t + 1) * P)
                    for k in range(KD):
                        last = products(ps[:, 6, t * 2 * NH:(t + 1) * 2 * NH], xT_high[:, k, tok], xT_low[:, k, tok],
                                        gw_high[:, k, :], gw_low[:, k, :], k == 0, k == KD - 1)
                last.then_inc(gates_in_psum, 1)

                def feature_piece(i):
                    weights_ready(w0 + i)
                    features_first((w0 + i) % RING, i % 4).then_inc(piece_used, 1)

                def token_piece(i):
                    weights_ready(w0 + i)
                    pe.wait_ge(ml_copied, i - 4 + 1)
                    for t in range(TILES):
                        last = tokens_first((w0 + i) % RING, ps[:, i % 4, t * 256:(t + 1) * 256], t)
                    last.then_inc(piece_used, 1)

                def scores(n):
                    if n >= 2:
                        pe.wait_ge(a_ready, n - 1)
                    nc.tensor.matmul(ps[:, 6 + n % 2, 0:P], mqT[:, n, 0:P], mkT[:, n, 0:P], start=True, stop=True)
                    nc.tensor.matmul(ps[:, 6 + n % 2, P:3 * P], mqT[:, n, P:2 * P], mkT[:, n, :], start=True,
                                     stop=True).then_inc(ml_scores, 1)

                def transpose_a(n):
                    pe.wait_ge(a_ready, n + 1)
                    if n >= 2:
                        pe.wait_ge(aT_done, n - 1)
                    for j in range(3):
                        last = nc.tensor.transpose(ps[:, 4 + n % 2, j * P:(j + 1) * P], a[:, n % 2, j * P:(j + 1) * P],
                                                   ident[:, :])
                    last.then_inc(aT_in_psum, 1)

                def numerator(n):
                    pe.wait_ge(aT_done, n + 1)
                    if n >= 2:
                        pe.wait_ge(mh_scaled, 2 * (n - 1))
                    nc.tensor.matmul(ps[:, 6 + n % 2, 0:DV], aT[:, n, 0:P], mv[:, n, 0, :], start=True, stop=True)
                    for s in range(2):
                        last = nc.tensor.matmul(ps[:, 6 + n % 2, DV:2 * DV], aT[:, n, (s + 1) * P:(s + 2) * P],
                                                mv[:, n, s, :], start=s == 0, stop=s == 1)
                    last.then_inc(num_ready, 1)

                def transpose_out(n):
                    pe.wait_ge(mh_scaled, 2 * n + 2)
                    pe.wait_ge(aT_done, NH)
                    if n >= 2:
                        pe.wait_ge(oT_split, ot_before(sub) + n - 1)
                    for j in range(2):
                        for t in range(TILES):
                            last = nc.tensor.transpose(ps[:, 4 + n % 2, j * SEQ + t * P:j * SEQ + (t + 1) * P],
                                                       mh[:, n % 2, t, j * P:(j + 1) * P], ident[:, :])
                    last.then_inc(mhT_in_psum, 1)

                feature_piece(0)
                feature_piece(1)
                pe.wait_ge(lf_ready, 1)
                nc.tensor.matmul(ps[:, 7, 0:NH], tri[:, :], lf[:, 0, :], start=True, stop=True)
                nc.tensor.matmul(ps[:, 7, NH:2 * NH], ones[:, :], lf[:, 0, :], start=True, stop=False)
                nc.tensor.matmul(ps[:, 7, NH:2 * NH], tri[:, :], lf[:, 1, :], start=False,
                                 stop=True).then_inc(cum_in_psum, 1)
                feature_piece(2)
                feature_piece(3)
                for n in range(NH):
                    pe.wait_ge(diag_ready, n + 1)
                    nc.tensor.matmul(ps[:, 4 + n // 2, n % 2 * SEQ:n % 2 * SEQ + SEQ], ones[:, :], diag[:, n % 2, :],
                                     start=True, stop=True).then_inc(rows_in_psum, 1)
                for n in range(NH):
                    token_piece(4 + n)
                    if n == 0:
                        pe.wait_ge(ml_copied, 4)
                        pe.wait_ge(ml_max_ready, 1)
                    scores(n)
                    if n:
                        transpose_a(n - 1)
                for n in range(NH):
                    token_piece(8 + n)
                    if n == 0:
                        transpose_a(NH - 1)
                    numerator(n)
                    if n:
                        transpose_out(n - 1)
                transpose_out(NH - 1)
                project_out(sub)

            program = {"ffn": ffn, "conv": conv, "att": attention, "ml": mlstm}
            for sub, kind in enumerate(KINDS):
                program[kind](sub)

        @block.scalar
        def _(act):
            act.dma_start(ident[:, :], ident_in).then_inc(ident_landed, 16)
            act.dma_start(gain[:, 1, :], gains[0].partition_broadcast(P)).then_inc(gain_landed, 16)

            def high(p, turn=0):
                if p >= PIECES:
                    return
                act.wait_ge(raw_landed[p % RAW], 16 * (p // RAW + 1) + 32 * turn)
                if p >= RING:
                    act.wait_ge(piece_used, p - RING + 1 + RING * turn)
                nc.scalar.activation(w_high[:, p % RING, :], raw[:, p % RAW, :], ACT.Copy).then_inc(piece_high, 1)

            def square_y(joint, t):
                if t == 0:
                    act.wait_ge(y_ready, joint)
                else:
                    act.wait_ge(piece_used, BASE[joint])
                y = ps[:, Y_BANK + 2 * t:Y_BANK + 2 * t + 2, :].rearrange("p a b -> p (a b)")
                nc.scalar.activation(xn[:, t, :], y, ACT.Square, scale=1.0 / 32,
                                     accum_out=mean_y[:, t:t + 1]).then_inc(y_mean, 1)

            def square_x(joint, t):
                if joint:
                    act.wait_ge(x_updated, TILES * (joint - 1) + t + 1)
                else:
                    act.wait_ge(x_landed[t], 16)
                nc.scalar.activation(xn[:, t, :], x[:, t, :], ACT.Square, scale=1.0 / 32,
                                     accum_out=mean_x[:, t:t + 1]).then_inc(x_mean, 1)

            def xT(joint, t):
                for b in range(2):
                    act.wait_ge(xT_in_psum, 4 * joint + 2 * t + b + 1)
                    nc.scalar.activation(xT_high[:, 4 * b:4 * b + 4, t * P:(t + 1) * P],
                                         ps[:, xT_bank(joint, t, b), :].rearrange("p (k c) -> p k c", k=4),
                                         ACT.Copy).then_inc(xT_high_done, 1)

            def silu_of(sub, i, turn=0):
                if i < EARLY and early(i)[1] == 0:
                    act.wait_ge(gu_ready, 2 * ffn_no(sub) + early(i)[0] + 1)
                else:
                    p = early_piece(early(i)[0]) + 1 if i < EARLY else block_piece(i)
                    act.wait_ge(piece_used, w_of(sub) + p + 1 + RING * turn)
                nc.scalar.activation(silu[:, i % 2, :], ps[:, GU_BANK + i % 2, 0:SEQ], ACT.Silu).then_inc(silu_done, 1)

            def early_h_high(sub, c):
                act.wait_ge(hT_in_psum, 2 * ffn_no(sub) + c + 1)
                nc.scalar.activation(oT_hi[:, FT * c:FT * (c + 1), :].rearrange("p a b -> p (a b)"), ps[:, T_BANK + c, :],
                                     ACT.Copy).then_inc(hT_high_done, 1)

            def h_high(sub, i, turn=0):
                act.wait_ge(h_ready, BLOCKS * ffn_no(sub) + i + 1 + 4 * turn)
                if i == EARLY:
                    act.wait_ge(piece_used, w_of(sub) + down_piece(0) + 1)
                nc.scalar.activation(oT_hi[:, h_slot(i), :], h[:, i % 2, :], ACT.Copy).then_inc(hT_high_done, 1)

            def joint_part(joint):
                w0 = w_of(joint)
                if joint:
                    square_y(joint, 0)
                    if not after_ffn(joint):
                        high(w0 + 2)
                if joint == SUBLAYERS:
                    square_y(joint, 1)
                    return
                square_x(joint, 0)
                if joint == 0:
                    square_x(joint, 1)
                    high(0)
                    xT(joint, 0)
                    for p in range(1, 4):
                        high(p)
                else:
                    high(w0 + 3)
                    if after_ffn(joint):
                        square_y(joint, 1)
                        xT(joint, 0)
                    else:
                        xT(joint, 0)
                        square_y(joint, 1)
                    square_x(joint, 1)
                if before_ffn(joint):
                    silu_of(joint, 0)
                xT(joint, 1)
                act.dma_start(gain[:, 0, :], gains[2 * joint + 1].partition_broadcast(P)).then_inc(gain_landed, 16)
                if joint + 1 < SUBLAYERS:
                    act.dma_start(gain[:, 1, :], gains[2 * joint + 2].partition_broadcast(P)).then_inc(gain_landed, 16)

            def ffn(sub):
                w0 = w_of(sub)

                def unit(c, turn):
                    p = w0 + block_piece(2 * c + 2)
                    silu_of(sub, 2 * c + 2, turn=turn)
                    high(p + 5, turn)
                    h_high(sub, 2 * c + 2, turn)
                    silu_of(sub, 2 * c + 3, turn=turn)
                    high(p + 6, turn)
                    h_high(sub, 2 * c + 3, turn)
                    high(p + 7, turn)

                silu_of(sub, 1)
                high(w0 + 4)
                high(w0 + 5)
                silu_of(sub, 2)
                high(w0 + 6)
                high(w0 + 7)
                silu_of(sub, 3)
                early_h_high(sub, 0)
                high(w0 + 8)
                silu_of(sub, 4)
                early_h_high(sub, 1)
                high(w0 + 9)
                h_high(sub, 4)
                high(w0 + 10)
                silu_of(sub, 5)
                high(w0 + 11)
                h_high(sub, 5)
                high(w0 + 12)
                with act.Fori(0, (CHUNKS - 5) // 2) as turn:
                    unit(2, turn)
                    unit(3, turn)
                for i in range(BLOCKS - 4, BLOCKS):
                    silu_of(sub, i)
                    if i < BLOCKS - 1:
                        high(w0 + block_piece(i) + 5)
                    h_high(sub, i)
                high(w0 + FFN_PIECES + 1)
                high(w0 + FFN_PIECES + 2)

            def conv(sub):
                w0, n0 = w_of(sub), CONV_STEPS * conv_no(sub)
                for s in range(CONV_STEPS):
                    p = w0 + 3 * s
                    act.wait_ge(piece_used, p + 1)
                    nc.scalar.activation(c_sb.rearrange("p a b -> p (a b)"), ps[:, CONV_BANKS[s % 2][0], :],
                                         ACT.Copy).then_inc(c_copied, 1)
                    high(p + 5)
                    high(p + 6)
                    high(p + 7)
                    act.wait_ge(conv_ready, n0 + s + 1)
                    nc.scalar.activation(oT_hi[:, 2 * s:2 * s + 2, :], z, ACT.Copy).then_inc(oT_high_done, 1)

            def attention(sub):
                w0 = w_of(sub)

                def project(quarter, qs, turn):
                    def copy_out(i, t):
                        p = w0 + QP * qs + i
                        if t == 0:
                            act.wait_ge(proj_ready, QP * quarter + i + 1)
                        else:
                            act.wait_ge(piece_used, p + 1 + 3 * RING * turn)
                        to = v[:, i // 3, t, :] if i % 3 == 2 else qk[:, i % 2, t, :]
                        nc.scalar.activation(to, ps[:, (2 * i + t) % 4, 0:256], ACT.Copy).then_inc(proj_copied, 1)

                    def copy_qkT(i, t):
                        act.wait_ge(qkT_in_psum, 4 * NG * quarter + 2 * (i // 3 * 2 + i % 3) + t + 1)
                        to = (kT if i % 3 else qT)[:, i // 3, :, t * P:(t + 1) * P]
                        nc.scalar.activation(to, ps[:, 4 + t, 0:2 * P].rearrange("p (j c) -> p j c", j=2),
                                             ACT.Copy).then_inc(qkT_done, 1)

                    for i in range(QP):
                        for t in range(TILES):
                            copy_out(i, t)
                            if i % 3:
                                copy_qkT(i - 1, t)
                        high(w0 + QP * qs + i + 5, 3 * turn)

                def attend(quarter, qs):
                    def exp(hh):
                        pr = probs[hh % 2]
                        act.wait_ge(max_ready, QH * quarter + hh + 1)
                        for t, cols in ((1, slice(P, 3 * P)), (0, slice(0, P))):
                            last = nc.scalar.activation(pr[:, :, cols], pr[:, :, cols], ACT.Exp, scale=HD ** -0.5,
                                                        bias=nmax[:, hh % 2, t:t + 1], accum_out=den[:, hh % 2, t:t + 1])
                        last.then_inc(exp_done, 1)

                    exp(0)
                    for hh in range(QH):
                        act.wait_ge(pT_in_psum, QH * quarter + hh + 1)
                        nc.scalar.activation(pT, ps[:, 3:6, 0:3 * P], ACT.Copy).then_inc(pT_done, 1)
                        if hh + 1 < QH:
                            exp(hh + 1)
                        if hh % 2 == 0 and hh:
                            o_high(quarter, qs, hh // 2 - 1)
                    o_high(quarter, qs, QH // 2 - 1)

                def o_high(quarter, qs, j):
                    act.wait_ge(o_ready, 2 * quarter + j + 1)
                    nc.scalar.activation(oT_hi[:, bass.ds(2 * quarter + j, 1), :].rearrange("p a b -> p (a b)"),
                                         ps[:, 6 + j, 0:SEQ], ACT.Copy).then_inc(oT_high_done, 1)

                with act.Fori(0, QUARTERS // 2) as turn:
                    for qs in range(2):
                        project(2 * turn + qs, qs, turn)
                        attend(2 * turn + qs, qs)

            def mlstm(sub):
                w0 = w_of(sub)
                act.wait_ge(loaded, CONSTS)
                nc.scalar.activation(gw_high[:, :, :], gw_raw[:, :, :], ACT.Copy).then_inc(gw_high_done, 1)
                act.wait_ge(gate_step, 3)
                nc.scalar.activation(exp_f, neg_abs, ACT.Exp).then_inc(gate_exp, 1)
                act.wait_ge(gate_exp, 1)
                nc.scalar.activation(ln_f, exp_f, ACT.Ln, bias=1.0).then_inc(gate_ln, 1)

                def copy_out(i):
                    act.wait_ge(piece_used, w0 + i + 1)
                    if i < 4:
                        to = (mqT if i < 2 else mkT)[:, 2 * (i % 2):2 * (i % 2) + 2, :].rearrange("p a b -> p (a b)")
                        nc.scalar.activation(to, ps[:, i % 4, :], ACT.Copy, scale=1.0 if i < 2 else DQK ** -0.5)\
                          .then_inc(ml_copied, 1)
                    elif i < 8:
                        nc.scalar.activation(mv[:, i - 4, :, :].rearrange("p a b -> p (a b)"), ps[:, i % 4, :],
                                             ACT.Copy).then_inc(ml_copied, 1)
                    else:
                        nc.scalar.activation(mog[:, i - 8, :, :].rearrange("p a b -> p (a b)"), ps[:, i % 4, :],
                                             ACT.Sigmoid).then_inc(ml_copied, 1)

                def decay_of(n):
                    if n >= 2:
                        act.wait_ge(a_ready, n - 1)
                    act.wait_ge(ml_max_ready, 1)
                    if n == 0:
                        act.wait_ge(ml_floor_sum, 1)
                        nc.scalar.activation(floor_e, floor_in, ACT.Exp).then_inc(ml_floor, 1)
                    nc.scalar.activation(decay[:, n % 2, 0:P], masked_row(n, 0), ACT.Exp, bias=neg_m[:, n, 0:1])
                    nc.scalar.activation(decay[:, n % 2, P:3 * P], masked_row(n, 1), ACT.Exp,
                                         bias=neg_m[:, n, 1:2]).then_inc(decay_ready, 1)

                def copy_aT(n):
                    act.wait_ge(aT_in_psum, n + 1)
                    nc.scalar.activation(aT[:, n, :], ps[:, 4 + n % 2, 0:3 * P], ACT.Copy).then_inc(aT_done, 1)

                def o_high(n):
                    act.wait_ge(mhT_in_psum, n + 1)
                    nc.scalar.activation(oT_hi[:, 2 * n:2 * n + 2, :].rearrange("p a b -> p (a b)"), ps[:, 4 + n % 2, :],
                                         ACT.Copy).then_inc(oT_high_done, 1)

                for i in range(4):
                    copy_out(i)
                    high(w0 + i + 5)
                decay_of(0)
                for n in range(NH):
                    if n + 1 < NH:
                        decay_of(n + 1)
                    copy_out(4 + n)
                    high(w0 + 4 + n + 5)
                    if n:
                        copy_aT(n - 1)
                for n in range(NH):
                    copy_out(8 + n)
                    if n == 0:
                        copy_aT(NH - 1)
                    high(w0 + 8 + n + 5)
                    if n:
                        o_high(n - 1)
                o_high(NH - 1)

            program = {"ffn": ffn, "conv": conv, "att": attention, "ml": mlstm}
            for sub, kind in enumerate(KINDS):
                joint_part(sub)
                if kind != "ffn":
                    high(w_of(sub) + 4)
                program[kind](sub)
                if kind != "ffn":
                    high(w_of(sub + 1) + 1)
            joint_part(SUBLAYERS)

        @block.vector
        def _(dve):
            nc.vector.memset(minus_half[:, :], -0.5).then_inc(consts_set, 1)
            nc.vector.memset(ones[:, :], 1.0).then_inc(consts_set, 1)

            def low(p, turn=0):
                if p >= PIECES:
                    return
                dve.wait_ge(piece_high, p + 1 + RING * turn)
                nc.vector.tensor_tensor(w_low[:, p % RING, :], raw[:, p % RAW, :], w_high[:, p % RING, :],
                                        ALU.subtract).then_inc(piece_split, 1)

            def update_x(joint, t):
                n = TILES * (joint - 1) + t + 1
                dve.wait_ge(y_rstd, n)
                dve.wait_ge(gain_landed, 16 * min(1 + 2 * joint, 2 * SUBLAYERS))
                y = ps[:, Y_BANK + 2 * t:Y_BANK + 2 * t + 2, :].rearrange("p a b -> p (a b)")
                nc.vector.scalar_tensor_tensor(out=xn[:, t, :], in0=y, scalar=rstd_y[:, t:t + 1], in1=gain[:, 0, :],
                                               op0=ALU.mult, op1=ALU.mult).then_inc(y_scaled, 1)
                dve.wait_ge(y_scaled, n)
                scale = 0.5 if KINDS[joint - 1] == "ffn" else 1.0
                nc.vector.scalar_tensor_tensor(out=x[:, t, :], in0=xn[:, t, :], scalar=scale, in1=x[:, t, :],
                                               op0=ALU.mult, op1=ALU.add).then_inc(x_updated, 1)

            def pre_norm(joint, t):
                dve.wait_ge(x_rstd, TILES * joint + t + 1)
                if joint == 0:
                    dve.wait_ge(gain_landed, 16)
                nc.vector.scalar_tensor_tensor(out=xn[:, t, :], in0=x[:, t, :], scalar=rstd_x[:, t:t + 1],
                                               in1=gain[:, 1, :], op0=ALU.mult, op1=ALU.mult).then_inc(xn_ready, 1)

            def xT(joint, t):
                for b in range(2):
                    dve.wait_ge(xT_high_done, 4 * joint + 2 * t + b + 1)
                    cols = slice(t * P, (t + 1) * P)
                    nc.vector.tensor_tensor(xT_low[:, 4 * b:4 * b + 4, cols],
                                            ps[:, xT_bank(joint, t, b), :].rearrange("p (k c) -> p k c", k=4),
                                            xT_high[:, 4 * b:4 * b + 4, cols], ALU.subtract).then_inc(xT_split, 1)

            def times_up(sub, i, turn=0):
                dve.wait_ge(silu_done, BLOCKS * ffn_no(sub) + i + 1 + 4 * turn)
                if i >= EARLY + 2:
                    dve.wait_ge(hT_split, H_SPLITS * ffn_no(sub) + splits_up_to(i - 2) + 4 * turn)
                nc.vector.tensor_tensor(h[:, i % 2, :], silu[:, i % 2, :], ps[:, GU_BANK + i % 2, SEQ:2 * SEQ],
                                        ALU.mult).then_inc(h_ready, 1)

            def early_h_low(sub, c):
                dve.wait_ge(hT_high_done, H_SPLITS * ffn_no(sub) + c + 1)
                at = slice(FT * c, FT * (c + 1))
                nc.vector.tensor_tensor(oT_lo[:, at, :].rearrange("p a b -> p (a b)"), ps[:, T_BANK + c, :],
                                        oT_hi[:, at, :].rearrange("p a b -> p (a b)"), ALU.subtract).then_inc(hT_split, 1)

            def h_low(sub, i, turn=0):
                dve.wait_ge(hT_high_done, H_SPLITS * ffn_no(sub) + splits_up_to(i) + 4 * turn)
                nc.vector.tensor_tensor(oT_lo[:, h_slot(i), :], h[:, i % 2, :], oT_hi[:, h_slot(i), :],
                                        ALU.subtract).then_inc(hT_split, 1)

            def joint_part(joint):
                w0 = w_of(joint)
                if joint:
                    update_x(joint, 0)
                    if not after_ffn(joint):
                        low(w0 + 2)
                if joint < SUBLAYERS:
                    pre_norm(joint, 0)
                    if joint == 0:
                        low(0)
                    xT(joint, 0)
                if joint:
                    update_x(joint, 1)
                if joint == SUBLAYERS:
                    return
                if joint == 0:
                    low(1)
                    pre_norm(joint, 1)
                    low(2)
                    low(3)
                else:
                    low(w0 + 3)
                    pre_norm(joint, 1)
                if before_ffn(joint):
                    times_up(joint, 0)
                xT(joint, 1)

            def ffn(sub):
                w0 = w_of(sub)

                def unit(c, turn):
                    p = w0 + block_piece(2 * c + 2)
                    times_up(sub, 2 * c + 2, turn)
                    low(p + 5, turn)
                    h_low(sub, 2 * c + 2, turn)
                    times_up(sub, 2 * c + 3, turn)
                    low(p + 6, turn)
                    h_low(sub, 2 * c + 3, turn)
                    low(p + 7, turn)

                times_up(sub, 1)
                low(w0 + 4)
                low(w0 + 5)
                times_up(sub, 2)
                low(w0 + 6)
                low(w0 + 7)
                times_up(sub, 3)
                early_h_low(sub, 0)
                low(w0 + 8)
                times_up(sub, 4)
                early_h_low(sub, 1)
                low(w0 + 9)
                h_low(sub, 4)
                low(w0 + 10)
                times_up(sub, 5)
                low(w0 + 11)
                h_low(sub, 5)
                low(w0 + 12)
                with dve.Fori(0, (CHUNKS - 5) // 2) as turn:
                    unit(2, turn)
                    unit(3, turn)
                for i in range(BLOCKS - 4, BLOCKS):
                    times_up(sub, i)
                    if i < BLOCKS - 1:
                        low(w0 + block_piece(i) + 5)
                    h_low(sub, i)
                low(w0 + FFN_PIECES + 1)
                low(w0 + FFN_PIECES + 2)

            def conv(sub):
                w0, layer = w_of(sub), conv_no(sub)
                n0, o0 = CONV_STEPS * layer, ot_before(sub)
                dve.wait_ge(loaded, CONSTS)
                nc.vector.memset(cu[:, :, 0:2], 0.0).then_inc(pads_zeroed, 1)
                dve.wait_ge(pads_zeroed, layer + 1)
                for s in range(CONV_STEPS):
                    p, n, banks = w0 + 3 * s, n0 + s, CONV_BANKS[s % 2]
                    low(p + 5)
                    dve.wait_ge(c_copied, n + 1)
                    dve.wait_ge(piece_used, p + 2)
                    nc.vector.tensor_tensor(cu[:, :, 2:SEQ + 2], c_sb,
                                            ps[:, banks[1], :].rearrange("p (j c) -> p j c", j=2),
                                            ALU.mult).then_inc(cu_ready, 1)
                    dve.wait_ge(cu_ready, n + 1)
                    taps = 2 * CONV_W * n
                    for j in range(CONV_W):
                        for e in range(2):
                            k = conv_kT[:, layer, j, 2 * s + e:2 * s + e + 1]
                            shifted = cu[:, e, CONV_W - 1 - j:CONV_W - 1 - j + SEQ]
                            if j == 0:
                                tap = nc.vector.tensor_scalar(z[:, e, :], shifted, k, None, ALU.mult)
                            else:
                                dve.wait_ge(tap_done, taps + 2 * (j - 1) + e + 1)
                                tap = nc.vector.scalar_tensor_tensor(out=z[:, e, :], in0=shifted, scalar=k,
                                                                     in1=z[:, e, :], op0=ALU.mult, op1=ALU.add)
                            tap.then_inc(tap_done, 1)
                    low(p + 6)
                    dve.wait_ge(piece_used, p + 3)
                    dve.wait_ge(tap_done, taps + 2 * CONV_W)
                    nc.vector.tensor_tensor(z, z, ps[:, banks[2], :].rearrange("p (j c) -> p j c", j=2),
                                            ALU.mult).then_inc(conv_ready, 1)
                    if s + 1 < CONV_STEPS:
                        low(p + 7)
                    dve.wait_ge(oT_high_done, o0 + s + 1)
                    nc.vector.tensor_tensor(oT_lo[:, 2 * s:2 * s + 2, :], z, oT_hi[:, 2 * s:2 * s + 2, :],
                                            ALU.subtract).then_inc(oT_split, 1)
                low(p + 7)

            def attention(sub):
                w0, o0 = w_of(sub), ot_before(sub)
                dve.wait_ge(loaded, CONSTS)

                def rotate(quarter, i, t):
                    n = 2 * (i // 3 * 2 + i % 3) + t
                    dve.wait_ge(proj_copied, 2 * QP * quarter + 2 * i + t + 1)
                    q = qk[:, i % 2, t, :].rearrange("p (h c) -> p h c", h=QH)
                    cos, sin = (rope[:, t, e, :].rearrange("p (h c) -> p h c", h=QH) for e in range(2))
                    by_cos, by_sin = rope_c[t], rope_s[t]
                    if n >= 2:
                        dve.wait_ge(rope_done, 4 * NG * quarter + n - 1)
                    nc.vector.tensor_tensor(by_cos, q[:, :, 0:ROT], cos, ALU.mult)
                    nc.vector.tensor_tensor(by_sin, q[:, :, 0:ROT], sin, ALU.mult).then_inc(rope_products, 1)
                    dve.wait_ge(rope_products, 4 * NG * quarter + n + 1)
                    half = ROT // 2
                    nc.vector.tensor_tensor(q[:, :, 0:half], by_cos[:, :, 0:half], by_sin[:, :, half:ROT], ALU.subtract)
                    nc.vector.tensor_tensor(q[:, :, half:ROT], by_cos[:, :, half:ROT], by_sin[:, :, 0:half],
                                            ALU.add).then_inc(rope_done, 1)

                def attend(quarter, qs):
                    for hh in range(QH):
                        n, pr = QH * quarter + hh, probs[hh % 2]
                        dve.wait_ge(scores_ready, n + 1)
                        nc.vector.memset(den[:, hh % 2, :], 0.0)
                        s1 = ps[:, 0:2, :].rearrange("p a b -> p (a b)")[:, 0:NG * 2 * P].rearrange("p (g c) -> p g c", g=NG)
                        nc.vector.tensor_tensor_reduce(pr[:, :, P:3 * P], s1, att_mask[:, :, :], 1.0, MASK_LOW, ALU.add,
                                                       ALU.max, smax[:, hh % 2, 1:2])
                        s0 = ps[:, 2, 0:NG * P].rearrange("p (g c) -> p g c", g=NG)
                        nc.vector.tensor_tensor_reduce(pr[:, :, 0:P], s0, att_mask[:, :, P:2 * P], 1.0, MASK_LOW,
                                                       ALU.add, ALU.max, smax[:, hh % 2, 0:1]).then_inc(masked, 1)
                        dve.wait_ge(masked, n + 1)
                        nc.vector.tensor_scalar(nmax[:, hh % 2, :], smax[:, hh % 2, :], -HD ** -0.5, None,
                                                ALU.mult).then_inc(max_ready, 1)
                        dve.wait_ge(exp_done, n + 1)
                        nc.vector.reciprocal(rden[:, hh % 2, :], den[:, hh % 2, :]).then_inc(recip_done, 1)
                        dve.wait_ge(recip_done, n + 1)
                        nc.vector.tensor_scalar(pr[:, :, 0:P], pr[:, :, 0:P], rden[:, hh % 2, 0:1], None, ALU.mult)
                        nc.vector.tensor_scalar(pr[:, :, P:3 * P], pr[:, :, P:3 * P], rden[:, hh % 2, 1:2], None,
                                                ALU.mult).then_inc(probs_ready, 1)
                    for j in range(QH // 2):
                        o_low(quarter, j)

                def o_low(quarter, j):
                    dve.wait_ge(oT_high_done, o0 + 2 * quarter + j + 1)
                    at = bass.ds(2 * quarter + j, 1)
                    nc.vector.tensor_tensor(oT_lo[:, at, :].rearrange("p a b -> p (a b)"), ps[:, 6 + j, 0:SEQ],
                                            oT_hi[:, at, :].rearrange("p a b -> p (a b)"),
                                            ALU.subtract).then_inc(oT_split, 1)

                with dve.Fori(0, QUARTERS // 2) as turn:
                    for qs in range(2):
                        quarter = 2 * turn + qs
                        for i in range(QP):
                            if i % 3 < 2:
                                for t in range(TILES):
                                    rotate(quarter, i, t)
                            low(w0 + QP * qs + i + 5, 3 * turn)
                        attend(quarter, qs)

            def mlstm(sub):
                w0, o0 = w_of(sub), ot_before(sub)
                dve.wait_ge(loaded, CONSTS)
                dve.wait_ge(gw_high_done, 1)
                nc.vector.tensor_tensor(gw_low[:, :, :], gw_raw[:, :, :], gw_high[:, :, :], ALU.subtract).then_inc(gw_split, 1)
                dve.wait_ge(gates_in_psum, 1)
                for t in range(TILES):
                    step = nc.vector.tensor_tensor(gates[:, t, :], ps[:, 6, t * 2 * NH:(t + 1) * 2 * NH],
                                                   gate_bias[:, :], ALU.add)
                step.then_inc(gate_step, 1)
                forget = gates[:, :, NH:2 * NH]
                dve.wait_ge(gate_step, 1)
                nc.vector.tensor_scalar(neg_f, forget, -1.0, None, ALU.mult).then_inc(gate_step, 1)
                dve.wait_ge(gate_step, 2)
                nc.vector.tensor_tensor(neg_abs, forget, neg_f, ALU.min).then_inc(gate_step, 1)
                dve.wait_ge(gate_ln, 1)
                nc.vector.scalar_tensor_tensor(out=lf, in0=forget, scalar=0.0, in1=ln_f, op0=ALU.min,
                                               op1=ALU.subtract).then_inc(lf_ready, 1)
                low(w0 + 5)
                low(w0 + 6)
                dve.wait_ge(cum_in_psum, 1)
                nc.vector.tensor_copy(cum, ps[:, 7, 0:2 * NH].rearrange("p (t n) -> p t n", t=TILES)).then_inc(gate_step, 1)
                dve.wait_ge(gate_step, 4)
                nc.vector.tensor_tensor(r_col, gates[:, :, 0:NH], cum, ALU.subtract).then_inc(gate_step, 1)
                dve.wait_ge(gate_step, 5)
                for n in range(NH):
                    if n >= 2:
                        dve.wait_ge(rows_in_psum, n - 1)
                    for t in range(TILES):
                        last = nc.vector.tensor_scalar(diag[:, n % 2, t * P:(t + 1) * P], ident[:, :],
                                                       r_col[:, t, n:n + 1], None, ALU.mult)
                    last.then_inc(diag_ready, 1)
                low(w0 + 7)
                low(w0 + 8)
                for n in range(NH):
                    dve.wait_ge(rows_in_psum, n + 1 if n % 2 else n + 2)
                    rows = ps[:, 4 + n // 2, n % 2 * SEQ:n % 2 * SEQ + SEQ]
                    nc.vector.tensor_tensor_reduce(masked_row(n, 0), rows[:, 0:P], ml_mask[:, P:2 * P], 1.0, MASK_LOW,
                                                   ALU.add, ALU.max, rmax[:, n, 0:1])
                    last = nc.vector.tensor_tensor_reduce(masked_row(n, 1), rows, ml_mask[:, :], 1.0, MASK_LOW,
                                                          ALU.add, ALU.max, rmax[:, n, 1:2])
                last.then_inc(ml_masked, 1)
                dve.wait_ge(ml_masked, 1)
                nc.vector.tensor_scalar(neg_m, rmax, 0.0, -1.0, ALU.max, ALU.mult).then_inc(ml_max_ready, 1)
                dve.wait_ge(ml_max_ready, 1)
                nc.vector.tensor_tensor(floor_in, neg_m, cum.rearrange("p t n -> p n t"), ALU.subtract)\
                    .then_inc(ml_floor_sum, 1)

                def a_of(n):
                    dve.wait_ge(ml_scores, n + 1)
                    dve.wait_ge(decay_ready, n + 1)
                    if n >= 2:
                        dve.wait_ge(aT_in_psum, n - 1)
                    for t, cols in ((0, slice(0, P)), (1, slice(P, 3 * P))):
                        last = nc.vector.tensor_tensor_reduce(a[:, n % 2, cols], ps[:, 6 + n % 2, cols],
                                                              decay[:, n % 2, cols], 1.0, 0.0, ALU.mult, ALU.add,
                                                              mden[:, n, t:t + 1])
                    last.then_inc(a_ready, 1)
                    dve.wait_ge(a_ready, n + 1)
                    nc.vector.tensor_scalar(neg_den[:, n, :], mden[:, n, :], -1.0, None, ALU.mult).then_inc(den_step, 1)
                    dve.wait_ge(den_step, 4 * n + 1)
                    nc.vector.tensor_tensor(abs_den[:, n, :], mden[:, n, :], neg_den[:, n, :], ALU.max).then_inc(den_step, 1)
                    dve.wait_ge(den_step, 4 * n + 2)
                    dve.wait_ge(ml_floor, 1)
                    nc.vector.tensor_tensor(safe_den[:, n, :], abs_den[:, n, :], floor_e[:, n, :], ALU.max)\
                        .then_inc(den_step, 1)
                    dve.wait_ge(den_step, 4 * n + 3)
                    nc.vector.reciprocal(mrden[:, n, :], safe_den[:, n, :]).then_inc(den_step, 1)

                def gated_h(n):
                    dve.wait_ge(num_ready, n + 1)
                    dve.wait_ge(ml_copied, 8 + n + 1)
                    dve.wait_ge(den_step, 4 * n + 4)
                    if n >= 2:
                        dve.wait_ge(mhT_in_psum, n - 1)
                    for t in range(TILES):
                        nc.vector.scalar_tensor_tensor(out=mh[:, n % 2, t, :], in0=ps[:, 6 + n % 2, t * DV:(t + 1) * DV],
                                                       scalar=mrden[:, n, t:t + 1], in1=mog[:, n, t, :], op0=ALU.mult,
                                                       op1=ALU.mult).then_inc(mh_scaled, 1)

                def o_low(n):
                    dve.wait_ge(oT_high_done, o0 + n + 1)
                    nc.vector.tensor_tensor(oT_lo[:, 2 * n:2 * n + 2, :].rearrange("p a b -> p (a b)"),
                                            ps[:, 4 + n % 2, :], oT_hi[:, 2 * n:2 * n + 2, :].rearrange("p a b -> p (a b)"),
                                            ALU.subtract).then_inc(oT_split, 1)

                for n in range(NH):
                    a_of(n)
                    low(w0 + 9 + n)
                for n in range(NH):
                    gated_h(n)
                    low(w0 + 13 + n)
                    if n:
                        o_low(n - 1)
                o_low(NH - 1)

            program = {"ffn": ffn, "conv": conv, "att": attention, "ml": mlstm}
            for sub, kind in enumerate(KINDS):
                joint_part(sub)
                if kind != "ffn":
                    low(w_of(sub) + 4)
                program[kind](sub)
                if kind != "ffn":
                    low(w_of(sub + 1) + 1)
            joint_part(SUBLAYERS)

        @block.gpsimd
        def _(pool):
            pool.wait_ge(consts_set, 1)
            steps = [0]

            def rstd(to, mean, n, arrived, value, done):
                pool.wait_ge(arrived, value)
                nc.gpsimd.tensor_scalar(mean_eps[:, n:n + 1], mean, EPS, None, ALU.add).then_inc(eps_added, 1)
                steps[0] += 1
                pool.wait_ge(eps_added, steps[0])
                nc.gpsimd.tensor_tensor(to, mean_eps[:, n:n + 1], minus_half[:, :], ALU.pow).then_inc(done, 1)

            def of_y(joint, t):
                rstd(rstd_y[:, t:t + 1], mean_y[:, t:t + 1], t, y_mean, TILES * (joint - 1) + t + 1, y_rstd)

            def of_x(joint, t):
                rstd(rstd_x[:, t:t + 1], mean_x[:, t:t + 1], TILES + t, x_mean, TILES * joint + t + 1, x_rstd)

            for joint in range(SUBLAYERS + 1):
                for t in range(TILES):
                    if joint:
                        of_y(joint, t)
                    if joint < SUBLAYERS:
                        of_x(joint, t)


def lay_out(inputs):
    import numpy as np

    w = {k: np.asarray(v) for k, v in inputs.items()}
    stream = np.empty((PIECES, P, PIECE), np.float32)

    def columns(m, c, n):
        return m[:, c:c + n].reshape(KD, P, n).transpose(1, 0, 2)

    def put_out(p, m):
        for q in range(OUT_PIECES):
            stream[p + q] = columns(m, 512 * (q // 2), 512)[:, 4 * (q % 2):4 * (q % 2) + 4].reshape(P, PIECE)

    done = {"ffn": 0, "conv": 0, "att": 0, "ml": 0}
    for sub, kind in enumerate(KINDS):
        p, n = BASE[sub], done[kind]
        done[kind] += 1
        if kind == "ffn":
            name = "ffn1" if sub % 3 == 0 else "ffn2"
            wg, wu, wd = (w[f"{name}_{s}"][sub // 3] for s in ("wg", "wu", "wd"))
            for c in range(EARLY // 2):
                both = np.stack([columns(wg, c * CHUNK, CHUNK), columns(wu, c * CHUNK, CHUNK)], axis=2)
                for half in range(2):
                    stream[p + early_piece(c) + half] = both[:, 4 * half:4 * half + 4].reshape(P, PIECE)
            for i in range(EARLY, BLOCKS):
                both = np.stack([columns(wg, i * P, P), columns(wu, i * P, P)], axis=2)
                stream[p + block_piece(i)] = both.reshape(P, PIECE)
            for c in range(CHUNKS):
                stream[p + down_piece(c)] = wd[c * CHUNK:(c + 1) * CHUNK].reshape(FT, P, D).transpose(1, 0, 2).reshape(P, PIECE)
        elif kind == "conv":
            for s in range(CONV_STEPS):
                for part, third in enumerate((1, 2, 0)):
                    stream[p + 3 * s + part] = columns(w["conv_w_in"][n], third * D + 256 * s, 256).reshape(P, PIECE)
            put_out(p + 3 * CONV_STEPS, w["conv_w_out"][n])
        elif kind == "att":
            for quarter in range(QUARTERS):
                for i in range(QP):
                    stream[p + QP * quarter + i] = columns(w["attn_w_in"][n], i * D + 256 * quarter, 256).reshape(P, PIECE)
            put_out(p + QP * QUARTERS, w["attn_w_out"][n])
        else:
            for i in range(12):
                stream[p + i] = columns(w["mlstm_w_in"][n], 256 * i, 256).reshape(P, PIECE)
            put_out(p + 12, w["mlstm_w_out"][n])

    gate_w = np.ascontiguousarray(columns(w["mlstm_w_in"][0], 12 * 256, 2 * NH))
    gate_b = np.concatenate([w["mlstm_b_i"][0], w["mlstm_b_f"][0]])
    conv_k = np.ascontiguousarray(w["conv_k"].reshape(2, CONV_W, KD, P).transpose(3, 0, 1, 2))

    inv = np.float32(500000.0) ** (-np.arange(0, ROT, 2, dtype=np.float32) / np.float32(ROT))
    ang = np.arange(SEQ, dtype=np.float32)[:, None] * inv[None, :].astype(np.float32)
    tables = np.stack([np.tile(np.cos(ang), (1, 2 * QH)), np.tile(np.sin(ang), (1, 2 * QH))], axis=1).astype(np.float32)
    rope = np.ascontiguousarray(tables.reshape(TILES, P, 2, QH * ROT).transpose(1, 0, 2, 3))
    q, k = np.arange(P)[:, None], np.arange(P)[None, :]
    att_mask = np.full((P, NG, 2 * P), NEG, np.float32)
    for g, (win, dil) in enumerate(GROUPS):
        for b, rel in enumerate((q + P - k, q - k)):
            att_mask[:, g, b * P:(b + 1) * P][(rel >= 0) & (rel % dil == 0) & (rel // dil <= win // dil)] = 0.0
    ml_mask = np.zeros((P, 2 * P), np.float32)
    ml_mask[:, P:][k > q] = NEG
    tri = np.triu(np.ones((P, P), np.float32))
    return {
        "x_in": w["x"].reshape(SEQ, D), "gains": w["norm_g"].reshape(-1, D), "stream": stream, "gate_w": gate_w,
        "gate_b": gate_b, "conv_k": conv_k, "ident_in": np.eye(P, dtype=np.float32), "rope_in": rope,
        "att_mask_in": att_mask, "ml_mask_in": ml_mask, "tri_in": tri,
    }


def kernel(**inputs):
    import concourse.bacc as bacc
    from concourse.bass_utils import run_bass_kernel_spmd

    nc = bacc.Bacc("TRN2", target_bir_lowering=False, num_devices=1, dynamic_dma_scratch_size=1024)
    arrays = lay_out(inputs)
    aps = {n: nc.dram_tensor(n, a.shape, F32, kind="ExternalInput").ap() for n, a in arrays.items()}
    out = nc.dram_tensor("out", (SEQ, D), F32, kind="ExternalOutput").ap()
    build(nc, out=out, **aps)
    result = run_bass_kernel_spmd(nc, [arrays], core_ids=[0])
    return result.results[0]["out"].reshape(1, SEQ, D)
```

```python
from contextlib import ExitStack

import concourse.bass as bass
from concourse import mybir

F32 = mybir.dt.float32
F32R = mybir.dt.float32r
ALU = mybir.AluOpType
ACT = mybir.ActivationFunctionType

P = 128
D = 1024
SEQ = 256
TILES = SEQ // P
DEPTH = 4
D_FF = 2816
EPS = 1e-6
KD = D // P
CHUNK = 256
CHUNKS = D_FF // CHUNK
FT = CHUNK // P
BLOCKS = D_FF // P
EARLY = 4
PIECE = 2048
RAW = 3
RING = 6
CONV_W = 3
CONV_STEPS = D // 256
GROUPS = ((128, 1), (512, 4), (2048, 16))
NG = len(GROUPS)
HD = 64
ROT = HD // 4
QUARTERS = 4
QH = 4
QP = 3 * NG
NH = 4
DQK = 128
DV = D // NH
NEG = -1e30
MASK_LOW = -3e38

REGION = 9900

FFN_PIECES = 3 * CHUNKS
OUT_PIECES = 4
CONV_PIECES = 3 * CONV_STEPS + OUT_PIECES
ATT_PIECES = QUARTERS * QP + OUT_PIECES
ML_PIECES = 12 + OUT_PIECES
LAYER_KINDS = ("conv", "att", "ml", "conv")
KINDS = [k for mixer in LAYER_KINDS for k in ("ffn", mixer, "ffn")]
COUNT = {"ffn": FFN_PIECES, "conv": CONV_PIECES, "att": ATT_PIECES, "ml": ML_PIECES}
BASE = [sum(COUNT[k] for k in KINDS[:n]) for n in range(len(KINDS) + 1)]
PIECES = BASE[-1]
SUBLAYERS = len(KINDS)

QK = 2 * NG

ML_ORDER = (8, 9, 10, 0, 1, 2, 3, 4, 5, 6, 7, 11)

Y_SCALE = {"ffn": 0.5, "conv": 1.0, "att": 1.0, "ml": 1.0}

GU_BANK = 0
T_BANK = 2
Y_BANK = 4
O_BANK = (1, 0)
FIRST_BANKS = ((4, 5, 0), (1, 6, 7))


def early_piece(c):
    return 2 * c


def block_piece(i):
    return {4: 4, 5: 6}.get(i, i + i // 2 - 1) if i < BLOCKS - 2 else 3 * CHUNKS - 5 + i - (BLOCKS - 2)


def down_piece(c):
    return {0: 5, CHUNKS - 3: 3 * CHUNKS - 3, CHUNKS - 2: 3 * CHUNKS - 2, CHUNKS - 1: 3 * CHUNKS - 1}.get(c, 3 * c + 4)


def build(nc, x_in, gains, stream, gate_w, gate_b, conv_k, ident_in, rope_in, att_mask_in, ml_mask_in,
          tri_in, out):
    with ExitStack() as ctx:
        def sb(name, shape, dt=F32):
            return ctx.enter_context(nc.sbuf_tensor(name, shape, dt))

        def sem(name):
            return ctx.enter_context(nc.semaphore(name))

        ps = ctx.enter_context(nc.psum_tensor("ps", [P, 8, 512], F32))

        raw = sb("raw", [P, RAW, PIECE])
        w_high = sb("w_high", [P, RING, PIECE], F32R)
        w_low = sb("w_low", [P, RING, PIECE], F32R)
        x = sb("x", [P, TILES, D])
        xn = sb("xn", [P, TILES, D])
        gain = sb("gain", [P, 2, D])
        mean_y = sb("mean_y", [P, TILES, 2])
        mean_x = sb("mean_x", [P, TILES])
        mean_eps = sb("mean_eps", [P, 2 * TILES])
        rstd_y = sb("rstd_y", [P, TILES])
        rstd_x = sb("rstd_x", [P, TILES])
        minus_half = sb("minus_half", [P, 1])
        xT_high = sb("xT_high", [P, KD, SEQ], F32R)
        xT_low = sb("xT_low", [P, KD, SEQ], F32R)
        ident = sb("ident", [P, P])

        region = sb("region", [P, REGION])
        used = [0]

        def from_region(shape, dt=F32):
            n = 1
            for s in shape:
                n *= s
            a = region[:, used[0]:used[0] + n]
            used[0] += n
            assert used[0] <= REGION, used[0]
            if dt is not F32:
                a = a.bitcast(dt)
            if len(shape) == 2:
                a = a.rearrange("p (a b) -> p a b", a=shape[0])
            if len(shape) == 3:
                a = a.rearrange("p (a b c) -> p a b c", a=shape[0], b=shape[1])
            return a

        conv_kT = sb("conv_kT", [P, 2, CONV_W, KD])
        rope = sb("rope", [P, TILES, 2, QH * ROT])
        att_mask = sb("att_mask", [P, NG, 2 * P])
        ml_mask = sb("ml_mask", [P, 2 * P])
        tri = sb("tri", [P, P])
        ones = sb("ones", [P, P])
        gw_raw = sb("gw_raw", [P, KD, 2 * NH])
        gw_high = sb("gw_high", [P, KD, 2 * NH], F32R)
        gw_low = sb("gw_low", [P, KD, 2 * NH], F32R)
        gate_bias = sb("gate_bias", [P, 2 * NH])
        oT_hi = sb("oT_hi", [P, KD, SEQ], F32R)
        oT_lo = sb("oT_lo", [P, KD, SEQ], F32R)
        silu = from_region([2, SEQ])
        h = from_region([2, SEQ])

        x_landed = [sem(f"x_landed{t}") for t in range(TILES)]
        ident_landed = sem("ident_landed")
        loaded = sem("loaded")
        raw_landed = [sem(f"raw_landed{n}") for n in range(RAW)]
        piece_high = sem("piece_high")
        piece_split = sem("piece_split")
        piece_used = sem("piece_used")
        y_ready = sem("y_ready")
        y_mean = sem("y_mean")
        y_rstd = sem("y_rstd")
        y_gained = sem("y_gained")
        x_updated = sem("x_updated")
        x_mean = sem("x_mean")
        x_rstd = sem("x_rstd")
        eps_added = sem("eps_added")
        xn_ready = sem("xn_ready")
        xT_in_psum = sem("xT_in_psum")
        xT_high_done = sem("xT_high_done")
        xT_split = sem("xT_split")
        gain_landed = sem("gain_landed")
        consts_set = sem("consts_set")
        gu_ready = sem("gu_ready")
        silu_done = sem("silu_done")
        h_ready = sem("h_ready")
        hT_in_psum = sem("hT_in_psum")
        hT_high_done = sem("hT_high_done")
        hT_split = sem("hT_split")
        oT_high_done = sem("oT_high_done")
        oT_split = sem("oT_split")
        c_copied = sem("c_copied")
        pads_zeroed = sem("pads_zeroed")
        cu_ready = sem("cu_ready")
        conv_tile0 = sem("conv_tile0")
        token_copied = sem("token_copied")
        token_cu_ready = sem("token_cu_ready")
        step0_in_psum = sem("step0_in_psum")
        tap_done = sem("tap_done")
        conv_ready = sem("conv_ready")
        proj_ready = sem("proj_ready")
        proj_copied = sem("proj_copied")
        rope_products = sem("rope_products")
        rope_done = sem("rope_done")
        qkT_in_psum = sem("qkT_in_psum")
        qkT_done = sem("qkT_done")
        scores_ready = sem("scores_ready")
        masked = sem("masked")
        max_ready = sem("max_ready")
        exp_done = sem("exp_done")
        recip_done = sem("recip_done")
        probs_ready = sem("probs_ready")
        pT_in_psum = sem("pT_in_psum")
        pT_done = sem("pT_done")
        o_ready = sem("o_ready")
        gw_high_done = sem("gw_high_done")
        gw_split = sem("gw_split")
        ml_tile0 = sem("ml_tile0")
        gates_in_psum = sem("gates_in_psum")
        gT_copied = sem("gT_copied")
        gates_turned = sem("gates_turned")
        gate_step = sem("gate_step")
        gate_exp = sem("gate_exp")
        gate_ln = sem("gate_ln")
        lf_ready = sem("lf_ready")
        cum_in_psum = sem("cum_in_psum")
        diag_ready = sem("diag_ready")
        rows_in_psum = sem("rows_in_psum")
        ml_masked = sem("ml_masked")
        ml_max_ready = sem("ml_max_ready")
        ml_floor_sum = sem("ml_floor_sum")
        ml_floor = sem("ml_floor")
        decay_ready = sem("decay_ready")
        ml_copied = sem("ml_copied")
        ml_scores = sem("ml_scores")
        a_ready = sem("a_ready")
        den_step = sem("den_step")
        aT_in_psum = sem("aT_in_psum")
        aT_done = sem("aT_done")
        num_ready = sem("num_ready")
        mh_scaled = sem("mh_scaled")
        mhT_in_psum = sem("mhT_in_psum")
        stored = sem("stored")

        CONSTS = 16 * 7

        used[0] = 0
        c_sb = from_region([2, SEQ])
        cu = from_region([2, SEQ + 2])
        z = from_region([2, SEQ])
        c_tok, cu_tok, b_tok = (from_region([TILES, 256]) for _ in range(3))
        used[0] = 0
        pT = from_region([NG, 3 * P])
        used[0] = 0
        qk = from_region([2, TILES * QH * HD]).rearrange("p a (t c) -> p a t c", t=TILES)
        rope_c, rope_s = ([from_region([QH, ROT]) for _ in range(TILES)] for _ in range(2))
        qT = from_region([NG, 2, SEQ])
        kT = from_region([NG, 2, SEQ])
        v = from_region([NG, TILES, QH * HD])
        probs = [from_region([NG, 3 * P]) for _ in range(3)]
        smax = from_region([2, 2])
        nmax = from_region([2, 2])
        den = from_region([2, 2])
        rden = from_region([2, 2])
        used[0] = 0
        mqT = from_region([NH, SEQ])
        mkT = from_region([NH, SEQ])
        mv = from_region([NH, TILES, DV])
        mog = from_region([NH, TILES, DV])
        gT = from_region([SEQ])
        gates = from_region([TILES, 2 * NH])
        neg_f = from_region([TILES, NH])
        neg_abs = from_region([TILES, NH])
        exp_f = from_region([TILES, NH])
        ln_f = from_region([TILES, NH])
        lf = from_region([TILES, NH])
        cum = from_region([TILES, NH])
        r_col = from_region([TILES, NH])
        diag = xn[:, :, 3 * TILES * P:4 * TILES * P]
        decay = from_region([2, 3 * P])
        rmax = from_region([NH, TILES])
        neg_m = from_region([NH, TILES])
        floor_in = from_region([NH, TILES])
        floor_e = from_region([NH, TILES])
        a = from_region([2, 3 * P])
        aT = from_region([2, 3 * P])
        mden = from_region([NH, TILES])
        neg_den = from_region([NH, TILES])
        abs_den = from_region([NH, TILES])
        safe_den = from_region([NH, TILES])
        mrden = from_region([NH, TILES])
        mh = from_region([2, TILES * DV]).rearrange("p a (t c) -> p a t c", t=TILES)

        def w_of(sub):
            return BASE[sub]

        def ffn_no(sub):
            return KINDS[:sub].count("ffn")

        def conv_no(sub):
            return KINDS[:sub].count("conv")

        OT = {"ffn": 0, "conv": CONV_STEPS, "att": 2 * QUARTERS, "ml": NH}

        def ot_before(sub):
            return sum(OT[k] for k in KINDS[:sub])

        def early(i):
            return i % 2, i // 2

        H_SPLITS = EARLY // 2 + BLOCKS - EARLY

        def splits_up_to(i):
            return EARLY // 2 + i - EARLY + 1

        def h_slot(i):
            return i % 4 if i < BLOCKS - 2 else 4 + i - (BLOCKS - 2)

        def after_ffn(joint):
            return joint > 0 and KINDS[joint - 1] == "ffn"

        def before_ffn(joint):
            return joint < SUBLAYERS and KINDS[joint] == "ffn"

        def xT_bank(joint, t, b):
            if t and joint < SUBLAYERS and KINDS[joint] in ("ffn", "att"):
                return Y_BANK + (2 if KINDS[joint] == "att" else 0) + b
            return T_BANK + b

        def masked_row(n, t):
            base = xn[:, n // 2, :]
            return base[:, (n % 2) * 384:(n % 2) * 384 + P] if t == 0 else \
                base[:, (n % 2) * 384 + P:(n % 2) * 384 + 3 * P]

        block = ctx.enter_context(nc.Block())

        @block.sync
        def _(sp):
            sp.dma_start(x[:, 0, :], x_in[0:P, :]).then_inc(x_landed[0], 16)
            sp.dma_start(gain[:, 1, :], gains[0].partition_broadcast(P)).then_inc(gain_landed, 16)
            sp.dma_start(raw[:, 0, :], stream[0]).then_inc(raw_landed[0], 16)
            sp.dma_start(x[:, 1, :], x_in[P:2 * P, :]).then_inc(x_landed[1], 16)
            for n in range(1, RAW):
                sp.dma_start(raw[:, n, :], stream[n]).then_inc(raw_landed[n], 16)
            for p in range(RAW, 2 * RAW):
                sp.wait_ge(piece_split, p - RAW + 1)
                sp.dma_start(raw[:, p % RAW, :], stream[p]).then_inc(raw_landed[p % RAW], 16)
            sp.dma_start(conv_kT[:, :, :, :], conv_k).then_inc(loaded, 16)
            sp.dma_start(rope[:, :, :, :], rope_in).then_inc(loaded, 16)
            sp.dma_start(att_mask[:, :, :], att_mask_in).then_inc(loaded, 16)
            sp.dma_start(ml_mask[:, :], ml_mask_in).then_inc(loaded, 16)
            sp.dma_start(tri[:, :], tri_in).then_inc(loaded, 16)
            sp.dma_start(gw_raw[:, :, :], gate_w).then_inc(loaded, 16)
            sp.dma_start(gate_bias[:, :], gate_b.partition_broadcast(P)).then_inc(loaded, 16)
            with sp.Fori(2, PIECES // RAW) as turn:
                for n in range(RAW):
                    sp.wait_ge(piece_split, RAW * turn + n - RAW + 1)
                    sp.dma_start(raw[:, n, :], stream[RAW * turn + n]).then_inc(raw_landed[n], 16)
            for p in range(PIECES // RAW * RAW, PIECES):
                sp.wait_ge(piece_split, p - RAW + 1)
                sp.dma_start(raw[:, p % RAW, :], stream[p]).then_inc(raw_landed[p % RAW], 16)
            for t in range(TILES):
                sp.wait_ge(x_updated, TILES * (SUBLAYERS - 1) + t + 1)
                sp.dma_start(out[t * P:(t + 1) * P, :], x[:, t, :]).then_inc(stored, 16)
            sp.wait_ge(stored, 16 * TILES)

        @block.tensor
        def _(pe):
            def products(acc, lh, ll, rh, rl, start, stop):
                nc.tensor.matmul(acc, lh, rh, start=start, stop=False)
                nc.tensor.matmul(acc, lh, rl, start=False, stop=False)
                return nc.tensor.matmul(acc, ll, rh, start=False, stop=stop)

            def arriving(acc, joint, t, half, p, width, first_col):
                tok, slot = slice(t * P, (t + 1) * P), p % RING
                rows = [(k, slice(first_col + (k - 4 * half) * width, first_col + (k - 4 * half + 1) * width))
                        for k in range(4 * half, 4 * half + 4)]
                pe.wait_ge(xT_high_done, 4 * joint + 2 * t + half + 1)
                pe.wait_ge(piece_high, p + 1)
                for k, cols in rows:
                    nc.tensor.matmul(acc, xT_high[:, k, tok], w_high[:, slot, cols], start=k == 0, stop=False)
                x_ready(joint, t, half)
                for k, cols in rows:
                    nc.tensor.matmul(acc, xT_low[:, k, tok], w_high[:, slot, cols], start=False, stop=False)
                weights_ready(p)
                for k, cols in rows:
                    last = nc.tensor.matmul(acc, xT_high[:, k, tok], w_low[:, slot, cols], start=False, stop=k == KD - 1)
                return last

            def weights_ready(p):
                pe.wait_ge(piece_split, p + 1)

            def transpose_x(joint, t):
                pe.wait_ge(xn_ready, TILES * joint + t + 1)
                if joint == 0 and t == 0:
                    pe.wait_ge(ident_landed, 16)
                for b in range(2):
                    if t == 1:
                        pe.wait_ge(xT_split, 4 * joint + b + 1)
                    for k in range(4):
                        f = (4 * b + k) * P
                        last = nc.tensor.transpose(ps[:, xT_bank(joint, t, b), k * P:(k + 1) * P], xn[:, t, f:f + P], ident[:, :])
                    last.then_inc(xT_in_psum, 1)

            def x_ready(joint, t, half=1):
                pe.wait_ge(xT_split, 4 * joint + 2 * t + half + 1)

            def ffn(sub):
                h0, s0, w0 = BLOCKS * ffn_no(sub), H_SPLITS * ffn_no(sub), w_of(sub)

                def bank_free(i):
                    if i >= 2:
                        pe.wait_ge(h_ready, h0 + i - 1)

                def early_block(i, first_x=False, meanwhile=None):
                    c, t = early(i)
                    bank_free(i)
                    for half in range(2):
                        p = w0 + early_piece(c) + half
                        slot = p % RING
                        if first_x:
                            last = arriving(ps[:, GU_BANK + i % 2, :], sub, t, half, p, 512, 0)
                        else:
                            weights_ready(p)
                        for k in () if first_x else range(4 * half, 4 * half + 4):
                            tok = slice(t * P, (t + 1) * P)
                            cols = slice((k - 4 * half) * 512, (k - 4 * half + 1) * 512)
                            last = products(ps[:, GU_BANK + i % 2, :], xT_high[:, k, tok], xT_low[:, k, tok],
                                            w_high[:, slot, cols], w_low[:, slot, cols], k == 0, k == KD - 1)
                            if meanwhile and k == meanwhile[0]:
                                meanwhile[1]()
                        if t == 1:
                            last.then_inc(piece_used, 1)
                    if t == 0:
                        last.then_inc(gu_ready, 1)

                def block(i, p, turn=0, before=0):
                    bank_free(i + before)
                    weights_ready(p + RING * turn)
                    for e in range(2):
                        for k in range(KD):
                            cols = slice(k * 256 + e * P, k * 256 + (e + 1) * P)
                            last = products(ps[:, GU_BANK + i % 2, e * SEQ:(e + 1) * SEQ], w_high[:, p % RING, cols],
                                            w_low[:, p % RING, cols], xT_high[:, k, :], xT_low[:, k, :],
                                            k == 0, k == KD - 1)
                    last.then_inc(piece_used, 1)

                def transpose_h(i):
                    c, t = early(i)
                    pe.wait_ge(h_ready, h0 + i + 1)
                    for j in range(FT):
                        last = nc.tensor.transpose(ps[:, T_BANK + c, j * SEQ + t * P:j * SEQ + (t + 1) * P],
                                                   h[:, i % 2, j * P:(j + 1) * P], ident[:, :])
                    if t == 1:
                        last.then_inc(hT_in_psum, 1)

                def down(c, p, t, turn=0):
                    weights_ready(p + RING * turn)
                    for half in range(2):
                        for j in range(FT):
                            cols = slice(j * D + half * 512, j * D + half * 512 + 512)
                            tok, at = slice(t * P, (t + 1) * P), h_slot(FT * c + j)
                            last = products(ps[:, Y_BANK + 2 * t + half, :], oT_hi[:, at, tok], oT_lo[:, at, tok],
                                            w_high[:, p % RING, cols], w_low[:, p % RING, cols],
                                            c == 0 and j == 0, c == CHUNKS - 1 and j == FT - 1)
                    if t == 1:
                        last.then_inc(piece_used, 1)
                    elif c == CHUNKS - 1:
                        last.then_inc(y_ready, 1)

                def down_both(c, turn=0):
                    if c < EARLY // 2:
                        pe.wait_ge(hT_split, s0 + c + 1)
                    else:
                        pe.wait_ge(hT_split, s0 + splits_up_to(FT * c + 1) + 4 * turn)
                    for t in range(TILES):
                        down(c, w0 + down_piece(c), t, turn)

                def unit(c, turn=0):
                    block(2 * c + 2, w0 + block_piece(2 * c + 2), turn, 4 * turn)
                    block(2 * c + 3, w0 + block_piece(2 * c + 3), turn, 4 * turn)
                    down_both(c, turn)

                transpose_x(sub, 0)
                early_block(0, first_x=True)
                early_block(1, meanwhile=(4, lambda: transpose_x(sub, 1)))
                transpose_h(0)
                early_block(2, first_x=True)
                transpose_h(1)
                early_block(3)
                transpose_h(2)
                block(4, w0 + block_piece(4))
                transpose_h(3)
                down_both(0)
                block(5, w0 + block_piece(5))
                down_both(1)
                with pe.Fori(0, (CHUNKS - 5) // 2) as turn:
                    unit(2, turn)
                    unit(3, turn)
                for i in range(BLOCKS - 4, BLOCKS):
                    block(i, w0 + block_piece(i))
                for t in range(TILES):
                    for c in range(CHUNKS - 3, CHUNKS):
                        if t == 0:
                            pe.wait_ge(hT_split, s0 + splits_up_to(FT * c + 1))
                        down(c, w0 + down_piece(c), t)

            def project_out(sub):
                p0 = w_of(sub + 1) - OUT_PIECES
                for t in range(TILES):
                    tok = slice(t * P, (t + 1) * P)
                    for q in range(OUT_PIECES):
                        slot = (p0 + q) % RING
                        weights_ready(p0 + q)
                        if t == 0 and q % 2 == 0:
                            pe.wait_ge(oT_split, ot_before(sub) + OT[KINDS[sub]] * (q // 2 + 1) // 2)
                        for k4 in range(4):
                            k, cols = 4 * (q // 2) + k4, slice(k4 * 512, (k4 + 1) * 512)
                            last = products(ps[:, Y_BANK + 2 * t + q % 2, :], oT_hi[:, k, tok], oT_lo[:, k, tok],
                                            w_high[:, slot, cols], w_low[:, slot, cols], k == 0, k == KD - 1)
                        if t == 1:
                            last.then_inc(piece_used, 1)
                    if t == 0:
                        last.then_inc(y_ready, 1)

            def features_first(slot, bank):
                for j in range(2):
                    for k in range(KD):
                        cols = slice(k * 256 + j * P, k * 256 + (j + 1) * P)
                        last = products(ps[:, bank, j * SEQ:(j + 1) * SEQ], w_high[:, slot, cols],
                                        w_low[:, slot, cols], xT_high[:, k, :], xT_low[:, k, :],
                                        k == 0, k == KD - 1)
                return last

            def tokens_first(slot, acc, t):
                for k in range(KD):
                    tok, cols = slice(t * P, (t + 1) * P), slice(k * 256, (k + 1) * 256)
                    last = products(acc, xT_high[:, k, tok], xT_low[:, k, tok], w_high[:, slot, cols],
                                    w_low[:, slot, cols], k == 0, k == KD - 1)
                return last

            def first_three(sub, t, tile0_done):
                transpose_x(sub, t)
                for i in range(3):
                    p, acc = w_of(sub) + i, ps[:, FIRST_BANKS[t][i], 0:256]
                    if i == 0:
                        arriving(acc, sub, t, 0, p, 256, 0)
                        last = arriving(acc, sub, t, 1, p, 256, 4 * 256)
                    else:
                        weights_ready(p)
                        last = tokens_first(p % RING, acc, t)
                    last.then_inc(tile0_done if t == 0 else piece_used, 1)

            def conv(sub):
                w0 = w_of(sub)
                for t in range(TILES):
                    first_three(sub, t, conv_tile0)
                for s in range(1, CONV_STEPS):
                    for part in range(3):
                        p = w0 + 3 * s + part
                        if p == w0 + 3:
                            pe.wait_ge(token_copied, 4 * conv_no(sub) + 3)
                        weights_ready(p)
                        features_first(p % RING, FIRST_BANKS[s % 2][part]).then_inc(piece_used, 1)
                        if p == w0 + 3:
                            pe.wait_ge(token_copied, 4 * conv_no(sub) + 4)
                            pe.wait_ge(token_cu_ready, 2 * conv_no(sub) + 2)
                            for e, rows in enumerate((cu_tok, b_tok)):
                                for j in range(2):
                                    for t in range(TILES):
                                        last = nc.tensor.transpose(ps[:, T_BANK + e, j * SEQ + t * P:j * SEQ + (t + 1) * P],
                                                                   rows[:, t, j * P:(j + 1) * P], ident[:, :])
                            last.then_inc(step0_in_psum, 1)
                pe.wait_ge(cu_ready, CONV_STEPS * (conv_no(sub) + 1) - 1)
                project_out(sub)

            def attention(sub):
                w0 = w_of(sub)
                for t in range(TILES):
                    transpose_x(sub, t)

                with pe.Fori(0, QUARTERS // 2) as turn:
                    for qs in range(2):
                        quarter = 2 * turn + qs
                        head0, part0 = QH * quarter, NG * QH * quarter

                        def project(i, t):
                            m, p = 2 * i + t, w0 + QP * qs + i
                            weights_ready(p + 3 * RING * turn)
                            if i == 0:
                                x_ready(sub, t)
                            if i >= QK:
                                bank = ((0, 1), (7, 0), (1, 0))[i - QK][t]
                                if i == QK:
                                    pe.wait_ge(oT_split, ot_before(sub) + 2 * quarter)
                                else:
                                    pe.wait_ge(proj_copied, 2 * QP * quarter + (m - 2 if m < 2 * QP - 1 else m - 1))
                            else:
                                bank = 2 + m % 3
                                if m >= 3:
                                    pe.wait_ge(proj_copied, 2 * QP * quarter + m - 2)
                            last = tokens_first(p % RING, ps[:, bank, 0:256], t)
                            last.then_inc(proj_ready if t == 0 else piece_used, 1)

                        def transpose_qk(m):
                            pe.wait_ge(rope_done, 2 * QK * quarter + m + 1)
                            if m >= 2:
                                pe.wait_ge(qkT_done, 2 * QK * quarter + m - 1)
                            for j in range(2):
                                last = nc.tensor.transpose(ps[:, 5 + m % 2, j * P:(j + 1) * P],
                                                           qk[:, m // 2 % 2, m % 2, j * P:(j + 1) * P], ident[:, :])
                            last.then_inc(qkT_in_psum, 1)

                        def scores(hh):
                            rows, j = slice(hh % 2 * HD, hh % 2 * HD + HD), hh // 2
                            if hh == 0:
                                pe.wait_ge(proj_copied, 2 * QP * quarter + 2 * QK)
                                pe.wait_ge(qkT_done, 2 * QK * (quarter + 1))
                            else:
                                pe.wait_ge(masked, head0 + hh)
                            for g in range(NG):
                                nc.tensor.matmul(ps[:, 2 + g // 2, g % 2 * 256:g % 2 * 256 + 256], qT[rows, g, j, P:2 * P],
                                                 kT[rows, g, j, :], start=True, stop=True)
                                last = nc.tensor.matmul(ps[:, 4, g * P:(g + 1) * P], qT[rows, g, j, 0:P],
                                                        kT[rows, g, j, 0:P], start=True, stop=True)
                            last.then_inc(scores_ready, 1)

                        def transpose_probs(hh):
                            pe.wait_ge(probs_ready, head0 + hh + 1)
                            if hh == 0:
                                pe.wait_ge(proj_copied, 2 * QP * quarter + 2 * QK + 3)
                            for g in range(NG):
                                for n in range(3):
                                    last = nc.tensor.transpose(ps[:, 5 + g, n * P:(n + 1) * P],
                                                               probs[hh % 3][:, g, n * P:(n + 1) * P], ident[:, :])
                                last.then_inc(pT_in_psum, 1)

                        def times_v(hh):
                            cols = slice(hh * HD, (hh + 1) * HD)
                            rows = slice(hh % 2 * HD, hh % 2 * HD + HD)
                            if hh == 0:
                                pe.wait_ge(proj_copied, 2 * QP * (quarter + 1))
                            for g in range(NG):
                                pe.wait_ge(pT_done, part0 + NG * hh + g + 1)
                                nc.tensor.matmul(ps[rows, O_BANK[hh // 2], 0:SEQ], v[:, g, 0, cols], pT[:, g, 0:2 * P],
                                                 start=g == 0, stop=False, skip_group_check=True)
                                last = nc.tensor.matmul(ps[rows, O_BANK[hh // 2], P:SEQ], v[:, g, 1, cols],
                                                        pT[:, g, 2 * P:3 * P], start=False, stop=g == NG - 1,
                                                        skip_group_check=True)
                            if hh % 2:
                                last.then_inc(o_ready, 1)

                        for m in range(2 * QK + 2):
                            project(m // 2, m % 2)
                            if 1 <= m <= 2 * QK:
                                transpose_qk(m - 1)
                        scores(0)
                        project(QK + 1, 0)
                        project(QK + 1, 1)
                        scores(1)
                        transpose_probs(0)
                        project(QK + 2, 0)
                        project(QK + 2, 1)
                        scores(2)
                        times_v(0)
                        scores(3)
                        transpose_probs(1)
                        times_v(1)
                        transpose_probs(2)
                        times_v(2)
                        transpose_probs(3)
                        times_v(3)
                project_out(sub)

            def mlstm(sub):
                w0 = w_of(sub)
                for t in range(TILES):
                    first_three(sub, t, ml_tile0)
                pe.wait_ge(gw_split, 1)
                pe.wait_ge(loaded, CONSTS)
                for k in range(KD):
                    last = products(ps[0:2 * NH, 2, 0:SEQ], gw_high[:, k, :], gw_low[:, k, :], xT_high[:, k, :],
                                    xT_low[:, k, :], k == 0, k == KD - 1)
                last.then_inc(gates_in_psum, 1)

                def feature_piece(i, bank):
                    weights_ready(w0 + i)
                    pe.wait_ge(ml_copied, i - 2)
                    features_first((w0 + i) % RING, bank).then_inc(piece_used, 1)

                def token_piece(i):
                    weights_ready(w0 + i)
                    pe.wait_ge(ml_copied, i + 2)
                    for t in range(TILES):
                        last = tokens_first((w0 + i) % RING, ps[:, (i + 1) % 2, t * 256:(t + 1) * 256], t)
                    last.then_inc(piece_used, 1)

                def scores(n):
                    if n == 0:
                        pe.wait_ge(ml_copied, 10)
                        pe.wait_ge(ml_max_ready, 1)
                    if n >= 2:
                        pe.wait_ge(a_ready, n - 1)
                    nc.tensor.matmul(ps[:, 2 + n % 2, 0:P], mqT[:, n, 0:P], mkT[:, n, 0:P], start=True, stop=True)
                    nc.tensor.matmul(ps[:, 2 + n % 2, P:3 * P], mqT[:, n, P:2 * P], mkT[:, n, :], start=True,
                                     stop=True).then_inc(ml_scores, 1)

                def transpose_a(n):
                    pe.wait_ge(a_ready, n + 1)
                    if n >= 2:
                        pe.wait_ge(aT_done, n - 1)
                    for j in range(3):
                        last = nc.tensor.transpose(ps[:, 4 + n % 2, j * P:(j + 1) * P], a[:, n % 2, j * P:(j + 1) * P],
                                                   ident[:, :])
                    last.then_inc(aT_in_psum, 1)

                def numerator(n):
                    pe.wait_ge(aT_done, n + 1)
                    pe.wait_ge(ml_copied, 11 + n)
                    if n >= 2:
                        pe.wait_ge(mh_scaled, 2 * (n - 1))
                    nc.tensor.matmul(ps[:, 6 + n % 2, 0:DV], aT[:, n % 2, 0:P], mv[:, n, 0, :], start=True, stop=True)
                    for s in range(2):
                        last = nc.tensor.matmul(ps[:, 6 + n % 2, DV:2 * DV], aT[:, n % 2, (s + 1) * P:(s + 2) * P],
                                                mv[:, n, s, :], start=s == 0, stop=s == 1)
                    last.then_inc(num_ready, 1)

                def transpose_out(n):
                    pe.wait_ge(mh_scaled, 2 * n + 2)
                    if n < 2:
                        pe.wait_ge(a_ready, n + 3)
                    else:
                        pe.wait_ge(oT_split, ot_before(sub) + n - 1)
                    for j in range(2):
                        for t in range(TILES):
                            last = nc.tensor.transpose(ps[:, 2 + n % 2, j * SEQ + t * P:j * SEQ + (t + 1) * P],
                                                       mh[:, n % 2, t, j * P:(j + 1) * P], ident[:, :])
                    last.then_inc(mhT_in_psum, 1)

                feature_piece(3, 4)
                pe.wait_ge(ml_copied, 5)
                pe.wait_ge(gT_copied, 1)
                for t in range(TILES):
                    last = nc.tensor.transpose(ps[:, 6, t * 2 * NH:(t + 1) * 2 * NH], gT[0:2 * NH, t * P:(t + 1) * P],
                                               ident[0:2 * NH, 0:2 * NH])
                last.then_inc(gates_turned, 1)
                feature_piece(4, 5)
                pe.wait_ge(ml_copied, 6)
                pe.wait_ge(lf_ready, 1)
                nc.tensor.matmul(ps[:, 7, 0:NH], tri[:, :], lf[:, 0, :], start=True, stop=True)
                nc.tensor.matmul(ps[:, 7, NH:2 * NH], ones[:, :], lf[:, 0, :], start=True, stop=False)
                nc.tensor.matmul(ps[:, 7, NH:2 * NH], tri[:, :], lf[:, 1, :], start=False,
                                 stop=True).then_inc(cum_in_psum, 1)
                feature_piece(5, 0)
                for n in range(NH):
                    pe.wait_ge(diag_ready, n + 1)
                    nc.tensor.matmul(ps[:, 2 + n // 2, n % 2 * SEQ:n % 2 * SEQ + SEQ], ones[:, :], diag[:, n % 2, :],
                                     start=True, stop=True).then_inc(rows_in_psum, 1)
                feature_piece(6, 1)
                token_piece(7)
                scores(0)
                token_piece(8)
                scores(1)
                transpose_a(0)
                token_piece(9)
                scores(2)
                transpose_a(1)
                numerator(0)
                token_piece(10)
                scores(3)
                transpose_a(2)
                numerator(1)
                transpose_out(0)
                token_piece(11)
                transpose_a(3)
                numerator(2)
                transpose_out(1)
                numerator(3)
                transpose_out(2)
                transpose_out(3)
                project_out(sub)

            program = {"ffn": ffn, "conv": conv, "att": attention, "ml": mlstm}
            for sub, kind in enumerate(KINDS):
                program[kind](sub)

        @block.scalar
        def _(act):
            act.dma_start(ident[:, :], ident_in).then_inc(ident_landed, 16)

            def high(p, turn=0):
                if p >= PIECES:
                    return
                act.wait_ge(raw_landed[p % RAW], 16 * (p // RAW + 1) + 32 * turn)
                if p >= RING:
                    act.wait_ge(piece_used, p - RING + 1 + RING * turn)
                nc.scalar.activation(w_high[:, p % RING, :], raw[:, p % RAW, :], ACT.Copy).then_inc(piece_high, 1)

            def square_y(joint, t):
                if t == 0:
                    act.wait_ge(y_ready, joint)
                else:
                    act.wait_ge(piece_used, BASE[joint])
                for half in range(2):
                    nc.scalar.activation(xn[:, t, half * 512:(half + 1) * 512], ps[:, Y_BANK + 2 * t + half, :], ACT.Square,
                                         scale=1.0 / (32 * Y_SCALE[KINDS[joint - 1]]),
                                         accum_out=mean_y[:, t, half:half + 1]).then_inc(y_mean, 1)

            def square_x(joint, t):
                if joint:
                    act.wait_ge(x_updated, TILES * (joint - 1) + t + 1)
                else:
                    act.wait_ge(x_landed[t], 16)
                nc.scalar.activation(xn[:, t, :], x[:, t, :], ACT.Square, scale=1.0 / 32,
                                     accum_out=mean_x[:, t:t + 1]).then_inc(x_mean, 1)

            def xT(joint, t, halves=(0, 1)):
                for b in halves:
                    act.wait_ge(xT_in_psum, 4 * joint + 2 * t + b + 1)
                    nc.scalar.activation(xT_high[:, 4 * b:4 * b + 4, t * P:(t + 1) * P],
                                         ps[:, xT_bank(joint, t, b), :].rearrange("p (k c) -> p k c", k=4),
                                         ACT.Copy).then_inc(xT_high_done, 1)

            def silu_of(sub, i, turn=0):
                if i < EARLY and early(i)[1] == 0:
                    act.wait_ge(gu_ready, 2 * ffn_no(sub) + early(i)[0] + 1)
                else:
                    p = early_piece(early(i)[0]) + 1 if i < EARLY else block_piece(i)
                    act.wait_ge(piece_used, w_of(sub) + p + 1 + RING * turn)
                nc.scalar.activation(silu[:, i % 2, :], ps[:, GU_BANK + i % 2, 0:SEQ], ACT.Silu).then_inc(silu_done, 1)

            def early_h_high(sub, c):
                act.wait_ge(hT_in_psum, 2 * ffn_no(sub) + c + 1)
                nc.scalar.activation(oT_hi[:, FT * c:FT * (c + 1), :].rearrange("p a b -> p (a b)"), ps[:, T_BANK + c, :],
                                     ACT.Copy).then_inc(hT_high_done, 1)

            def h_high(sub, i, turn=0):
                act.wait_ge(h_ready, BLOCKS * ffn_no(sub) + i + 1 + 4 * turn)
                if i == EARLY:
                    act.wait_ge(piece_used, w_of(sub) + down_piece(0) + 1)
                nc.scalar.activation(oT_hi[:, h_slot(i), :], h[:, i % 2, :], ACT.Copy).then_inc(hT_high_done, 1)

            def joint_part(joint):
                w0 = w_of(joint)
                if joint:
                    square_y(joint, 0)
                    if not after_ffn(joint):
                        high(w0 + 2)
                if joint == SUBLAYERS:
                    square_y(joint, 1)
                    return
                square_x(joint, 0)
                if joint == 0:
                    xT(joint, 0, (0,))
                    high(0)
                    xT(joint, 0, (1,))
                    square_x(joint, 1)
                    for p in range(1, 4):
                        high(p)
                else:
                    high(w0 + 3)
                    if before_ffn(joint):
                        xT(joint, 0)
                        square_y(joint, 1)
                    else:
                        square_y(joint, 1)
                        xT(joint, 0)
                    square_x(joint, 1)
                if before_ffn(joint):
                    silu_of(joint, 0)
                xT(joint, 1)
                act.dma_start(gain[:, 0, :], gains[2 * joint + 1].partition_broadcast(P)).then_inc(gain_landed, 16)
                if joint + 1 < SUBLAYERS:
                    act.dma_start(gain[:, 1, :], gains[2 * joint + 2].partition_broadcast(P)).then_inc(gain_landed, 16)

            def ffn(sub):
                w0 = w_of(sub)

                def unit(c, turn):
                    p = w0 + block_piece(2 * c + 2)
                    silu_of(sub, 2 * c + 2, turn=turn)
                    high(p + 5, turn)
                    h_high(sub, 2 * c + 2, turn)
                    silu_of(sub, 2 * c + 3, turn=turn)
                    high(p + 6, turn)
                    h_high(sub, 2 * c + 3, turn)
                    high(p + 7, turn)

                silu_of(sub, 1)
                high(w0 + 4)
                high(w0 + 5)
                silu_of(sub, 2)
                high(w0 + 6)
                high(w0 + 7)
                silu_of(sub, 3)
                early_h_high(sub, 0)
                high(w0 + 8)
                silu_of(sub, 4)
                early_h_high(sub, 1)
                high(w0 + 9)
                h_high(sub, 4)
                high(w0 + 10)
                silu_of(sub, 5)
                high(w0 + 11)
                h_high(sub, 5)
                high(w0 + 12)
                with act.Fori(0, (CHUNKS - 5) // 2) as turn:
                    unit(2, turn)
                    unit(3, turn)
                for i in range(BLOCKS - 4, BLOCKS):
                    silu_of(sub, i)
                    if i < BLOCKS - 1:
                        high(w0 + block_piece(i) + 5)
                    h_high(sub, i)
                high(w0 + FFN_PIECES + 1)
                high(w0 + FFN_PIECES + 2)

            def conv(sub):
                w0, n0 = w_of(sub), CONV_STEPS * conv_no(sub)

                def copy_token_rows(t, part, to):
                    if t == 0:
                        act.wait_ge(conv_tile0, 3 * conv_no(sub) + part + 1)
                    else:
                        act.wait_ge(piece_used, w0 + part + 1)
                    nc.scalar.activation(to[:, t, :], ps[:, FIRST_BANKS[t][part], 0:256], ACT.Copy).then_inc(token_copied, 1)

                def o_high(s):
                    act.wait_ge(conv_ready, n0 + s + 1)
                    nc.scalar.activation(oT_hi[:, 2 * s:2 * s + 2, :], z, ACT.Copy).then_inc(oT_high_done, 1)

                copy_token_rows(0, 0, c_tok)
                copy_token_rows(0, 2, b_tok)
                high(w0 + 5)
                copy_token_rows(1, 0, c_tok)
                high(w0 + 6)
                copy_token_rows(1, 2, b_tok)
                high(w0 + 7)
                for s in range(1, CONV_STEPS):
                    p = w0 + 3 * s
                    act.wait_ge(piece_used, p + 1)
                    if s >= 2:
                        act.wait_ge(cu_ready, n0 + s)
                    nc.scalar.activation(c_sb.rearrange("p a b -> p (a b)"), ps[:, FIRST_BANKS[s % 2][0], :],
                                         ACT.Copy).then_inc(c_copied, 1)
                    high(p + 5)
                    high(p + 6)
                    if s == 1:
                        o_high(0)
                    high(p + 7)
                    o_high(s)

            def attention(sub):
                w0 = w_of(sub)

                with act.Fori(0, QUARTERS // 2) as turn:
                    for qs in range(2):
                        quarter = 2 * turn + qs
                        head0, part0 = QH * quarter, NG * QH * quarter

                        def copy_out(i, t):
                            if t == 0:
                                act.wait_ge(proj_ready, QP * quarter + i + 1)
                            else:
                                act.wait_ge(piece_used, w0 + QP * qs + i + 1 + 3 * RING * turn)
                            if i >= QK:
                                to, bank = v[:, i - QK, t, :], ((0, 1), (7, 0), (1, 0))[i - QK][t]
                            else:
                                to, bank = qk[:, i % 2, t, :], 2 + (2 * i + t) % 3
                            nc.scalar.activation(to, ps[:, bank, 0:256], ACT.Copy).then_inc(proj_copied, 1)

                        def copy_qkT(m):
                            act.wait_ge(qkT_in_psum, 2 * QK * quarter + m + 1)
                            to = (kT if m // 2 % 2 else qT)[:, m // 4, :, m % 2 * P:(m % 2 + 1) * P]
                            nc.scalar.activation(to, ps[:, 5 + m % 2, 0:2 * P].rearrange("p (j c) -> p j c", j=2),
                                                 ACT.Copy).then_inc(qkT_done, 1)

                        def piece(i):
                            high(w0 + QP * qs + i + 5, 3 * turn)

                        def exp(hh):
                            pr = probs[hh % 3]
                            act.wait_ge(max_ready, head0 + hh + 1)
                            for t, cols in ((1, slice(P, 3 * P)), (0, slice(0, P))):
                                last = nc.scalar.activation(pr[:, :, cols], pr[:, :, cols], ACT.Exp, scale=HD ** -0.5,
                                                            bias=nmax[:, hh % 2, t:t + 1],
                                                            accum_out=den[:, hh % 2, t:t + 1])
                            last.then_inc(exp_done, 1)

                        def copy_pT(hh):
                            for g in range(NG):
                                act.wait_ge(pT_in_psum, part0 + NG * hh + g + 1)
                                nc.scalar.activation(pT[:, g, :], ps[:, 5 + g, 0:3 * P], ACT.Copy).then_inc(pT_done, 1)

                        def o_high(j):
                            act.wait_ge(o_ready, 2 * quarter + j + 1)
                            nc.scalar.activation(oT_hi[:, bass.ds(2 * quarter + j, 1), :].rearrange("p a b -> p (a b)"),
                                                 ps[:, O_BANK[j], 0:SEQ], ACT.Copy).then_inc(oT_high_done, 1)

                        for i in range(QK + 1):
                            for t in range(TILES):
                                copy_out(i, t)
                                if 1 <= 2 * i + t <= 2 * QK:
                                    copy_qkT(2 * i + t - 1)
                            piece(i)
                        exp(0)
                        copy_out(QK + 1, 0)
                        piece(QK + 1)
                        copy_out(QK + 1, 1)
                        exp(1)
                        copy_pT(0)
                        copy_out(QK + 2, 0)
                        copy_out(QK + 2, 1)
                        piece(QK + 2)
                        exp(2)
                        copy_pT(1)
                        exp(3)
                        o_high(0)
                        copy_pT(3)
                        o_high(1)

            def mlstm(sub):
                w0 = w_of(sub)
                act.wait_ge(loaded, CONSTS)
                nc.scalar.activation(gw_high[:, :, :], gw_raw[:, :, :], ACT.Copy).then_inc(gw_high_done, 1)

                def gate_out(i, t):
                    if i == 3:
                        act.wait_ge(piece_used, w0 + 12)
                        to, at = mog[:, 3, :, :].rearrange("p a b -> p (a b)"), ps[:, 0, :]
                    else:
                        act.wait_ge(*((piece_used, w0 + i + 1) if t else (ml_tile0, i + 1)))
                        to, at = mog[:, i, t, :], ps[:, FIRST_BANKS[t][i], 0:256]
                    nc.scalar.activation(to, at, ACT.Sigmoid).then_inc(ml_copied, 1)

                for t in range(TILES):
                    for i in range(3):
                        gate_out(i, t)
                        if t or i == 2:
                            high(w0 + 5 + (i + 1 if t else 0))
                act.wait_ge(gates_in_psum, 1)
                nc.scalar.activation(gT[0:2 * NH, :], ps[0:2 * NH, 2, 0:SEQ], ACT.Copy).then_inc(gT_copied, 1)
                act.wait_ge(gate_step, 3)
                nc.scalar.activation(exp_f, neg_abs, ACT.Exp).then_inc(gate_exp, 1)
                act.wait_ge(gate_exp, 1)
                nc.scalar.activation(ln_f, exp_f, ACT.Ln, bias=1.0).then_inc(gate_ln, 1)

                def copy_out(i):
                    act.wait_ge(piece_used, w0 + i + 1)
                    if i < 7:
                        n, bank = (i - 3) % 2, (4, 5, 0, 1)[i - 3]
                        to = (mqT if i < 5 else mkT)[:, 2 * n:2 * n + 2, :]
                    else:
                        to, bank = mv[:, i - 7, :, :], (i + 1) % 2
                    nc.scalar.activation(to.rearrange("p a b -> p (a b)"), ps[:, bank, :], ACT.Copy,
                                         scale=DQK ** -0.5 if 5 <= i < 7 else 1.0).then_inc(ml_copied, 1)

                def decay_of(n):
                    if n >= 2:
                        act.wait_ge(a_ready, n - 1)
                    act.wait_ge(ml_max_ready, 1)
                    if n == 0:
                        act.wait_ge(ml_floor_sum, 1)
                        nc.scalar.activation(floor_e, floor_in, ACT.Exp).then_inc(ml_floor, 1)
                    nc.scalar.activation(decay[:, n % 2, 0:P], masked_row(n, 0), ACT.Exp, bias=neg_m[:, n, 0:1])
                    nc.scalar.activation(decay[:, n % 2, P:3 * P], masked_row(n, 1), ACT.Exp,
                                         bias=neg_m[:, n, 1:2]).then_inc(decay_ready, 1)

                def copy_aT(n):
                    act.wait_ge(aT_in_psum, n + 1)
                    if n >= 2:
                        act.wait_ge(num_ready, n - 1)
                    nc.scalar.activation(aT[:, n % 2, :], ps[:, 4 + n % 2, 0:3 * P], ACT.Copy).then_inc(aT_done, 1)

                def o_high(n):
                    act.wait_ge(mhT_in_psum, n + 1)
                    nc.scalar.activation(oT_hi[:, 2 * n:2 * n + 2, :].rearrange("p a b -> p (a b)"), ps[:, 2 + n % 2, :],
                                         ACT.Copy).then_inc(oT_high_done, 1)

                for i in range(3, 7):
                    copy_out(i)
                    high(w0 + i + 6)
                    if i >= 5:
                        decay_of(i - 5)
                for n in range(NH):
                    copy_out(7 + n)
                    if n:
                        copy_aT(n - 1)
                    if 1 <= n < 3:
                        decay_of(n + 1)
                    high(w0 + 13 + n)
                o_high(0)
                gate_out(3, None)
                copy_aT(3)
                for n in range(1, NH):
                    o_high(n)

            program = {"ffn": ffn, "conv": conv, "att": attention, "ml": mlstm}
            for sub, kind in enumerate(KINDS):
                joint_part(sub)
                if kind != "ffn":
                    high(w_of(sub) + 4)
                program[kind](sub)
                if kind != "ffn":
                    high(w_of(sub + 1) + 1)
            joint_part(SUBLAYERS)

        @block.vector
        def _(dve):
            nc.vector.memset(minus_half[:, :], -0.5).then_inc(consts_set, 1)
            nc.vector.memset(ones[:, :], 1.0).then_inc(consts_set, 1)

            def low(p, turn=0):
                if p >= PIECES:
                    return
                dve.wait_ge(piece_high, p + 1 + RING * turn)
                nc.vector.tensor_tensor(w_low[:, p % RING, :], raw[:, p % RAW, :], w_high[:, p % RING, :],
                                        ALU.subtract).then_inc(piece_split, 1)

            def update_x(joint, t):
                n = TILES * (joint - 1) + t
                dve.wait_ge(gain_landed, 16 * min(1 + 2 * joint, 2 * SUBLAYERS))
                for half in range(2):
                    cols = slice(half * 512, (half + 1) * 512)
                    dve.wait_ge(y_mean, 2 * n + half + 1)
                    nc.vector.tensor_tensor(xn[:, t, cols], ps[:, Y_BANK + 2 * t + half, :], gain[:, 0, cols],
                                            ALU.mult).then_inc(y_gained, 1)
                dve.wait_ge(y_gained, 2 * n + 2)
                dve.wait_ge(y_rstd, n + 1)
                nc.vector.scalar_tensor_tensor(out=x[:, t, :], in0=xn[:, t, :], scalar=rstd_y[:, t:t + 1], in1=x[:, t, :],
                                               op0=ALU.mult, op1=ALU.add).then_inc(x_updated, 1)

            def pre_norm(joint, t):
                dve.wait_ge(x_rstd, TILES * joint + t + 1)
                if joint == 0:
                    dve.wait_ge(gain_landed, 16)
                nc.vector.scalar_tensor_tensor(out=xn[:, t, :], in0=x[:, t, :], scalar=rstd_x[:, t:t + 1],
                                               in1=gain[:, 1, :], op0=ALU.mult, op1=ALU.mult).then_inc(xn_ready, 1)

            def xT(joint, t, halves=(0, 1)):
                for b in halves:
                    dve.wait_ge(xT_high_done, 4 * joint + 2 * t + b + 1)
                    cols = slice(t * P, (t + 1) * P)
                    nc.vector.tensor_tensor(xT_low[:, 4 * b:4 * b + 4, cols],
                                            ps[:, xT_bank(joint, t, b), :].rearrange("p (k c) -> p k c", k=4),
                                            xT_high[:, 4 * b:4 * b + 4, cols], ALU.subtract).then_inc(xT_split, 1)

            def times_up(sub, i, turn=0):
                dve.wait_ge(silu_done, BLOCKS * ffn_no(sub) + i + 1 + 4 * turn)
                if i >= EARLY + 2:
                    dve.wait_ge(hT_split, H_SPLITS * ffn_no(sub) + splits_up_to(i - 2) + 4 * turn)
                nc.vector.tensor_tensor(h[:, i % 2, :], silu[:, i % 2, :], ps[:, GU_BANK + i % 2, SEQ:2 * SEQ],
                                        ALU.mult).then_inc(h_ready, 1)

            def early_h_low(sub, c):
                dve.wait_ge(hT_high_done, H_SPLITS * ffn_no(sub) + c + 1)
                at = slice(FT * c, FT * (c + 1))
                nc.vector.tensor_tensor(oT_lo[:, at, :].rearrange("p a b -> p (a b)"), ps[:, T_BANK + c, :],
                                        oT_hi[:, at, :].rearrange("p a b -> p (a b)"), ALU.subtract).then_inc(hT_split, 1)

            def h_low(sub, i, turn=0):
                dve.wait_ge(hT_high_done, H_SPLITS * ffn_no(sub) + splits_up_to(i) + 4 * turn)
                nc.vector.tensor_tensor(oT_lo[:, h_slot(i), :], h[:, i % 2, :], oT_hi[:, h_slot(i), :],
                                        ALU.subtract).then_inc(hT_split, 1)

            def joint_part(joint):
                w0 = w_of(joint)
                if joint:
                    update_x(joint, 0)
                    if not after_ffn(joint):
                        low(w0 + 2)
                if joint < SUBLAYERS:
                    pre_norm(joint, 0)
                    if joint == 0:
                        xT(joint, 0, (0,))
                        low(0)
                        xT(joint, 0, (1,))
                    elif KINDS[joint] != "att":
                        xT(joint, 0)
                if joint:
                    update_x(joint, 1)
                if joint == SUBLAYERS:
                    return
                if joint == 0:
                    low(1)
                    pre_norm(joint, 1)
                    low(2)
                    low(3)
                elif KINDS[joint] == "att":
                    xT(joint, 0)
                    pre_norm(joint, 1)
                    low(w0 + 3)
                else:
                    low(w0 + 3)
                    pre_norm(joint, 1)
                if before_ffn(joint):
                    times_up(joint, 0)
                xT(joint, 1)

            def ffn(sub):
                w0 = w_of(sub)

                def unit(c, turn):
                    p = w0 + block_piece(2 * c + 2)
                    times_up(sub, 2 * c + 2, turn)
                    low(p + 5, turn)
                    h_low(sub, 2 * c + 2, turn)
                    times_up(sub, 2 * c + 3, turn)
                    low(p + 6, turn)
                    h_low(sub, 2 * c + 3, turn)
                    low(p + 7, turn)

                times_up(sub, 1)
                low(w0 + 4)
                low(w0 + 5)
                times_up(sub, 2)
                low(w0 + 6)
                low(w0 + 7)
                times_up(sub, 3)
                early_h_low(sub, 0)
                low(w0 + 8)
                times_up(sub, 4)
                early_h_low(sub, 1)
                low(w0 + 9)
                h_low(sub, 4)
                low(w0 + 10)
                times_up(sub, 5)
                low(w0 + 11)
                h_low(sub, 5)
                low(w0 + 12)
                with dve.Fori(0, (CHUNKS - 5) // 2) as turn:
                    unit(2, turn)
                    unit(3, turn)
                for i in range(BLOCKS - 4, BLOCKS):
                    times_up(sub, i)
                    if i < BLOCKS - 1:
                        low(w0 + block_piece(i) + 5)
                    h_low(sub, i)
                low(w0 + FFN_PIECES + 1)
                low(w0 + FFN_PIECES + 2)

            def conv(sub):
                w0, layer = w_of(sub), conv_no(sub)
                n0, o0 = CONV_STEPS * layer, ot_before(sub)
                dve.wait_ge(loaded, CONSTS)
                nc.vector.memset(cu[:, :, 0:2], 0.0).then_inc(pads_zeroed, 1)
                dve.wait_ge(pads_zeroed, layer + 1)
                for t in range(TILES):
                    dve.wait_ge(token_copied, 4 * layer + 2 * t + 1)
                    if t == 0:
                        dve.wait_ge(conv_tile0, 3 * layer + 2)
                    else:
                        dve.wait_ge(piece_used, w0 + 2)
                    nc.vector.tensor_tensor(cu_tok[:, t, :], c_tok[:, t, :], ps[:, FIRST_BANKS[t][1], 0:256],
                                            ALU.mult).then_inc(token_cu_ready, 1)
                    low(w0 + 5 + t)
                low(w0 + 7)
                for s in range(CONV_STEPS):
                    p, n, banks = w0 + 3 * s, n0 + s, FIRST_BANKS[s % 2]
                    b = ps[:, banks[2] if s else T_BANK + 1, :].rearrange("p (j c) -> p j c", j=2)
                    if s == 0:
                        dve.wait_ge(step0_in_psum, layer + 1)
                        nc.vector.tensor_copy(cu[:, :, 2:SEQ + 2], ps[:, T_BANK, :].rearrange("p (j c) -> p j c", j=2))\
                            .then_inc(cu_ready, 1)
                    else:
                        low(p + 5)
                        dve.wait_ge(c_copied, (CONV_STEPS - 1) * layer + s)
                        dve.wait_ge(piece_used, p + 2)
                        nc.vector.tensor_tensor(cu[:, :, 2:SEQ + 2], c_sb,
                                                ps[:, banks[1], :].rearrange("p (j c) -> p j c", j=2),
                                                ALU.mult).then_inc(cu_ready, 1)
                    dve.wait_ge(cu_ready, n + 1)
                    taps = 2 * CONV_W * n
                    for j in range(CONV_W):
                        for e in range(2):
                            k = conv_kT[:, layer, j, 2 * s + e:2 * s + e + 1]
                            shifted = cu[:, e, CONV_W - 1 - j:CONV_W - 1 - j + SEQ]
                            if j == 0:
                                tap = nc.vector.tensor_scalar(z[:, e, :], shifted, k, None, ALU.mult)
                            else:
                                dve.wait_ge(tap_done, taps + 2 * (j - 1) + e + 1)
                                tap = nc.vector.scalar_tensor_tensor(out=z[:, e, :], in0=shifted, scalar=k,
                                                                     in1=z[:, e, :], op0=ALU.mult, op1=ALU.add)
                            tap.then_inc(tap_done, 1)
                    if s:
                        low(p + 6)
                        dve.wait_ge(piece_used, p + 3)
                    dve.wait_ge(tap_done, taps + 2 * CONV_W)
                    nc.vector.tensor_tensor(z, z, b, ALU.mult).then_inc(conv_ready, 1)
                    if 0 < s < CONV_STEPS - 1:
                        low(p + 7)
                    dve.wait_ge(oT_high_done, o0 + s + 1)
                    nc.vector.tensor_tensor(oT_lo[:, 2 * s:2 * s + 2, :], z, oT_hi[:, 2 * s:2 * s + 2, :],
                                            ALU.subtract).then_inc(oT_split, 1)
                low(p + 7)

            def attention(sub):
                w0, o0 = w_of(sub), ot_before(sub)
                dve.wait_ge(loaded, CONSTS)

                with dve.Fori(0, QUARTERS // 2) as turn:
                    for qs in range(2):
                        quarter = 2 * turn + qs
                        head0 = QH * quarter

                        def rotate(i, t):
                            n = 2 * i + t
                            dve.wait_ge(proj_copied, 2 * QP * quarter + n + 1)
                            q = qk[:, i % 2, t, :].rearrange("p (h c) -> p h c", h=QH)
                            cos, sin = (rope[:, t, e, :].rearrange("p (h c) -> p h c", h=QH) for e in range(2))
                            by_cos, by_sin = rope_c[t], rope_s[t]
                            if n >= 2:
                                dve.wait_ge(rope_done, 2 * QK * quarter + n - 1)
                            nc.vector.tensor_tensor(by_cos, q[:, :, 0:ROT], cos, ALU.mult)
                            nc.vector.tensor_tensor(by_sin, q[:, :, 0:ROT], sin, ALU.mult).then_inc(rope_products, 1)
                            dve.wait_ge(rope_products, 2 * QK * quarter + n + 1)
                            half = ROT // 2
                            nc.vector.tensor_tensor(q[:, :, 0:half], by_cos[:, :, 0:half], by_sin[:, :, half:ROT],
                                                    ALU.subtract)
                            nc.vector.tensor_tensor(q[:, :, half:ROT], by_cos[:, :, half:ROT], by_sin[:, :, 0:half],
                                                    ALU.add).then_inc(rope_done, 1)

                        def mask(hh):
                            n, pr = head0 + hh, probs[hh % 3]
                            dve.wait_ge(scores_ready, n + 1)
                            nc.vector.memset(den[:, hh % 2, :], 0.0)
                            s1 = ps[:, 2:4, :].rearrange("p a b -> p (a b)")[:, 0:NG * 2 * P]
                            nc.vector.tensor_tensor_reduce(pr[:, :, P:3 * P], s1.rearrange("p (g c) -> p g c", g=NG),
                                                           att_mask[:, :, :], 1.0, MASK_LOW, ALU.add, ALU.max,
                                                           smax[:, hh % 2, 1:2])
                            s0 = ps[:, 4, 0:NG * P].rearrange("p (g c) -> p g c", g=NG)
                            nc.vector.tensor_tensor_reduce(pr[:, :, 0:P], s0, att_mask[:, :, P:2 * P], 1.0, MASK_LOW,
                                                           ALU.add, ALU.max, smax[:, hh % 2, 0:1]).then_inc(masked, 1)
                            dve.wait_ge(masked, n + 1)
                            nc.vector.tensor_scalar(nmax[:, hh % 2, :], smax[:, hh % 2, :], -HD ** -0.5, None,
                                                    ALU.mult).then_inc(max_ready, 1)

                        def normalize(hh):
                            n, pr = head0 + hh, probs[hh % 3]
                            dve.wait_ge(exp_done, n + 1)
                            nc.vector.reciprocal(rden[:, hh % 2, :], den[:, hh % 2, :]).then_inc(recip_done, 1)
                            dve.wait_ge(recip_done, n + 1)
                            nc.vector.tensor_scalar(pr[:, :, 0:P], pr[:, :, 0:P], rden[:, hh % 2, 0:1], None, ALU.mult)
                            nc.vector.tensor_scalar(pr[:, :, P:3 * P], pr[:, :, P:3 * P], rden[:, hh % 2, 1:2], None,
                                                    ALU.mult).then_inc(probs_ready, 1)

                        def o_low(j):
                            dve.wait_ge(oT_high_done, o0 + 2 * quarter + j + 1)
                            at = bass.ds(2 * quarter + j, 1)
                            nc.vector.tensor_tensor(oT_lo[:, at, :].rearrange("p a b -> p (a b)"),
                                                    ps[:, O_BANK[j], 0:SEQ],
                                                    oT_hi[:, at, :].rearrange("p a b -> p (a b)"),
                                                    ALU.subtract).then_inc(oT_split, 1)

                        for i in range(QP):
                            if i < QK:
                                for t in range(TILES):
                                    rotate(i, t)
                            if i < QP - 1:
                                low(w0 + QP * qs + i + 5, 3 * turn)
                            if i >= QK:
                                mask(i - QK)
                                normalize(i - QK)
                        mask(3)
                        for g in range(NG):
                            dve.wait_ge(pT_in_psum, NG * (head0 + 2) + g + 1)
                            nc.vector.tensor_copy(pT[:, g, :], ps[:, 5 + g, 0:3 * P]).then_inc(pT_done, 1)
                        normalize(3)
                        low(w0 + QP * (qs + 1) + 4, 3 * turn)
                        for j in range(QH // 2):
                            o_low(j)

            def mlstm(sub):
                w0, o0 = w_of(sub), ot_before(sub)
                dve.wait_ge(loaded, CONSTS)
                dve.wait_ge(gw_high_done, 1)
                nc.vector.tensor_tensor(gw_low[:, :, :], gw_raw[:, :, :], gw_high[:, :, :], ALU.subtract).then_inc(gw_split, 1)
                for i in range(5, 9):
                    low(w0 + i)
                dve.wait_ge(gates_turned, 1)
                for t in range(TILES):
                    step = nc.vector.tensor_tensor(gates[:, t, :], ps[:, 6, t * 2 * NH:(t + 1) * 2 * NH],
                                                   gate_bias[:, :], ALU.add)
                step.then_inc(gate_step, 1)
                forget = gates[:, :, NH:2 * NH]
                dve.wait_ge(gate_step, 1)
                nc.vector.tensor_scalar(neg_f, forget, -1.0, None, ALU.mult).then_inc(gate_step, 1)
                dve.wait_ge(gate_step, 2)
                nc.vector.tensor_tensor(neg_abs, forget, neg_f, ALU.min).then_inc(gate_step, 1)
                dve.wait_ge(gate_ln, 1)
                nc.vector.scalar_tensor_tensor(out=lf, in0=forget, scalar=0.0, in1=ln_f, op0=ALU.min,
                                               op1=ALU.subtract).then_inc(lf_ready, 1)
                low(w0 + 9)
                dve.wait_ge(cum_in_psum, 1)
                nc.vector.tensor_copy(cum, ps[:, 7, 0:2 * NH].rearrange("p (t n) -> p t n", t=TILES)).then_inc(gate_step, 1)
                dve.wait_ge(gate_step, 4)
                nc.vector.tensor_tensor(r_col, gates[:, :, 0:NH], cum, ALU.subtract).then_inc(gate_step, 1)
                dve.wait_ge(gate_step, 5)
                for n in range(NH):
                    if n >= 2:
                        dve.wait_ge(rows_in_psum, n - 1)
                    for t in range(TILES):
                        last = nc.vector.tensor_scalar(diag[:, n % 2, t * P:(t + 1) * P], ident[:, :],
                                                       r_col[:, t, n:n + 1], None, ALU.mult)
                    last.then_inc(diag_ready, 1)
                low(w0 + 10)
                for n in range(NH):
                    dve.wait_ge(rows_in_psum, n + 1 if n % 2 else n + 2)
                    rows = ps[:, 2 + n // 2, n % 2 * SEQ:n % 2 * SEQ + SEQ]
                    nc.vector.tensor_tensor_reduce(masked_row(n, 0), rows[:, 0:P], ml_mask[:, P:2 * P], 1.0, MASK_LOW,
                                                   ALU.add, ALU.max, rmax[:, n, 0:1])
                    last = nc.vector.tensor_tensor_reduce(masked_row(n, 1), rows, ml_mask[:, :], 1.0, MASK_LOW,
                                                          ALU.add, ALU.max, rmax[:, n, 1:2])
                last.then_inc(ml_masked, 1)
                dve.wait_ge(ml_masked, 1)
                nc.vector.tensor_scalar(neg_m, rmax, 0.0, -1.0, ALU.max, ALU.mult).then_inc(ml_max_ready, 1)
                dve.wait_ge(ml_max_ready, 1)
                nc.vector.tensor_tensor(floor_in, neg_m, cum.rearrange("p t n -> p n t"), ALU.subtract)\
                    .then_inc(ml_floor_sum, 1)

                def a_of(n):
                    dve.wait_ge(ml_scores, n + 1)
                    dve.wait_ge(decay_ready, n + 1)
                    if n >= 2:
                        dve.wait_ge(aT_in_psum, n - 1)
                    for t, cols in ((0, slice(0, P)), (1, slice(P, 3 * P))):
                        last = nc.vector.tensor_tensor_reduce(a[:, n % 2, cols], ps[:, 2 + n % 2, cols],
                                                              decay[:, n % 2, cols], 1.0, 0.0, ALU.mult, ALU.add,
                                                              mden[:, n, t:t + 1])
                    last.then_inc(a_ready, 1)
                    dve.wait_ge(a_ready, n + 1)
                    nc.vector.tensor_scalar(neg_den[:, n, :], mden[:, n, :], -1.0, None, ALU.mult).then_inc(den_step, 1)
                    dve.wait_ge(den_step, 4 * n + 1)
                    nc.vector.tensor_tensor(abs_den[:, n, :], mden[:, n, :], neg_den[:, n, :], ALU.max).then_inc(den_step, 1)
                    dve.wait_ge(den_step, 4 * n + 2)
                    dve.wait_ge(ml_floor, 1)
                    nc.vector.tensor_tensor(safe_den[:, n, :], abs_den[:, n, :], floor_e[:, n, :], ALU.max)\
                        .then_inc(den_step, 1)
                    dve.wait_ge(den_step, 4 * n + 3)
                    nc.vector.reciprocal(mrden[:, n, :], safe_den[:, n, :]).then_inc(den_step, 1)

                def gated_h(n):
                    dve.wait_ge(num_ready, n + 1)
                    dve.wait_ge(ml_copied, 6 if n < 3 else 15)
                    dve.wait_ge(den_step, 4 * n + 4)
                    if n >= 2:
                        dve.wait_ge(mhT_in_psum, n - 1)
                    for t in range(TILES):
                        nc.vector.scalar_tensor_tensor(out=mh[:, n % 2, t, :], in0=ps[:, 6 + n % 2, t * DV:(t + 1) * DV],
                                                       scalar=mrden[:, n, t:t + 1], in1=mog[:, n, t, :], op0=ALU.mult,
                                                       op1=ALU.mult).then_inc(mh_scaled, 1)

                def o_low(n):
                    dve.wait_ge(oT_high_done, o0 + n + 1)
                    nc.vector.tensor_tensor(oT_lo[:, 2 * n:2 * n + 2, :].rearrange("p a b -> p (a b)"),
                                            ps[:, 2 + n % 2, :], oT_hi[:, 2 * n:2 * n + 2, :].rearrange("p a b -> p (a b)"),
                                            ALU.subtract).then_inc(oT_split, 1)

                low(w0 + 11)
                for n in range(NH):
                    a_of(n)
                    if n >= 2:
                        gated_h(n - 2)
                    low(w0 + 12 + n)
                low(w0 + 16)
                o_low(0)
                gated_h(2)
                o_low(1)
                gated_h(3)
                o_low(2)
                o_low(3)

            program = {"ffn": ffn, "conv": conv, "att": attention, "ml": mlstm}
            for sub, kind in enumerate(KINDS):
                joint_part(sub)
                if kind != "ffn":
                    low(w_of(sub) + 4)
                program[kind](sub)
                if kind != "ffn":
                    low(w_of(sub + 1) + 1)
            joint_part(SUBLAYERS)

        @block.gpsimd
        def _(pool):
            pool.wait_ge(consts_set, 1)
            steps = [0]

            def rstd(to, mean, n, arrived, value, done):
                pool.wait_ge(arrived, value)
                nc.gpsimd.tensor_scalar(mean_eps[:, n:n + 1], mean, EPS, None, ALU.add).then_inc(eps_added, 1)
                steps[0] += 1
                pool.wait_ge(eps_added, steps[0])
                nc.gpsimd.tensor_tensor(to, mean_eps[:, n:n + 1], minus_half[:, :], ALU.pow).then_inc(done, 1)

            def of_y(joint, t):
                n = TILES * (joint - 1) + t
                pool.wait_ge(y_mean, 2 * n + 2)
                nc.gpsimd.tensor_scalar(mean_eps[:, t:t + 1], mean_y[:, t, 0:1], mean_y[:, t, 1:2],
                                        EPS / Y_SCALE[KINDS[joint - 1]] ** 2, ALU.add, ALU.add).then_inc(eps_added, 1)
                steps[0] += 1
                pool.wait_ge(eps_added, steps[0])
                nc.gpsimd.tensor_tensor(rstd_y[:, t:t + 1], mean_eps[:, t:t + 1], minus_half[:, :], ALU.pow)\
                    .then_inc(y_rstd, 1)

            def of_x(joint, t):
                rstd(rstd_x[:, t:t + 1], mean_x[:, t:t + 1], TILES + t, x_mean, TILES * joint + t + 1, x_rstd)

            for joint in range(SUBLAYERS + 1):
                for t in range(TILES):
                    if joint:
                        of_y(joint, t)
                    if joint < SUBLAYERS:
                        of_x(joint, t)


def lay_out(inputs):
    import numpy as np

    w = {k: np.asarray(v) for k, v in inputs.items()}
    stream = np.empty((PIECES, P, PIECE), np.float32)

    def columns(m, c, n):
        return m[:, c:c + n].reshape(KD, P, n).transpose(1, 0, 2)

    def put_out(p, m):
        for q in range(OUT_PIECES):
            stream[p + q] = columns(m, 512 * (q % 2), 512)[:, 4 * (q // 2):4 * (q // 2) + 4].reshape(P, PIECE)

    done = {"ffn": 0, "conv": 0, "att": 0, "ml": 0}
    for sub, kind in enumerate(KINDS):
        p, n = BASE[sub], done[kind]
        done[kind] += 1
        if kind == "ffn":
            name = "ffn1" if sub % 3 == 0 else "ffn2"
            wg, wu, wd = (w[f"{name}_{s}"][sub // 3] for s in ("wg", "wu", "wd"))
            for c in range(EARLY // 2):
                both = np.stack([columns(wg, c * CHUNK, CHUNK), columns(wu, c * CHUNK, CHUNK)], axis=2)
                for half in range(2):
                    stream[p + early_piece(c) + half] = both[:, 4 * half:4 * half + 4].reshape(P, PIECE)
            for i in range(EARLY, BLOCKS):
                both = np.stack([columns(wg, i * P, P), columns(wu, i * P, P)], axis=2)
                stream[p + block_piece(i)] = both.reshape(P, PIECE)
            for c in range(CHUNKS):
                stream[p + down_piece(c)] = wd[c * CHUNK:(c + 1) * CHUNK].reshape(FT, P, D).transpose(1, 0, 2).reshape(P, PIECE)
        elif kind == "conv":
            for s in range(CONV_STEPS):
                for part, third in enumerate((1, 2, 0)):
                    stream[p + 3 * s + part] = columns(w["conv_w_in"][n], third * D + 256 * s, 256).reshape(P, PIECE)
            put_out(p + 3 * CONV_STEPS, w["conv_w_out"][n])
        elif kind == "att":
            for quarter in range(QUARTERS):
                for i, third in enumerate([3 * g + e for g in range(NG) for e in range(2)] + [3 * g + 2 for g in range(NG)]):
                    stream[p + QP * quarter + i] = columns(w["attn_w_in"][n], third * D + 256 * quarter, 256).reshape(P, PIECE)
            put_out(p + QP * QUARTERS, w["attn_w_out"][n])
        else:
            for i, step in enumerate(ML_ORDER):
                stream[p + i] = columns(w["mlstm_w_in"][n], 256 * step, 256).reshape(P, PIECE)
            put_out(p + 12, w["mlstm_w_out"][n])

    gate_w = np.ascontiguousarray(columns(w["mlstm_w_in"][0], 12 * 256, 2 * NH))
    gate_b = np.concatenate([w["mlstm_b_i"][0], w["mlstm_b_f"][0]])
    conv_k = np.ascontiguousarray(w["conv_k"].reshape(2, CONV_W, KD, P).transpose(3, 0, 1, 2))

    inv = np.float32(500000.0) ** (-np.arange(0, ROT, 2, dtype=np.float32) / np.float32(ROT))
    ang = np.arange(SEQ, dtype=np.float32)[:, None] * inv[None, :].astype(np.float32)
    tables = np.stack([np.tile(np.cos(ang), (1, 2 * QH)), np.tile(np.sin(ang), (1, 2 * QH))], axis=1).astype(np.float32)
    rope = np.ascontiguousarray(tables.reshape(TILES, P, 2, QH * ROT).transpose(1, 0, 2, 3))
    q, k = np.arange(P)[:, None], np.arange(P)[None, :]
    att_mask = np.full((P, NG, 2 * P), NEG, np.float32)
    for g, (win, dil) in enumerate(GROUPS):
        for b, rel in enumerate((q + P - k, q - k)):
            att_mask[:, g, b * P:(b + 1) * P][(rel >= 0) & (rel % dil == 0) & (rel // dil <= win // dil)] = 0.0
    ml_mask = np.zeros((P, 2 * P), np.float32)
    ml_mask[:, P:][k > q] = NEG
    tri = np.triu(np.ones((P, P), np.float32))
    return {
        "x_in": w["x"].reshape(SEQ, D), "gains": w["norm_g"].reshape(-1, D), "stream": stream, "gate_w": gate_w,
        "gate_b": gate_b, "conv_k": conv_k, "ident_in": np.eye(P, dtype=np.float32), "rope_in": rope,
        "att_mask_in": att_mask, "ml_mask_in": ml_mask, "tri_in": tri,
    }


def kernel(**inputs):
    import concourse.bacc as bacc
    from concourse.bass_utils import run_bass_kernel_spmd

    nc = bacc.Bacc("TRN2", target_bir_lowering=False, num_devices=1, dynamic_dma_scratch_size=1024)
    arrays = lay_out(inputs)
    aps = {n: nc.dram_tensor(n, a.shape, F32, kind="ExternalInput").ap() for n, a in arrays.items()}
    out = nc.dram_tensor("out", (SEQ, D), F32, kind="ExternalOutput").ap()
    build(nc, out=out, **aps)
    result = run_bass_kernel_spmd(nc, [arrays], core_ids=[0])
    return result.results[0]["out"].reshape(1, SEQ, D)
```
